# Optimizing a Trainium2 kernel written in Bass

```python
import math
import jax, jax.numpy as jnp
from jax import lax
import numpy as np

D_MODEL = 1024
BATCH = 1
SEQ = 256
DEPTH = 2

MEM_LEN = 256
EPS = 1e-6

RW_HEAD = 64
RW_HEADS = D_MODEL // RW_HEAD
RW_DECAY_LORA = 64
RW_AAA_LORA = 64
RW_MV_LORA = 32
RW_GN_EPS = 64e-5

GDN_HEAD = 128
GDN_HEADS = D_MODEL // GDN_HEAD
GDN_CONV = 4
GDN_CHUNK = 64

MLA_HEADS = 8
MLA_HEAD = D_MODEL // MLA_HEADS
MLA_Q_RANK = 256
MLA_KV_RANK = 256
IDX_HEADS = 8
IDX_HEAD = 64
TOPK_MAX = 256
Q_BLOCK = 128

XA_HEADS = 4
XA_HEAD = D_MODEL // XA_HEADS

D_FF = 2816
N_EXPERTS = 8
TOP_K = 2
D_FF_EXPERT = 3584
N_DENSE = (DEPTH + 1) // 2
N_MOE = DEPTH // 2

A_SPLITS = (D_MODEL, D_MODEL, D_MODEL, RW_DECAY_LORA, RW_AAA_LORA)
B_SPLITS = (3 * D_MODEL, GDN_HEADS, GDN_HEADS)
C_SPLITS = (MLA_Q_RANK, MLA_KV_RANK, IDX_HEAD, IDX_HEADS)
A_IN = sum(A_SPLITS)
B_IN = sum(B_SPLITS)
C_IN = sum(C_SPLITS)
G_IN = 3 * D_MODEL
D_IN = A_IN + B_IN + C_IN + G_IN

kernel_name = 'hybrid_rwkv7_gdn_dsa_moe_block'

def _split(t, sizes):
    offs = np.cumsum(sizes)[:-1].tolist()
    return jnp.split(t, offs, axis=-1)

def rms_norm(x, g, eps=EPS):
    xf = x.astype(jnp.float32)
    y = xf * lax.rsqrt(jnp.mean(xf * xf, axis=-1, keepdims=True) + eps)
    return (y * g).astype(x.dtype)

def layer_norm(x, g, b, eps=EPS):
    xf = x.astype(jnp.float32)
    mu = jnp.mean(xf, axis=-1, keepdims=True)
    var = jnp.mean(jnp.square(xf - mu), axis=-1, keepdims=True)
    return ((xf - mu) * lax.rsqrt(var + eps) * g + b).astype(x.dtype)

def l2norm(x, eps=EPS):
    return x * lax.rsqrt(jnp.sum(x * x, axis=-1, keepdims=True) + eps)

def token_shift(x):
    return jnp.pad(x, ((0, 0), (1, 0), (0, 0)))[:, :-1]

def causal_dwconv(x, w):
    K, C = w.shape
    return lax.conv_general_dilated(x, w[:, None, :], window_strides=(1,), padding=[(K - 1, 0)],
                                    dimension_numbers=('NWC', 'WIO', 'NWC'), feature_group_count=C)

def rwkv7_branch(p_a, v_first, mu, w0, w2, a0, a2, k_k, k_a, r_k, gn_g, gn_b, vres):
    B, T, _ = p_a.shape
    H, N = RW_HEADS, RW_HEAD
    p_a = p_a + (token_shift(p_a) - p_a) * mu
    r, k, v, xw, xa = _split(p_a, A_SPLITS)
    log_w = -jnp.exp(-jax.nn.softplus(-(w0 + jnp.tanh(xw) @ w2).astype(jnp.float32)) - 0.5)
    a = jax.nn.sigmoid(a0 + xa @ a2)
    if vres is None:
        v_first = v
    else:
        v0, v1, v2 = vres
        v = v + (v_first - v) * jax.nn.sigmoid(v0 + (v @ v1) @ v2)
    heads = lambda t: t.reshape(B, T, H, N).astype(jnp.float32)
    kk = l2norm(heads(k * k_k))
    k = k * (1 + (a - 1) * k_a)
    r4, k4, v4, a4 = heads(r), heads(k), heads(v), heads(a)
    w4 = jnp.exp(log_w).reshape(B, T, H, N)

    def step(S, inp):
        r_t, w_t, k_t, v_t, kk_t, a_t = inp
        sa = jnp.einsum('bhvk,bhk->bhv', S, -kk_t)
        S = (S * w_t[:, :, None, :] + sa[..., None] * (kk_t * a_t)[:, :, None, :]
             + v_t[..., None] * k_t[:, :, None, :])
        return S, jnp.einsum('bhvk,bhk->bhv', S, r_t)

    xs = tuple(jnp.moveaxis(t, 1, 0) for t in (r4, w4, k4, v4, kk, a4))
    _, o = lax.scan(step, jnp.zeros((B, H, N, N), jnp.float32), xs)
    o = jnp.moveaxis(o, 0, 1)
    mean = jnp.mean(o, axis=-1, keepdims=True)
    var = jnp.mean(jnp.square(o - mean), axis=-1, keepdims=True)
    o = ((o - mean) * lax.rsqrt(var + RW_GN_EPS)).reshape(B, T, D_MODEL) * gn_g + gn_b
    bonus = jnp.sum(r4 * k4 * r_k, axis=-1, keepdims=True) * v4
    return (o + bonus.reshape(B, T, D_MODEL)).astype(p_a.dtype), v_first

def gated_deltanet_branch(p_b, conv_w, A_log, dt_bias, norm_g):
    B, T, _ = p_b.shape
    H, Dh, C = GDN_HEADS, GDN_HEAD, GDN_CHUNK
    n_chunks = T // C
    qkv, a_in, b_in = _split(p_b, B_SPLITS)
    qkv = jax.nn.silu(causal_dwconv(qkv, conv_w)).astype(jnp.float32)
    q, k, v = _split(qkv, (D_MODEL, D_MODEL, D_MODEL))
    q = l2norm(q.reshape(B, T, H, Dh)) * Dh ** -0.5
    k = l2norm(k.reshape(B, T, H, Dh))
    v = v.reshape(B, T, H, Dh)
    beta = jax.nn.sigmoid(b_in.astype(jnp.float32))
    g = -jnp.exp(A_log.astype(jnp.float32)) * jax.nn.softplus(a_in.astype(jnp.float32) + dt_bias)
    to_chunks = lambda t: jnp.moveaxis(t.reshape(B, n_chunks, C, H, -1), 3, 1)
    q, k, v = to_chunks(q), to_chunks(k), to_chunks(v)
    beta = to_chunks(beta[..., None])
    g = jnp.cumsum(to_chunks(g[..., None])[..., 0], axis=-1)
    incl = jnp.tril(jnp.ones((C, C), bool))
    strict = jnp.tril(jnp.ones((C, C), bool), -1)
    decay = jnp.exp(jnp.where(incl, g[..., :, None] - g[..., None, :], -jnp.inf))
    kb = k * beta
    Lmat = jnp.where(strict, jnp.einsum('bhnid,bhnjd->bhnij', kb, k) * decay, 0.0)
    rhs = jnp.concatenate([v * beta, kb * jnp.exp(g)[..., None]], axis=-1)
    sol = lax.linalg.triangular_solve(Lmat + jnp.eye(C, dtype=jnp.float32), rhs,
                                      left_side=True, lower=True, unit_diagonal=True)
    u, wc = sol[..., :Dh], sol[..., Dh:]
    A_intra = jnp.where(incl, jnp.einsum('bhnid,bhnjd->bhnij', q, k) * decay, 0.0)

    def step(S, inp):
        q_c, k_c, u_c, w_c, g_c, A_c = inp
        v_new = u_c - jnp.einsum('bhck,bhkv->bhcv', w_c, S)
        o_c = (jnp.einsum('bhck,bhkv->bhcv', q_c * jnp.exp(g_c)[..., None], S)
               + jnp.einsum('bhij,bhjv->bhiv', A_c, v_new))
        g_end = g_c[..., -1:]
        S = S * jnp.exp(g_end)[..., None] + jnp.einsum(
            'bhck,bhcv->bhkv', k_c * jnp.exp(g_end - g_c)[..., None], v_new)
        return S, o_c

    xs = tuple(jnp.moveaxis(t, 2, 0) for t in (q, k, u, wc, g, A_intra))
    _, o = lax.scan(step, jnp.zeros((B, H, Dh, Dh), jnp.float32), xs)
    o = jnp.transpose(o, (1, 0, 3, 2, 4)).reshape(B, T, H, Dh)
    return rms_norm(o, norm_g).reshape(B, T, D_MODEL).astype(p_b.dtype)

def dsa_mla_branch(p_c, q_norm, w_uq, kv_norm, w_uk, w_uv, w_qI, kI_g, kI_b):
    B, T, _ = p_c.shape
    c_q, c_kv, k_I, w_I = _split(p_c, C_SPLITS)
    c_q = rms_norm(c_q, q_norm)
    c_kv = rms_norm(c_kv, kv_norm)
    k_I = layer_norm(k_I, kI_g, kI_b)
    w_I = w_I * (IDX_HEADS ** -0.5 * IDX_HEAD ** -0.5)
    n_sel = min(TOPK_MAX, T // 4)
    key_pos = jnp.arange(T)

    def block(i):
        s0 = i * Q_BLOCK
        cq = lax.dynamic_slice_in_dim(c_q, s0, Q_BLOCK, axis=1)
        wI = lax.dynamic_slice_in_dim(w_I, s0, Q_BLOCK, axis=1)
        q_pos = s0 + jnp.arange(Q_BLOCK)
        qI = (cq @ w_qI).reshape(B, Q_BLOCK, IDX_HEADS, IDX_HEAD)
        score = jax.nn.relu(jnp.einsum('bqhd,bsd->bqhs', qI, k_I))
        score = jnp.einsum('bqhs,bqh->bqs', score, wI).astype(jnp.float32)
        causal = key_pos[None, :] <= q_pos[:, None]
        score = jnp.where(causal[None], score, -jnp.inf)
        _, sel = lax.top_k(score, n_sel)
        valid = sel <= q_pos[None, :, None]
        kv_sel = jax.vmap(lambda c, s: c[s])(c_kv, sel)
        q = (cq @ w_uq).reshape(B, Q_BLOCK, MLA_HEADS, MLA_HEAD)
        q_lat = jnp.einsum('bqhd,rhd->bqhr', q, w_uk) * MLA_HEAD ** -0.5
        logits = jnp.einsum('bqhr,bqkr->bqhk', q_lat, kv_sel).astype(jnp.float32)
        logits = jnp.where(valid[:, :, None, :], logits, -jnp.inf)
        prob = jax.nn.softmax(logits, axis=-1).astype(kv_sel.dtype)
        o_lat = jnp.einsum('bqhk,bqkr->bqhr', prob, kv_sel)
        return jnp.einsum('bqhr,rhd->bqhd', o_lat, w_uv)

    out = lax.map(block, jnp.arange(T // Q_BLOCK))
    return jnp.moveaxis(out, 0, 1).reshape(B, T, MLA_HEADS * MLA_HEAD)

def memory_xattn(h, mem_n, w_q, w_kv, w_o):
    B, T, _ = h.shape
    M = mem_n.shape[1]
    q = (h @ w_q).reshape(B, T, XA_HEADS, XA_HEAD)
    k, v = _split(mem_n @ w_kv, (D_MODEL, D_MODEL))
    k = k.reshape(B, M, XA_HEADS, XA_HEAD)
    v = v.reshape(B, M, XA_HEADS, XA_HEAD)
    logits = jnp.einsum('bthd,bmhd->bhtm', q, k).astype(jnp.float32) * XA_HEAD ** -0.5
    p = jax.nn.softmax(logits, axis=-1).astype(v.dtype)
    o = jnp.einsum('bhtm,bmhd->bthd', p, v).reshape(B, T, D_MODEL)
    return o @ w_o

def swiglu(h, w_gate, w_up, w_down):
    return (jax.nn.silu(h @ w_gate) * (h @ w_up)) @ w_down

def moe_swiglu(h, router, w_gate, w_up, w_down):
    logits = (h @ router).astype(jnp.float32)
    top_val, top_idx = lax.top_k(logits, TOP_K)
    top_p = jax.nn.softmax(top_val, axis=-1)
    gates = jnp.einsum('btk,btke->bte', top_p, jax.nn.one_hot(top_idx, N_EXPERTS, dtype=jnp.float32))
    out = jnp.zeros(h.shape, jnp.float32)
    for e in range(N_EXPERTS):
        out = out + gates[..., e:e + 1] * swiglu(h, w_gate[e], w_up[e], w_down[e])
    return out.astype(h.dtype)

def setup_inputs(seed: int = 0) -> dict:
    key = jax.random.key(seed)
    ks = iter(jax.random.split(key, 64))
    f32 = jnp.float32

    def nrm(shape, scale):
        return jax.random.normal(next(ks), shape, f32) * scale

    def gain(shape):
        return 1.0 + nrm(shape, 0.02)

    L, D = DEPTH, D_MODEL
    dt = jnp.exp(jax.random.uniform(next(ks), (L, GDN_HEADS)) * (math.log(0.1) - math.log(0.001))
                 + math.log(0.001))
    return {
        'x': nrm((BATCH, SEQ, D), 1.0),
        'mem': nrm((BATCH, MEM_LEN, D), 1.0),
        'norm_mix': gain((L, D)),
        'w_in': nrm((L, D, D_IN), D ** -0.5),
        'rw_mu': jax.random.uniform(next(ks), (L, A_IN), f32),
        'rw_w0': nrm((L, D), 0.5),
        'rw_w2': nrm((L, RW_DECAY_LORA, D), 0.1 * RW_DECAY_LORA ** -0.5),
        'rw_a0': nrm((L, D), 0.1),
        'rw_a2': nrm((L, RW_AAA_LORA, D), 0.1 * RW_AAA_LORA ** -0.5),
        'rw_k_k': 0.85 + nrm((L, D), 0.05),
        'rw_k_a': 1.0 + nrm((L, D), 0.05),
        'rw_r_k': nrm((L, RW_HEADS, RW_HEAD), 0.1),
        'rw_gn_g': gain((L, D)),
        'rw_gn_b': nrm((L, D), 0.01),
        'rw_v0': nrm((L - 1, D), 0.5),
        'rw_v1': nrm((L - 1, D, RW_MV_LORA), D ** -0.5),
        'rw_v2': nrm((L - 1, RW_MV_LORA, D), 0.5 * RW_MV_LORA ** -0.5),
        'gdn_conv': nrm((L, GDN_CONV, 3 * D), 0.5),
        'gdn_A_log': jnp.log(jax.random.uniform(next(ks), (L, GDN_HEADS), f32, 1.0, 16.0)),
        'gdn_dt_bias': dt + jnp.log(-jnp.expm1(-dt)),
        'gdn_norm_g': gain((L, GDN_HEAD)),
        'mla_q_norm': gain((L, MLA_Q_RANK)),
        'mla_w_uq': nrm((L, MLA_Q_RANK, MLA_HEADS * MLA_HEAD), MLA_Q_RANK ** -0.5),
        'mla_kv_norm': gain((L, MLA_KV_RANK)),
        'mla_w_uk': nrm((L, MLA_KV_RANK, MLA_HEADS, MLA_HEAD), MLA_KV_RANK ** -0.5),
        'mla_w_uv': nrm((L, MLA_KV_RANK, MLA_HEADS, MLA_HEAD), MLA_KV_RANK ** -0.5),
        'idx_w_q': nrm((L, MLA_Q_RANK, IDX_HEADS * IDX_HEAD), MLA_Q_RANK ** -0.5),
        'idx_k_g': gain((L, IDX_HEAD)),
        'idx_k_b': nrm((L, IDX_HEAD), 0.01),
        'w_mix_out': nrm((L, D, D), D ** -0.5),
        'mem_norm': gain((D,)),
        'norm_xattn': gain((L, D)),
        'xa_w_q': nrm((L, D, D), D ** -0.5),
        'xa_w_kv': nrm((L, D, 2 * D), D ** -0.5),
        'xa_w_o': nrm((L, D, D), D ** -0.5),
        'norm_ffn': gain((L, D)),
        'ffn_w_gate': nrm((N_DENSE, D, D_FF), D ** -0.5),
        'ffn_w_up': nrm((N_DENSE, D, D_FF), D ** -0.5),
        'ffn_w_down': nrm((N_DENSE, D_FF, D), D_FF ** -0.5),
        'moe_router': nrm((N_MOE, D, N_EXPERTS), D ** -0.5),
        'moe_w_gate': nrm((N_MOE, N_EXPERTS, D, D_FF_EXPERT), D ** -0.5),
        'moe_w_up': nrm((N_MOE, N_EXPERTS, D, D_FF_EXPERT), D ** -0.5),
        'moe_w_down': nrm((N_MOE, N_EXPERTS, D_FF_EXPERT, D), D_FF_EXPERT ** -0.5),
        'final_norm': gain((D,)),
    }

def reference(x, mem, norm_mix, w_in, rw_mu, rw_w0, rw_w2, rw_a0, rw_a2, rw_k_k, rw_k_a, rw_r_k,
              rw_gn_g, rw_gn_b, rw_v0, rw_v1, rw_v2, gdn_conv, gdn_A_log, gdn_dt_bias, gdn_norm_g,
              mla_q_norm, mla_w_uq, mla_kv_norm, mla_w_uk, mla_w_uv, idx_w_q, idx_k_g, idx_k_b,
              w_mix_out, mem_norm, norm_xattn, xa_w_q, xa_w_kv, xa_w_o, norm_ffn, ffn_w_gate,
              ffn_w_up, ffn_w_down, moe_router, moe_w_gate, moe_w_up, moe_w_down, final_norm):
    mem_n = rms_norm(mem, mem_norm)
    v_first = None
    for l in range(DEPTH):
        h = rms_norm(x, norm_mix[l])
        p = h @ w_in[l]
        p_a, p_b, p_c, p_g = _split(p, (A_IN, B_IN, C_IN, G_IN))
        vres = None if l == 0 else (rw_v0[l - 1], rw_v1[l - 1], rw_v2[l - 1])
        y_a, v_first = rwkv7_branch(p_a, v_first, rw_mu[l], rw_w0[l], rw_w2[l], rw_a0[l], rw_a2[l],
                                    rw_k_k[l], rw_k_a[l], rw_r_k[l], rw_gn_g[l], rw_gn_b[l], vres)
        y_b = gated_deltanet_branch(p_b, gdn_conv[l], gdn_A_log[l], gdn_dt_bias[l], gdn_norm_g[l])
        y_c = dsa_mla_branch(p_c, mla_q_norm[l], mla_w_uq[l], mla_kv_norm[l], mla_w_uk[l], mla_w_uv[l],
                             idx_w_q[l], idx_k_g[l], idx_k_b[l])
        g_a, g_b, g_c = _split(jax.nn.sigmoid(p_g), (D_MODEL, D_MODEL, D_MODEL))
        x = x + (g_a * y_a + g_b * y_b + g_c * y_c) @ w_mix_out[l]
        x = x + memory_xattn(rms_norm(x, norm_xattn[l]), mem_n, xa_w_q[l], xa_w_kv[l], xa_w_o[l])
        h = rms_norm(x, norm_ffn[l])
        i = l // 2
        if l % 2 == 0:
            x = x + swiglu(h, ffn_w_gate[i], ffn_w_up[i], ffn_w_down[i])
        else:
            x = x + moe_swiglu(h, moe_router[i], moe_w_gate[i], moe_w_up[i], moe_w_down[i])
    return rms_norm(x, final_norm)


_drawn_inputs = setup_inputs


def setup_inputs(seed=0):
    import zlib

    import numpy as np

    out = dict(_drawn_inputs(seed))
    spreads = {}
    factors = {'rw_gn_b': 3.452,
     'mla_kv_norm': 5.243,
     'idx_k_b': 3.722,
     'mem_norm': 3.861,
     'norm_xattn': 3.27,
     'final_norm': 2.827}
    for name, (base, spread) in spreads.items():
        noise = np.random.default_rng([zlib.crc32(name.encode()), seed]).standard_normal(out[name].shape)
        drawn = base * np.exp(spread * noise) if base else spread * noise
        out[name] = __import__('jax').numpy.asarray(drawn.astype(out[name].dtype))
    for name, factor in factors.items():
        out[name] = (out[name] * factor).astype(out[name].dtype)
    return out
```

```python
import math
from contextlib import ExitStack

import numpy as np

import concourse.bass as bass
from concourse import mybir

F32 = mybir.dt.float32
ALU = mybir.AluOpType
ACT = mybir.ActivationFunctionType
AX = mybir.AxisListType

P = 128
D = 1024
T = 256
LAYERS = 2
KT = D // P
TT = T // P
EPS = 1e-6
RW_N = 64
RW_CHUNKS = T // RW_N
RW_PAIRS = D // P
GN_EPS = 64e-5
GH = D // P
TOPK = 64
FF = 2816
FE = 3584
NE = 8
A_IN, B_IN = 3 * D + 128, 3 * D + 16
C0 = A_IN + B_IN
G0 = C0 + 256 + 256 + 64 + 8
DECAY = math.exp(-0.5)
SLOT = 4096
MIX_SLOTS = 3
FFN_SLOT, FFN_BUFS = 2048, 6
FE_CHUNKS = 3 * FE // 256
PASSES = ((0, 0), (0, 1), (1, 0))
FILL, TAKEN = -3.0e38, -3.39e38

PARAMS = [("norm_mix", 8), ("mu", 25), ("w0", 8), ("a0", 8), ("k_k", 8), ("k_a", 8), ("r_k", 8),
          ("gn_g", 8), ("gn_b", 8), ("v0", 8), ("norm_xattn", 8), ("norm_ffn", 8), ("q_norm", 2),
          ("kv_norm", 2), ("gdn_norm", 1), ("kI_g", 1), ("kI_b", 1), ("mem_norm", 8), ("conv", 96),
          ("A_log", 1), ("dt_bias", 1)]
PCOL, NPAR = {}, 0
for _n, _k in PARAMS:
    PCOL[_n] = NPAR
    NPAR += _k

LEVELS = 7
CONSTS = [("ident", 128), ("ones", 128), ("blk", 128), ("maskbd", 128), ("antibd", 128),
          ("maskGA", 128), ("maskGB", 128), ("gdnmask", 256), ("level", 128 * LEVELS),
          ("sel", 1024), ("fill", 512)]
CCOL, NCONST = {}, 0
for _n, _k in CONSTS:
    CCOL[_n] = (NCONST, _k)
    NCONST += _k


def make_consts():
    i = np.arange(P)
    s, t = i[:, None], i[None, :]
    sm, tm = s % 64, t % 64
    same = (s // 64 == t // 64)
    strict, incl = sm < tm, sm <= tm
    c = {
        "ident": s == t, "ones": np.ones((P, P)), "blk": same, "maskbd": same, "antibd": ~same,
        "maskGA": np.where(t < 64, strict, incl), "maskGB": np.where(t < 64, incl, strict),
        "gdnmask": np.concatenate([np.where(s < t, -1.0, 0.0), np.where(s <= t, 1.0, 0.0)], 1),
        "level": np.concatenate([(s // (2 * b) == t // (2 * b)) & ((s // b) % 2 == 1) & ((t // b) % 2 == 0)
                                 for b in (2 ** k for k in range(LEVELS))], 1),
        "sel": np.concatenate([(s == h) & (t >= 0) for h in range(8)], 1),
    }
    q = i[:, None]
    k = np.arange(T)[None, :]
    c["fill"] = np.concatenate([np.where(k <= q + P * a, 0.0, FILL) for a in range(TT)], 1)
    return np.concatenate([np.asarray(c[n], np.float32).reshape(P, w) for n, w in CONSTS], 1)


SEMS = ("in_dma par_dma mem_dma out_dma slot0 slot1 slot2 weights_used mixers_done "
        "dve_step act_step norm_ss norm_ms norm_sd norm_xn norm_T feat_ready x_new "
        "proj_full proj_evac raw_free gate_free rkv_ready vlow_full vlow vres_full vres_sig vres_done "
        "rw_lora rw_sig rw_cum rw_exp rw_kksq rw_bon rw_sums rw_nrm rw_sqrt rw_vv rw_fm rw_tr rw_G rw_tm rw_N "
        "inv_Y inv_Ym inv_D inv_X rc_P1 rc_R rc_U rc_UV rc_P2 rc_S rc_O rc_Sn rc_OT rc_Of "
        "gn_m gn_sq gn_v gn_var gn_sd gn_y merged "
        "gd_ab gd_abs gd_g gd_gT gd_sq gd_ss gd_nrm gd_sqrt gd_bc gd_eg gd_fm gd_kk gd_dif gd_dec gd_N gd_tr gd_tm "
        "gr_in gr_R gr_V gr_Vs gr_S gr_Ss gr_O gr_Of gt_sq gt_ss gt_ms gt_sd "
        "ml_sq ml_ss ml_ms ml_sd ml_n kI_m kI_v kI_var kI_ms kI_sd kI_n ix_full ix_rl ix_free "
        "at_L at_max at_exp at_p at_T at_PT at_O at_Of mix_full "
        "fslot0 fslot1 fslot2 fslot3 fslot4 fslot5 w_hi w_lo wb_used f_hi act_f gu_full silu act_t down_full rt_full rt_l rt_d rt_e").split()


class Counter:

    def __init__(self, sems):
        self.sems, self.sent, self.seen, self.loop, self.latest = sems, {}, {}, None, None

    def _at(self, name, n):
        return n if self.loop is None else n + self.loop[0] * self.loop[1][name]

    def inc(self, name):
        self.sent[name] = self.sent.get(name, 0) + 1
        self.latest = name
        return self.sems[name], 1

    def last(self):
        return self.sems[self.latest], self._at(self.latest, self.sent[self.latest])

    def need(self, name, k=1, spare=0, view=None):
        n = self.seen[name, view] = self.seen.get((name, view), 0) + k
        return self._at(name, n - spare) if n > spare else None

    def skip(self, name, k, view=None):
        self.seen[name, view] = self.seen.get((name, view), 0) + k

    def begin_loop(self, done, per):
        self.loop = (done, per)

    def end_loop(self, rounds):
        per = self.loop[1]
        self.loop = None
        for n in self.sent:
            self.sent[n] += (rounds - 1) * per.get(n, 0)
        for n, v in self.seen:
            self.seen[n, v] += (rounds - 1) * per.get(n, 0)


def build(nc, x, mem, consts, params, w_in, w2, a2, v1, v2, w_uq, w_uk, w_uv, w_qI, w_mix, xa_q, xa_kv, xa_o,
          ff_g, ff_u, ff_d, router, me_g, me_u, me_d, final_norm, out):
    ctx = ExitStack()
    with ctx:
        def sb(name, shape):
            return ctx.enter_context(nc.sbuf_tensor(name, shape, F32))

        S = {n: ctx.enter_context(nc.semaphore(n)) for n in SEMS}
        bank = [ctx.enter_context(nc.psum_tensor(f"bank{i}", [P, 512], F32)) for i in range(8)]

        xt = sb("xt", [P, TT, D])
        feat = sb("feat", [P, KT, T])
        memf = sb("memf", [P, KT, T])
        vfirst = sb("vfirst", [P, KT, T])
        cs = sb("cs", [P, NCONST])
        par = sb("par", [P, LAYERS, NPAR])
        ring = sb("ring", [P, MIX_SLOTS * SLOT])
        gates = sb("gates", [P, TT, NE])
        rout = sb("rout", [P, KT, NE])
        rtmp = sb("rtmp", [P, 64])
        small = sb("small", [P, 80])
        yacc = sb("yacc", [P, KT, T])
        MIXF = 25632
        NORM_AT = 16384
        arena = sb("arena", [P, MIXF])
        at = 0

        def view(buf, start, *shape):
            v = buf[:, start:start + math.prod(shape)]
            names = "abcd"[:len(shape)]
            if len(shape) > 1:
                v = v.rearrange(f"p ({' '.join(names)}) -> p {' '.join(names)}", **dict(zip(names, shape)))
            return v

        def area(*shape):
            nonlocal at
            v = view(arena, at, *shape)
            at += math.prod(shape)
            assert at <= MIXF
            return v

        yflat = yacc[:, :, :].rearrange("p a b -> p (a b)")
        xn = view(arena, NORM_AT, TT, D)
        sqj = view(arena, NORM_AT + TT * D, D)
        rkv = area(24, T)
        branch = rkv[:, 0:KT, :]
        BASE = at
        raw = area(4, 260)
        gate = area(4, T)
        at = BASE
        tmp = area(14, T)
        lora, vlo = area(T), area(T)
        ZR, BKt, Vad, GA, GB, XT = (area(4, 4, P) for _ in range(6))
        NT = area(4, P)
        Rbd, UV, Oad, Sst, Stmp = (area(4, P) for _ in range(5))
        wc = area(4, 4)
        X, Ym, BK, VV = (view(yflat, 512 * i, 4, P) for i in range(4))
        at = BASE
        gt = area(10, T)
        g8, b8, ab = area(T), area(T), area(4, T)
        gbt = area(TT, 16)
        ke, qe = area(4, T), area(4, T)
        kq = area(TT, 2, P)
        dec = area(TT, P)
        gNT, gXT, gAT = area(4, TT, P), area(4, TT, P), area(4, TT, P)
        ktm, vtm = area(4, P), area(4, TT, P)
        gX, gYm = area(4, P), area(4, P)
        gR, gV, gS = area(4, P), area(4, P), area(4, P)
        qf = branch
        at = KT * T
        kf = area(KT, T)
        qI = area(4, T)
        rl = area(4, T)
        at = BASE + 1040 + 1024
        cqk = area(4, T)
        kI = area(T)
        wI = area(TT, 8)
        mt = area(6, T)
        vt = area(TT, D)
        score, negm = area(TT, T), area(TT, T)
        m8 = area(8)
        Lm, Pr, PT = area(2, 2 * T), area(2, 2 * T), area(2, 2 * T)
        amax, asum, ainv = area(2, 2), area(2, 2), area(2, 2)
        at = 0

        def parts(*shape):
            a = area(math.prod(shape)).bitcast(mybir.dt.bfloat16)
            return [view(a, i * math.prod(shape), *shape) for i in range(2)]

        w_parts = [parts(FFN_SLOT) for _ in range(FFN_BUFS)]
        feat_parts = parts(KT, T)
        act_parts = parts(4, T)
        assert at <= NORM_AT
        silu_t = yacc[:, 0:4, :]

        def C(name, a=0, b=None):
            lo, w = CCOL[name]
            return cs[:, lo + a:lo + (w if b is None else b)]

        def pc(l, name, j=0):
            return par[:, l, PCOL[name] + j:PCOL[name] + j + 1]

        def b4(ap, n=4):
            return ap.unsqueeze(1).to_broadcast([ap.shape[0], n, ap.shape[1]])

        def bk(i, lo=0, w=512):
            return bank[i][:, lo:lo + w]

        def bk4(i):
            return bank[i][:, :].rearrange("p (a b) -> p a b", a=4)

        def slot_ap(s):
            return ring[:, s * SLOT:(s + 1) * SLOT]

        def rows(w):
            return w.rearrange("(k p) n -> p k n", p=P)

        def col_chunk(w, c0, n=512):
            k = w.shape[0] // P
            return [(0, (k, n), rows(w)[:, :, c0:c0 + n], 0, P)]

        def mix_chunks(l):
            w = w_in[l]
            for i in range(6):
                yield col_chunk(w, 512 * i)
            lo = [(0, (8, 128), rows(w)[:, :, 3 * D:3 * D + 128], 0, P),
                  (1024, (1, D), w2[l].unsqueeze(1), 0, 64), (1024, (1, D), a2[l].unsqueeze(1), 64, 64)]
            if l:
                lo += [(2048, (8, 32), rows(v1[l - 1]), 0, P), (2304, (1, D), v2[l - 1].unsqueeze(1), 0, 32)]
            yield lo
            for i in range(2):
                yield col_chunk(w, G0 + 512 * i)
            for i in range(6):
                yield col_chunk(w, A_IN + 512 * i)
            yield [(0, (8, 16), rows(w)[:, :, A_IN + 3 * D:A_IN + 3 * D + 16], 0, P)]
            for i in range(2):
                yield col_chunk(w, G0 + D + 512 * i)
            yield col_chunk(w, C0)
            kc = rows(w)[:, :, C0 + 512:C0 + 576]
            yield [(0, (8, 128), kc, 0, P), (1024, (8, 8), rows(w)[:, :, C0 + 576:C0 + 584], 0, P)]
            yield [(0, (2, D), rows(w_uq[l]), 0, P), (2048, (2, D), rows(w_uk[l]), 0, P)]
            yield [(0, (2, D), rows(w_uv[l]), 0, P), (2048, (2, 512), rows(w_qI[l]), 0, P)]
            for i in range(2):
                yield col_chunk(w, G0 + 2 * D + 512 * i)
            for w_, n in ((w_mix[l], 2), (xa_q[l], 2), (xa_kv[l], 4), (xa_o[l], 2)):
                for i in range(n):
                    yield col_chunk(w_, 512 * i)

        def ffn_chunks(g, u, d, n):
            for f in range(0, n, 256):
                w = 256
                yield col_chunk(g, f, w)
                yield col_chunk(u, f, w)
                yield [(0, (w // P, D), rows(d[f:f + w]), 0, P)]

        class Stream:
            def __init__(self):
                self.n, self.last, self.count = 0, {}, [0] * MIX_SLOTS

            def next(self, slots):
                s = self.pos % slots
                self.pos += 1
                need = self.last.get(s, -1) + 1
                self.last[s] = self.n
                self.n += 1
                return s, need

            def phase(self):
                self.pos = 0

        sp_s, pe_s = Stream(), Stream()

        block = ctx.enter_context(nc.Block())

        @block.sync
        def _(sp):
            sp.dma_start(par[:, :, :], params.rearrange("l p n -> p l n")).then_inc(S["par_dma"], 16)
            sp.dma_start(yacc[:, :, :].rearrange("p a b -> p (a b)").rearrange("p (a d) -> p a d", a=TT),
                         mem.rearrange("(a p) d -> p a d", p=P)).then_inc(S["mem_dma"], 16)
            sp.dma_start(xt[:, :, :], x.rearrange("(a p) d -> p a d", p=P)).then_inc(S["in_dma"], 16)
            sp.dma_start(cs[:, :], consts).then_inc(S["par_dma"], 16)
            sp.dma_start(rout[:, :, :], rows(router)).then_inc(S["par_dma"], 16)

            def load(chunk, slots, rounds=0):
                s, need = sp_s.next(slots)
                if need:
                    sp.wait_ge(S["weights_used"], rounds + need)
                for col, shape, src, p0, np_ in chunk:
                    dst = slot_ap(s)[p0:p0 + np_, col:col + math.prod(shape)].rearrange("p (k n) -> p k n", k=shape[0])
                    sp.dma_start(dst[:, :, 0:src.shape[-1]], src).then_inc(S[f"slot{s}"], 16)
                    if src.shape[-1] < shape[1]:
                        sp.dma_start(dst[:, :, src.shape[-1]:], src).then_inc(S[f"slot{s}"], 16)

            nff = [0]

            def load_ffn(chunks, done=0):
                for ch in chunks:
                    n = nff[0]
                    nff[0] += 1
                    if n in first_round:
                        sp.wait_ge(S["weights_used"], first_round[n])
                    else:
                        sp.wait_ge(S["w_lo"], done + n - FFN_BUFS + 1)
                    for _, shape, src, _, _ in ch:
                        sp.dma_start(view(ring, (n % FFN_BUFS) * FFN_SLOT, *shape), src
                                     ).then_inc(S[f"fslot{n % FFN_BUFS}"], 16)

            for l in range(LAYERS):
                sp_s.phase()
                if l:
                    sp.wait_ge(S["w_lo"], nff[0])
                for ch in mix_chunks(l):
                    load(ch, MIX_SLOTS)
                first_round = {nff[0] + i: sp_s.last[(nff[0] + i) % FFN_BUFS * FFN_SLOT // SLOT] + 1 for i in range(FFN_BUFS)}
                if l == 0:
                    load_ffn(ffn_chunks(ff_g[0], ff_u[0], ff_d[0], FF))
            load_ffn(ffn_chunks(me_g[0, 0], me_u[0, 0], me_d[0, 0], FE))
            sp.wait_ge(S["mixers_done"], LAYERS)
            sp.dma_start(memf[:, 0:4, :].rearrange("p a b -> p (a b)"),
                         final_norm.partition_broadcast(P)).then_inc(S["par_dma"], 16)
            with sp.Fori(1, NE - 1) as e:
                load_ffn(ffn_chunks(me_g[0, e], me_u[0, e], me_d[0, e], FE), (e - 1) * FE_CHUNKS)
            nff[0] += (NE - 3) * FE_CHUNKS
            load_ffn(ffn_chunks(me_g[0, NE - 1], me_u[0, NE - 1], me_d[0, NE - 1], FE))
            sp.wait_ge(S["norm_xn"], 2 * (2 + 3 * LAYERS))
            sp.dma_start(out.rearrange("(a p) d -> p a d", p=P),
                         yacc[:, :, :].rearrange("p a b -> p (a b)").rearrange("p (a d) -> p a d", a=TT)
                         ).then_inc(S["out_dma"], 16)
            sp.wait_ge(S["out_dma"], 16)

        @block.tensor
        def _(pe):
            c = Counter(S)
            owed = [0]
            slot_seen = [0] * MIX_SLOTS

            mm, tr_ = nc.tensor.matmul, nc.tensor.transpose

            def tr(o, i_):
                return tr_(o, i_, C("ident")[0:i_.shape[0], 0:i_.shape[0]])

            def release(i):
                if owed[0]:
                    i.then_inc(S["weights_used"], owed[0])
                    owed[0] = 0

            def chunk(slots, ndma=1):
                s, _ = pe_s.next(slots)
                slot_seen[s] += 16 * ndma
                pe.wait_ge(S[f"slot{s}"], slot_seen[s])
                return slot_ap(s)

            nproj = [0]

            def proj_slot():
                n = nproj[0] % 2
                nproj[0] += 1
                due = c.need("proj_evac", 1, spare=2)
                if due is not None:
                    pe.wait_ge(S["proj_evac"], due)
                return bk(n, 0, 256)

            def proj(w, ntiles, src, kt=KT):
                for j in range(ntiles):
                    o = proj_slot()
                    for k in range(kt):
                        m = mm(o, w[:, k, j * P:(j + 1) * P], src[:, k, :], start=k == 0, stop=k == kt - 1)
                        if k == 0:
                            release(m)
                        if k == kt - 1:
                            m.then_inc(S["proj_full"], 1)

            def proj_chunks(n, src):
                for _ in range(n):
                    w = chunk(MIX_SLOTS).rearrange("p (k n) -> p k n", k=KT)
                    proj(w, 4, src)
                    owed[0] += 1

            def proj_tok(w, src, kt, quarters):
                for t in range(TT):
                    for q in range(quarters):
                        o = proj_slot()
                        for k in range(kt):
                            m = mm(o, src[:, k, t * P:(t + 1) * P], w[:, k, q * 256:(q + 1) * 256], start=k == 0, stop=k == kt - 1)
                            if k == 0:
                                release(m)
                            if k == kt - 1:
                                m.then_inc(S["proj_full"], 1)

            def norm():
                pe.wait_ge(S["norm_xn"], c.need("norm_xn", 2))
                for b in range(4):
                    for k in (2 * b, 2 * b + 1):
                        for t in range(TT):
                            m = tr(bk(4 + b, (k % 2) * 256 + t * P, P), xn[:, t, k * P:(k + 1) * P])
                            if not k and not t:
                                release(m)
                            if k % 2 and t == 1:
                                m.then_inc(S["norm_T"], 1)
                pe.wait_ge(S["feat_ready"], c.need("feat_ready", 8))

            def invert(levels, nt, xtv, xv, yv, b0):
                for b in range(levels):
                    for i in range(4):
                        m = mm(bk(b0, i * P, P), nt[:, i, :], xv[:, i, :] if b else C("ident"), start=True, stop=True)
                        if i == 3:
                            m.then_inc(S["inv_Y"], 1)
                    pe.wait_ge(S["inv_Ym"], c.need("inv_Ym"))
                    if 0 < b < levels - 1:
                        for i in range(4):
                            mm(bk(b0 + 1, i * P, P), xtv[:, i, :], yv[:, i, :], start=True, stop=True)
                    for i in range(4):
                        m = mm(bk(b0 + 2, i * P, P), yv[:, i, :], xtv[:, i, :] if b else C("ident"), start=True, stop=True)
                        if i == 3:
                            m.then_inc(S["inv_D"], 1)
                    pe.wait_ge(S["inv_X"], c.need("inv_X"))

            def rwkv(l):
                proj_chunks(6, feat)
                w = chunk(MIX_SLOTS, 5 if l else 3)
                proj(w[:, 0:1024].rearrange("p (k n) -> p k n", k=KT), 1, feat)
                wl = w[:, 1024:2048]
                pe.wait_ge(S["rkv_ready"], c.need("rkv_ready"))
                if l:
                    for k in range(KT):
                        m = mm(bk(2, 0, T)[0:32], w[:, 2048 + 32 * k:2080 + 32 * k], rkv[:, 16 + k, :], start=k == 0, stop=k == KT - 1)
                        if k == KT - 1:
                            m.then_inc(S["vlow_full"], 1)
                    pe.wait_ge(S["vlow"], c.need("vlow"))
                    for j in range(KT):
                        due = c.need("vres_sig", 1, spare=2)
                        if due is not None:
                            pe.wait_ge(S["vres_sig"], due)
                        mm(bk(3 + j % 2, 0, T), w[0:32, 2304 + j * P:2304 + (j + 1) * P], vlo[0:32, :], start=True, stop=True).then_inc(S["vres_full"], 1)
                    pe.wait_ge(S["vres_sig"], c.need("vres_sig", 0))
                for j in range(RW_PAIRS):
                    jj = j % 4
                    mm(bk(2, 0, T), wl[0:64, j * P:(j + 1) * P], lora[0:64, :], start=True, stop=True)
                    mm(bk(3, 0, T), wl[64:128, j * P:(j + 1) * P], lora[64:128, :], start=True, stop=True).then_inc(S["rw_lora"], 1)
                    if j == RW_PAIRS - 1:
                        owed[0] += 1
                    pe.wait_ge(S["rw_kksq"], c.need("rw_kksq"))
                    release(mm(bk(4, 0, T), C("blk"), tmp[:, 5, :], start=True, stop=True))
                    pe.wait_ge(S["rw_bon"], c.need("rw_bon"))
                    mm(bk(4, T, T), C("blk"), tmp[:, 7, :], start=True, stop=True).then_inc(S["rw_sums"], 1)
                    pe.wait_ge(S["rw_fm"], c.need("rw_fm"))
                    pe.wait_ge(S["rw_vv"], c.need("rw_vv"))
                    for q in range(4):
                        tr(bk(5, q * P, P), BK[:, q, :])
                    for q in range(4):
                        m = tr(bk(6, q * P, P), VV[:, q, :])
                        if q == 3:
                            m.then_inc(S["rw_tr"], 1)
                    for q in range(4):
                        mm(bk(7, q * P, P), BK[0:64, q, :], ZR[0:64, jj, q, :], start=True, stop=True)
                    for q in range(4):
                        m = mm(bk(2, q * P, P), BK[64:128, q, :], ZR[64:128, jj, q, :], start=True, stop=True)
                        if q == 3:
                            m.then_inc(S["rw_G"], 1)
                    pe.wait_ge(S["rw_tm"], c.need("rw_tm"))
                    pe.wait_ge(S["rw_N"], c.need("rw_N"))
                    invert(6, NT, XT[:, jj], X, Ym, 3)
                    if jj == 3:
                        recur_rw()
                for i in range(4):
                    mm(bk(5), C("blk"), branch[:, 2 * i:2 * i + 2, :], start=True, stop=True).then_inc(S["gn_m"], 1)
                    pe.wait_ge(S["gn_sq"], c.need("gn_sq"))
                    mm(bk(6), C("blk"), tmp[:, 0:2, :], start=True, stop=True).then_inc(S["gn_v"], 1)
                    pe.wait_ge(S["gn_y"], c.need("gn_y"))
                proj_chunks(2, feat)

            def recur_rw():
                def outputs(b, rhs, q, sig):
                    for jj in range(4):
                        o = bk(b, jj * P, P)
                        if q:
                            mm(o, ZR[:, jj, q, :], Sst[:, jj, :], start=True, stop=False)
                        mm(o[:, 0:64], GA[:, jj, q, :], rhs[:, jj, 0:64], start=not q, stop=not q)
                        m = mm(o[:, 64:128], GB[:, jj, q, :], rhs[:, jj, 64:128], start=not q, stop=True)
                        if jj == 3:
                            m.then_inc(S[sig], 1)

                for q in range(RW_CHUNKS):
                    if q:
                        pe.wait_ge(S["rc_Sn"], c.need("rc_Sn"))
                    outputs(6, Vad[:, :, q, :], q, "rc_P1")
                    pe.wait_ge(S["rc_R"], c.need("rc_R"))
                    for jj in range(4):
                        m = mm(bk(7, jj * P, P), XT[:, jj, q, :], Rbd[:, jj, :], start=True, stop=True)
                        if jj == 3:
                            m.then_inc(S["rc_U"], 1)
                    pe.wait_ge(S["rc_UV"], c.need("rc_UV"))
                    if q < RW_CHUNKS - 1:
                        for jj in range(4):
                            m = mm(bk(3, jj * P, P), BKt[:, jj, q, :], UV[:, jj, :], start=True, stop=True)
                            if jj == 3:
                                m.then_inc(S["rc_S"], 1)
                    outputs(2, UV, q, "rc_P2")
                    pe.wait_ge(S["rc_O"], c.need("rc_O"))
                    due = c.need("rc_Of", 1, spare=1)
                    if due is not None:
                        pe.wait_ge(S["rc_Of"], due)
                    for jj in range(4):
                        m = tr(bk(4, jj * P, P), Oad[:, jj, :])
                        if jj == 3:
                            m.then_inc(S["rc_OT"], 1)
                pe.wait_ge(S["rc_Of"], c.need("rc_Of", 0))

            def gdn(l):
                proj_chunks(6, feat)
                w = chunk(MIX_SLOTS)[:, 0:128].rearrange("p (k n) -> p k n", k=KT)
                for h in range(2):
                    for k in range(KT):
                        m = mm(bk(2 + h, 0, T)[0:8], w[:, k, 8 * h:8 * h + 8], feat[:, k, :], start=k == 0, stop=k == KT - 1)
                        if k == KT - 1:
                            m.then_inc(S["gd_ab"], 1)
                owed[0] += 1
                pe.wait_ge(S["gd_g"], c.need("gd_g"))
                for t in range(TT):
                    release(tr(bk(4, 16 * t, 8), g8[0:8, t * P:(t + 1) * P]))
                    m = tr(bk(4, 16 * t + 8, 8), b8[0:8, t * P:(t + 1) * P])
                    if t:
                        m.then_inc(S["gd_gT"], 1)
                pe.wait_ge(S["rkv_ready"], c.need("rkv_ready"))
                for h in range(GH):
                    hh = h % 4
                    sel = C("sel", P * h, P * h + P)[0:8]
                    mm(bk(3, 0, T), sel, g8[0:8, :], start=True, stop=True)
                    mm(bk(3, T, T), sel, b8[0:8, :], start=True, stop=True).then_inc(S["gd_bc"], 1)
                    pe.wait_ge(S["gd_sq"], c.need("gd_sq"))
                    mm(bk(2), C("ones"), gt[:, 0:2, :], start=True, stop=True).then_inc(S["gd_ss"], 1)
                    pe.wait_ge(S["gd_fm"], c.need("gd_fm"))
                    for t in range(TT):
                        m = mm(bk(5, 256 * t, 256), gt[:, 3, t * P:(t + 1) * P], kq[:, t], start=True, stop=True)
                        if t:
                            m.then_inc(S["gd_kk"], 1)
                    tr(bk(6, 0, P), gt[:, 3, 0:P])
                    for t in range(TT):
                        m = tr(bk(6, (1 + t) * P, P), rkv[:, 16 + h, t * P:(t + 1) * P])
                        if t:
                            m.then_inc(S["gd_tr"], 1)
                    pe.wait_ge(S["gd_N"], c.need("gd_N"))
                    pe.wait_ge(S["gd_tm"], c.need("gd_tm"))
                    if h % 2:
                        invert(7, gNT[:, hh - 1:hh + 1].rearrange("p a b c -> p (a b) c"),
                               gXT[:, hh - 1:hh + 1].rearrange("p a b c -> p (a b) c"), gX, gYm, 2)
                    if hh == 3:
                        recur_gd()
                for i in range(4):
                    pe.wait_ge(S["gt_sq"], c.need("gt_sq"))
                    mm(bk(2), C("ones"), gt[:, 0:2, :], start=True, stop=True).then_inc(S["gt_ss"], 1)
                pe.wait_ge(S["gn_y"], c.need("gn_y"))
                proj_chunks(2, feat)

            def recur_gd():
                for t in range(TT):
                    if t:
                        pe.wait_ge(S["gr_Ss"], c.need("gr_Ss"))
                        for i in range(4):
                            m = mm(bk(5, i * P, P), ke[:, i, P:T], gS[:, i, :], start=True, stop=True)
                            if i == 3:
                                m.then_inc(S["gr_in"], 1)
                    pe.wait_ge(S["gr_R"], c.need("gr_R"))
                    for i in range(4):
                        m = mm(bk(6, i * P, P), gXT[:, i, t, :], gR[:, i, :], start=True, stop=True)
                        if i == 3:
                            m.then_inc(S["gr_V"], 1)
                    pe.wait_ge(S["gr_Vs"], c.need("gr_Vs"))
                    if t == 0:
                        for i in range(4):
                            m = mm(bk(7, i * P, P), ktm[:, i, :], gV[:, i, :], start=True, stop=True)
                            if i == 3:
                                m.then_inc(S["gr_S"], 1)
                    for i in range(4):
                        o = bk(3 + t, i * P, P)
                        if t:
                            mm(o, gS[:, i, :], qe[:, i, P:T], start=True, stop=False)
                        m = mm(o, gV[:, i, :], gAT[:, i, t, :], start=not t, stop=True)
                        if i == 3:
                            m.then_inc(S["gr_O"], 1)
                pe.wait_ge(S["gr_Of"], c.need("gr_Of", 2))

            def attention(heads, kt):
                def logits(h):
                    for qt in range(TT):
                        for k in range(kt):
                            m = mm(bk(2 + h % 2, 256 * qt, 256), qf[:, h * kt + k, qt * P:(qt + 1) * P], kf[:, h * kt + k, :], start=k == 0, stop=k == kt - 1)
                            if not qt and not k:
                                release(m)
                            if qt and k == kt - 1:
                                m.then_inc(S["at_L"], 1)

                logits(0)
                for h in range(heads):
                    if h + 1 < heads:
                        logits(h + 1)
                    pe.wait_ge(S["at_p"], c.need("at_p"))
                    for s in range(TT):
                        for qt in range(TT):
                            m = tr(bk(4 + h % 2, 256 * s + P * qt, P), Pr[:, h % 2, qt * 256 + s * P:qt * 256 + (s + 1) * P])
                            if s and qt:
                                m.then_inc(S["at_T"], 1)
                    pe.wait_ge(S["at_PT"], c.need("at_PT"))
                    for d in range(kt):
                        j = h * kt + d
                        due = c.need("at_Of", 1, spare=2)
                        if due is not None:
                            pe.wait_ge(S["at_Of"], due)
                        for s in range(TT):
                            m = mm(bk(6 + j % 2, 0, T), vt[:, s, j * P:(j + 1) * P], PT[:, h % 2, s * 256:(s + 1) * 256], start=s == 0, stop=s == 1)
                            if s:
                                m.then_inc(S["at_O"], 1)
                pe.wait_ge(S["at_Of"], c.need("at_Of", 0))

            def mla(l):
                proj_chunks(1, feat)
                w = chunk(MIX_SLOTS, 3)
                proj(w[:, 0:1024].rearrange("p (k n) -> p k n", k=KT), 1, feat)
                o = proj_slot()
                for t in range(TT):
                    for k in range(KT):
                        m = mm(o[:, 8 * t:8 * t + 8], feat[:, k, t * P:(t + 1) * P], w[:, 1024 + 8 * k:1032 + 8 * k], start=k == 0, stop=k == KT - 1)
                        if t and k == KT - 1:
                            m.then_inc(S["proj_full"], 1)
                owed[0] += 1
                pe.wait_ge(S["ml_sq"], c.need("ml_sq"))
                for i in range(4):
                    m = mm(bk(2, 256 * (i // 2), T), C("ones"), mt[:, i, :], start=i % 2 == 0, stop=i % 2 == 1)
                    if i == 3:
                        m.then_inc(S["ml_ss"], 1)
                    if i == 0:
                        release(m)
                mm(bk(3, 0, T), C("blk"), kI, start=True, stop=True).then_inc(S["kI_m"], 1)
                pe.wait_ge(S["kI_v"], c.need("kI_v"))
                mm(bk(3, T, T), C("blk"), mt[:, 4, :], start=True, stop=True).then_inc(S["kI_var"], 1)
                pe.wait_ge(S["ml_n"], c.need("ml_n"))
                w = chunk(MIX_SLOTS, 2)
                proj(w[:, 0:2048].rearrange("p (k n) -> p k n", k=2), 8, cqk[:, 0:2], 2)
                proj(w[:, 2048:4096].rearrange("p (k n) -> p k n", k=2), 8, cqk[:, 2:4], 2)
                owed[0] += 1
                w = chunk(MIX_SLOTS, 2)
                proj_tok(w[:, 0:2048].rearrange("p (k n) -> p k n", k=2), cqk[:, 2:4], 2, 4)
                proj(w[:, 2048:3072].rearrange("p (k n) -> p k n", k=2), 4, cqk[:, 0:2], 2)
                owed[0] += 1
                pe.wait_ge(S["kI_n"], c.need("kI_n"))
                pe.wait_ge(S["proj_evac"], c.need("proj_evac", 0))
                for n in range(TT * 8):
                    qt, h = n // 8, n % 8
                    r = 64 * (h % 2)
                    due = c.need("ix_rl", 1, spare=4)
                    if due is not None:
                        pe.wait_ge(S["ix_rl"], due)
                    mm(bk(2 + h % 4, 0, 256), qI[r:r + 64, h // 2, qt * P:(qt + 1) * P], kI[r:r + 64, :], start=True, stop=True).then_inc(S["ix_full"], 1)
                pe.wait_ge(S["ix_rl"], c.need("ix_rl", 0))
                attention(8, 1)
                proj_chunks(2, feat)

            def to_residual(src):
                for h in range(2):
                    w = chunk(MIX_SLOTS).rearrange("p (k n) -> p k n", k=KT)
                    for t in range(TT):
                        for k in range(KT):
                            m = mm(bk(4 + 2 * h + t), src[:, k, t * P:(t + 1) * P], w[:, k, :], start=k == 0, stop=k == KT - 1)
                            if k == 0:
                                release(m)
                            if k == KT - 1:
                                m.then_inc(S["mix_full"], 1)
                    owed[0] += 1
                c.skip("x_new", 4)

            def xattn(l):
                proj_chunks(2, feat)
                proj_chunks(2, memf)
                for i in range(2):
                    w = chunk(MIX_SLOTS).rearrange("p (k n) -> p k n", k=KT)
                    proj_tok(w, memf, KT, 2)
                    owed[0] += 1
                pe.wait_ge(S["proj_evac"], c.need("proj_evac", 0))
                attention(4, 2)
                to_residual(branch)

            ngu = [0]

            nff = [0]

            def weights_of(*shape):
                b = nff[0] % FFN_BUFS
                nff[0] += 1
                pe.wait_ge(S["w_lo"], c.need("w_lo"))
                return [view(w_parts[b][i], 0, *shape) for i in range(2)]

            def ffn(steps):
                for f in range(steps):
                    wg = weights_of(KT, 2 * P)
                    wu = weights_of(KT, 2 * P)
                    for j in range(2):
                        b = ngu[0] % 4
                        ngu[0] += 1
                        due = c.need("act_t", 1, spare=4, view="bank")
                        if due is not None:
                            pe.wait_ge(S["act_t"], due)
                        for col, w in ((0, wg), (T, wu)):
                            for n, (wi, xi) in enumerate(PASSES):
                                for k in range(KT):
                                    m = mm(bk(b, col, T), w[wi][:, k, j * P:(j + 1) * P], feat_parts[xi][:, k, :],
                                           start=n == 0 and k == 0, stop=n == 2 and k == KT - 1)
                                    if n == 0 and k == 0 and not col and bufs_owed[0]:
                                        m.then_inc(S["wb_used"], bufs_owed[0])
                                        bufs_owed[0] = 0
                        m.then_inc(S["gu_full"], 1)
                    wd = weights_of(2, D)
                    if f == 0:
                        pe.wait_ge(S["x_new"], c.need("x_new", 0))
                    for j in range(2):
                        pe.wait_ge(S["act_t"], c.need("act_t"))
                        for t in range(TT):
                            for h in range(2):
                                for n, (wi, xi) in enumerate(PASSES):
                                    m = mm(bk(4 + 2 * t + h), act_parts[xi][:, nact[0] % 4, t * P:(t + 1) * P],
                                           wd[wi][:, j, h * 512:(h + 1) * 512],
                                           start=f == 0 and j == 0 and n == 0, stop=f == steps - 1 and j == 1 and n == 2)
                                    if j == 0 and t == 0 and h == 0 and n == 0:
                                        m.then_inc(S["wb_used"], 2)
                        nact[0] += 1
                    bufs_owed[0] = 1
                m.then_inc(S["down_full"], 1)
                c.skip("x_new", 4)

            nact = [0]
            bufs_owed = [0]

            pe.wait_ge(S["par_dma"], c.need("par_dma", 48))
            norm()
            for l in range(LAYERS):
                norm()
                pe_s.phase()
                rwkv(l)
                gdn(l)
                mla(l)
                pe.wait_ge(S["merged"], c.need("merged"))
                to_residual(yacc)
                norm()
                xattn(l)
                norm()
                pe_s.phase()
                if l == 0:
                    ffn(FF // 256)
                else:
                    for t in range(TT):
                        for k in range(KT):
                            m = mm(bk(3, 8 * t, 8), feat[:, k, t * P:(t + 1) * P], rout[:, k, :], start=k == 0, stop=k == KT - 1)
                            if t and k == KT - 1:
                                m.then_inc(S["rt_full"], 1)
                    pe.wait_ge(S["rt_l"], c.need("rt_l"))
                    ffn(FE // 256)
                    with pe.Fori(1, NE - 1) as e:
                        c.begin_loop(e - 1, dict(act_t=FE // P, x_new=4, w_lo=FE_CHUNKS))
                        ffn(FE // 256)
                    c.end_loop(NE - 2)
                    ffn(FE // 256)

        @block.scalar
        def _(act):
            c = Counter(S)

            sc = nc.scalar

            def norm(src, gain, l, dst):
                for t in range(TT):
                    act.wait_ge(*c.last())
                    sc.activation(sqj, src[:, t, :], ACT.Square, accum_out=small[:, t:t + 1]).then_inc(*c.inc("norm_ss"))
                act.wait_ge(S["norm_ms"], c.need("norm_ms"))
                act.wait_ge(*c.last())
                sc.activation(small[:, 4:6], small[:, 2:4], ACT.Sqrt).then_inc(*c.inc("norm_sd"))
                if dst is None:
                    return
                for k in range(KT):
                    if k % 2 == 0:
                        act.wait_ge(S["norm_T"], c.need("norm_T"))
                    act.wait_ge(*c.last())
                    sc.activation(dst[:, k, :], bk(4 + k // 2, (k % 2) * 256, T), ACT.Copy, scale=pc(l, gain, k)).then_inc(*c.inc("feat_ready"))

            nproj = [0]

            def evac(dst, f=ACT.Copy, **kw):
                n = nproj[0] % 2
                nproj[0] += 1
                act.wait_ge(S["proj_full"], c.need("proj_full"))
                act.wait_ge(*c.last())
                sc.activation(dst, bk(n, 0, 256) if dst.shape[-1] != 8 else
                  bk(n, 0, 16).rearrange("p (a b) -> p a b", a=2), f, **kw).then_inc(*c.inc("proj_evac"))

            def gates_of():
                for j in range(KT):
                    due = c.need("gate_free", 1, spare=4)
                    if due is not None:
                        act.wait_ge(S["gate_free"], due)
                    evac(gate[:, j % 4, :], ACT.Sigmoid)

            def rwkv(l):
                for n in range(25):
                    due = c.need("raw_free", 1, spare=4)
                    if due is not None:
                        act.wait_ge(S["raw_free"], due)
                    evac(raw[:, n % 4, 3:259])
                act.wait_ge(S["raw_free"], c.need("raw_free", 0))
                if l == 0:
                    act.wait_ge(*c.last())
                    sc.activation(vfirst[:, :, :], rkv[:, 16:24, :], ACT.Copy).then_inc(*c.inc("act_step"))
                act.wait_ge(*c.last())
                sc.activation(lora[0:64, :], lora[0:64, :], ACT.Tanh).then_inc(*c.inc("rkv_ready"))
                if l:
                    act.wait_ge(S["vlow_full"], c.need("vlow_full"))
                    act.wait_ge(*c.last())
                    sc.activation(vlo[0:32, :], bk(2, 0, T)[0:32], ACT.Copy).then_inc(*c.inc("vlow"))
                    for j in range(KT):
                        act.wait_ge(S["vres_full"], c.need("vres_full"))
                        due = c.need("vres_done", 1, spare=2)
                        if due is not None:
                            act.wait_ge(S["vres_done"], due)
                        act.wait_ge(*c.last())
                        sc.activation(tmp[:, j % 2, :], bk(3 + j % 2, 0, T), ACT.Sigmoid, bias=pc(l, "v0", j)).then_inc(*c.inc("vres_sig"))
                for j in range(RW_PAIRS):
                    if l and j == 0:
                        act.wait_ge(S["vres_done"], c.need("vres_done", 0))
                    act.wait_ge(*c.last())
                    sc.activation(VV[0:64, :, 64:128], rkv[0:64, 16 + j, :].rearrange("p (a b) -> p a b", a=4), ACT.Copy).then_inc(*c.inc("act_step"))
                    act.wait_ge(*c.last())
                    sc.activation(VV[64:128, :, 0:64], rkv[64:128, 16 + j, :].rearrange("p (a b) -> p a b", a=4), ACT.Copy).then_inc(*c.inc("rw_vv"))
                    act.wait_ge(S["rw_lora"], c.need("rw_lora"))
                    act.wait_ge(*c.last())
                    sc.activation(tmp[:, 0, :], bk(2, 0, T), ACT.Sigmoid, bias=pc(l, "w0", j)).then_inc(*c.inc("act_step"))
                    act.wait_ge(*c.last())
                    sc.activation(tmp[:, 8, :], bk(3, 0, T), ACT.Sigmoid, bias=pc(l, "a0", j)).then_inc(*c.inc("rw_sig"))
                    act.wait_ge(S["rw_cum"], c.need("rw_cum"))
                    act.wait_ge(*c.last())
                    sc.activation(tmp[:, 3, :], tmp[:, 1, :], ACT.Exp, scale=-DECAY).then_inc(*c.inc("act_step"))
                    act.wait_ge(*c.last())
                    sc.activation(tmp[:, 4, :], tmp[:, 2, :], ACT.Exp, scale=-DECAY).then_inc(*c.inc("act_step"))
                    act.wait_ge(*c.last())
                    sc.activation(tmp[:, 6, :], tmp[:, 1, :], ACT.Exp, scale=DECAY).then_inc(*c.inc("rw_exp"))
                    act.wait_ge(S["rw_nrm"], c.need("rw_nrm"))
                    act.wait_ge(*c.last())
                    sc.activation(tmp[:, 13, :], tmp[:, 11, :], ACT.Sqrt).then_inc(*c.inc("rw_sqrt"))
                    act.wait_ge(S["rw_tr"], c.need("rw_tr"))
                    act.wait_ge(*c.last())
                    sc.activation(BKt[:, j % 4], bk4(5), ACT.Copy).then_inc(*c.inc("act_step"))
                    act.wait_ge(*c.last())
                    sc.activation(Vad[:, j % 4], bk4(6), ACT.Copy).then_inc(*c.inc("rw_tm"))
                    if j % 4 == 3:
                        for q in range(RW_CHUNKS):
                            act.wait_ge(S["rc_OT"], c.need("rc_OT"))
                            for lo in (0, 64):
                                act.wait_ge(*c.last())
                                sc.activation(branch[lo:lo + 64, j - 3:j + 1, 64 * q:64 * q + 64], bk4(4)[lo:lo + 64, :, 64 - lo:128 - lo], ACT.Copy).then_inc(*c.inc("rc_Of" if lo else "act_step"))
                for i in range(4):
                    act.wait_ge(S["gn_var"], c.need("gn_var"))
                    act.wait_ge(*c.last())
                    sc.activation(tmp[:, 4:6, :], tmp[:, 2:4, :], ACT.Sqrt).then_inc(*c.inc("gn_sd"))
                gates_of()

            def gdn(l):
                for n in range(24):
                    due = c.need("raw_free", 1, spare=4)
                    if due is not None:
                        act.wait_ge(S["raw_free"], due)
                    if n >= 2:
                        act.wait_ge(S["raw_free"], 49 * l + 25 + n - 1)
                        act.wait_ge(*c.last())
                        sc.activation(rkv[:, n - 2, :], rkv[:, n - 2, :], ACT.Silu).then_inc(*c.inc("act_step"))
                    evac(raw[:, n % 4, 3:259])
                for n in (22, 23):
                    act.wait_ge(S["raw_free"], 49 * l + 25 + n + 1)
                    act.wait_ge(*c.last())
                    sc.activation(rkv[:, n, :], rkv[:, n, :], ACT.Silu).then_inc(*c.inc("rkv_ready" if n == 23 else "act_step"))
                act.wait_ge(S["gd_ab"], c.need("gd_ab", 2))
                act.wait_ge(*c.last())
                sc.activation(b8[0:8, :], bk(3, 0, T)[0:8], ACT.Sigmoid).then_inc(*c.inc("act_step"))
                act.wait_ge(*c.last())
                sc.activation(ab[0:8, 0, :], bk(2, 0, T)[0:8], ACT.Abs, bias=pc(l, "dt_bias")[0:8]).then_inc(*c.inc("act_step"))
                act.wait_ge(*c.last())
                sc.activation(ab[0:8, 3, :], bk(2, 0, T)[0:8], ACT.Relu, bias=pc(l, "dt_bias")[0:8]).then_inc(*c.inc("act_step"))
                act.wait_ge(*c.last())
                sc.activation(small[0:8, 8:9], pc(l, "A_log")[0:8], ACT.Exp).then_inc(*c.inc("act_step"))
                act.wait_ge(*c.last())
                sc.activation(ab[0:8, 1, :], ab[0:8, 0, :], ACT.Exp, scale=-1.0).then_inc(*c.inc("act_step"))
                act.wait_ge(*c.last())
                sc.activation(ab[0:8, 2, :], ab[0:8, 1, :], ACT.Ln, bias=1.0).then_inc(*c.inc("gd_abs"))
                for h in range(GH):
                    hh = h % 4
                    act.wait_ge(S["gd_bc"], c.need("gd_bc"))
                    act.wait_ge(*c.last())
                    sc.activation(gt[:, 2, :], bk(3, 0, T), ACT.Exp).then_inc(*c.inc("gd_eg"))
                    act.wait_ge(S["gd_nrm"], c.need("gd_nrm"))
                    act.wait_ge(*c.last())
                    sc.activation(gt[:, 6:8, :], gt[:, 4:6, :], ACT.Sqrt).then_inc(*c.inc("gd_sqrt"))
                    act.wait_ge(S["gd_dif"], c.need("gd_dif"))
                    act.wait_ge(*c.last())
                    sc.activation(small[:, 32 + h:33 + h], small[:, 24 + h:25 + h], ACT.Exp).then_inc(*c.inc("act_step"))
                    act.wait_ge(*c.last())
                    sc.activation(dec, dec, ACT.Exp).then_inc(*c.inc("gd_dec"))
                    act.wait_ge(S["gd_tr"], c.need("gd_tr"))
                    act.wait_ge(*c.last())
                    sc.activation(ktm[:, hh, :], bk(6, 0, P), ACT.Copy, scale=small[:, 32 + h:33 + h]).then_inc(*c.inc("act_step"))
                    act.wait_ge(*c.last())
                    sc.activation(vtm[:, hh].rearrange("p a b -> p (a b)"), bk(6, P, T), ACT.Copy).then_inc(*c.inc("gd_tm"))
                    if hh == 3:
                        for t in range(TT):
                            act.wait_ge(S["gr_O"], c.need("gr_O"))
                            act.wait_ge(*c.last())
                            sc.activation(branch[:, h - 3:h + 1, t * P:(t + 1) * P], bk4(3 + t), ACT.Copy).then_inc(*c.inc("gr_Of"))
                for i in range(4):
                    act.wait_ge(S["gt_ms"], c.need("gt_ms"))
                    act.wait_ge(*c.last())
                    sc.activation(gt[:, 4:6, :], gt[:, 2:4, :], ACT.Sqrt).then_inc(*c.inc("gt_sd"))
                gates_of()

            def attention(heads, kt, masked):
                for h in range(heads):
                    act.wait_ge(S["at_max"], c.need("at_max"))
                    for qt in range(TT):
                        src = Lm[:, h % 2, qt * T:(qt + 1) * T] if masked else bk(2 + h % 2, qt * T, T)
                        act.wait_ge(*c.last())
                        sc.activation(Pr[:, h % 2, qt * T:(qt + 1) * T], src, ACT.Exp, bias=amax[:, h % 2, qt:qt + 1], accum_out=asum[:, h % 2, qt:qt + 1]).then_inc(*c.inc("at_exp"))
                    act.wait_ge(S["at_T"], c.need("at_T"))
                    act.wait_ge(*c.last())
                    sc.activation(PT[:, h % 2, :], bk(4 + h % 2), ACT.Copy).then_inc(*c.inc("at_PT"))
                    for d in range(kt):
                        j = h * kt + d
                        act.wait_ge(S["at_O"], c.need("at_O"))
                        act.wait_ge(*c.last())
                        sc.activation(branch[:, j, :], bk(6 + j % 2, 0, T), ACT.Copy).then_inc(*c.inc("at_Of"))

            def mla(l):
                for n in range(4):
                    evac(cqk[:, n, :])
                evac(kI)
                evac(wI, scale=8 ** -0.5 * 64 ** -0.5)
                act.wait_ge(S["kI_ms"], c.need("kI_ms"))
                act.wait_ge(*c.last())
                sc.activation(mt[:, 5, :], mt[:, 4, :], ACT.Sqrt).then_inc(*c.inc("kI_sd"))
                act.wait_ge(S["ml_ms"], c.need("ml_ms"))
                act.wait_ge(*c.last())
                sc.activation(mt[:, 2:4, :], mt[:, 0:2, :], ACT.Sqrt).then_inc(*c.inc("ml_sd"))
                for n in range(8):
                    evac(qf[:, n, :], scale=P ** -0.5)
                for n in range(8):
                    evac(kf[:, n, :])
                for n in range(8):
                    evac(vt[:, n // 4, (n % 4) * 256:(n % 4 + 1) * 256])
                for n in range(4):
                    evac(qI[:, n, :])
                for n in range(16):
                    h = n % 8
                    act.wait_ge(S["ix_full"], c.need("ix_full"))
                    due = c.need("ix_free", 1, spare=4)
                    if due is not None:
                        act.wait_ge(S["ix_free"], due)
                    act.wait_ge(*c.last())
                    sc.activation(rl[:, n % 4, :], bk(2 + h % 4, 0, 256), ACT.Relu).then_inc(*c.inc("ix_rl"))
                attention(8, 1, True)
                gates_of()

            def xattn(l):
                for n in range(8):
                    evac(qf[:, n, :], scale=256 ** -0.5)
                for n in range(8):
                    evac(kf[:, n, :])
                for i in range(2):
                    for n in range(4):
                        t, q = n // 2, n % 2
                        evac(vt[:, t, i * 512 + q * 256:i * 512 + (q + 1) * 256])
                attention(4, 2, False)

            nf = [0]

            nff = [0]

            def high_part():
                n = nff[0]
                nff[0] += 1
                b = n % FFN_BUFS
                act.wait_ge(S[f"fslot{b}"], c.need(f"fslot{b}", 16))
                due = c.need("wb_used", 1, spare=FFN_BUFS)
                if due is not None:
                    act.wait_ge(S["wb_used"], due)
                sc.activation(w_parts[b][0], ring[:, b * FFN_SLOT:(b + 1) * FFN_SLOT], ACT.Copy).then_inc(*c.inc("w_hi"))

            def ffn(steps, more=False):
                for f in range(steps):
                    for j in range(2):
                        n = nf[0] % 4
                        nf[0] += 1
                        act.wait_ge(S["gu_full"], c.need("gu_full"))
                        sc.activation(silu_t[:, n, :], bk(n, 0, T), ACT.Silu).then_inc(*c.inc("silu"))
                        if f < steps - 1 or more:
                            high_part()
                    if f < steps - 1 or more:
                        high_part()

            act.wait_ge(S["par_dma"], 48)
            sc.activation(small[0:1, 78:79], par[0:1, 0, 0:1], ACT.Copy).then_inc(*c.inc("act_step"))
            act.wait_ge(S["mem_dma"], 16)
            norm(yflat.rearrange("p (a b) -> p a b", a=TT), "mem_norm", 0, memf)
            act.wait_ge(S["in_dma"], 16)
            for l in range(LAYERS):
                if l:
                    act.wait_ge(S["x_new"], c.need("x_new", 4))
                norm(xt, "norm_mix", l, feat)
                rwkv(l)
                gdn(l)
                mla(l)
                act.wait_ge(S["x_new"], c.need("x_new", 4))
                norm(xt, "norm_xattn", l, feat)
                xattn(l)
                act.wait_ge(S["x_new"], c.need("x_new", 4))
                norm(xt, "norm_ffn", l, feat)
                act.wait_ge(*c.last())
                sc.activation(feat_parts[0], feat[:, :, :], ACT.Copy).then_inc(*c.inc("f_hi"))
                for _ in range(3):
                    high_part()
                if l == 0:
                    ffn(FF // 256)
                else:
                    act.wait_ge(S["rt_d"], c.need("rt_d"))
                    sc.activation(small[:, 44:46], small[:, 42:44], ACT.Exp).then_inc(*c.inc("rt_e"))
                    ffn(FE // 256, True)
                    with act.Fori(1, NE - 1) as e:
                        c.begin_loop(e - 1, dict(gu_full=FE // P, wb_used=FE_CHUNKS,
                                                 **{f"fslot{b}": 16 * FE_CHUNKS // FFN_BUFS for b in range(FFN_BUFS)}))
                        ffn(FE // 256, True)
                    c.end_loop(NE - 2)
                    ffn(FE // 256)
            act.wait_ge(S["x_new"], c.need("x_new", 4 * NE))
            norm(xt, None, 0, None)

        @block.vector
        def _(dve):
            c = Counter(S)

            v = nc.vector

            def norm(src, final=False):
                dve.wait_ge(S["norm_ss"], c.need("norm_ss", 2))
                v.tensor_scalar(small[:, 2:4], small[:, 0:2], 1.0 / D, EPS, ALU.mult, ALU.add).then_inc(*c.inc("norm_ms"))
                dve.wait_ge(*c.last())
                dve.wait_ge(S["norm_sd"], c.need("norm_sd"))
                v.reciprocal(small[:, 6:8], small[:, 4:6]).then_inc(*c.inc("dve_step"))
                dve.wait_ge(*c.last())
                for t in range(TT):
                    if final:
                        if t == 0:
                            dve.wait_ge(S["par_dma"], 64)
                        v.scalar_tensor_tensor(yflat[:, t * D:(t + 1) * D], src[:, t, :], small[:, 6 + t:7 + t],
                                                 memf[:, 0:4, :].rearrange("p a b -> p (a b)"), ALU.mult, ALU.mult).then_inc(*c.inc("norm_xn"))
                        dve.wait_ge(*c.last())
                    else:
                        v.tensor_scalar(xn[:, t, :], src[:, t, :], small[:, 6 + t:7 + t], None, ALU.mult).then_inc(*c.inc("norm_xn"))
                        dve.wait_ge(*c.last())

            def pad_raw():
                for n in range(4):
                    v.memset(raw[:, n, 0:3], 0.0).then_inc(*c.inc("dve_step"))
                    dve.wait_ge(*c.last())

            def gated(first, last):
                for j in range(KT):
                    dve.wait_ge(S["proj_evac"], c.need("proj_evac"))
                    if first:
                        v.tensor_tensor(yacc[:, j, :], gate[:, j % 4, :], branch[:, j, :], ALU.mult).then_inc(*c.inc("gate_free"))
                        dve.wait_ge(*c.last())
                    else:
                        v.tensor_tensor(branch[:, j, :], gate[:, j % 4, :], branch[:, j, :], ALU.mult).then_inc(*c.inc("gate_free"))
                        dve.wait_ge(*c.last())
                        v.tensor_tensor(yacc[:, j, :], yacc[:, j, :], branch[:, j, :], ALU.add).then_inc(*c.inc("merged" if last and j == KT - 1 else "dve_step"))
                        dve.wait_ge(*c.last())

            def inverted(levels, xtv, xv, yv, b0):
                ident = b4(C("ident"))
                for b in range(levels):
                    dve.wait_ge(S["inv_Y"], c.need("inv_Y"))
                    v.tensor_tensor(yv, bk4(b0), b4(C("level", P * b, P * b + P)), ALU.mult).then_inc(*c.inc("inv_Ym"))
                    dve.wait_ge(*c.last())
                    if b == 0:
                        v.tensor_tensor(xv, ident, yv, ALU.add).then_inc(*c.inc("dve_step"))
                        dve.wait_ge(*c.last())
                    dve.wait_ge(S["inv_D"], c.need("inv_D"))
                    if 0 < b < levels - 1:
                        v.tensor_tensor(xv, bk4(b0 + 1), xv, ALU.add).then_inc(*c.inc("dve_step"))
                        dve.wait_ge(*c.last())
                    v.tensor_tensor(xtv, bk4(b0 + 2), xtv if b else ident, ALU.add).then_inc(*c.inc("inv_X"))
                    dve.wait_ge(*c.last())

            def r4(ap):
                return ap.rearrange("p (a b) -> p a b", a=4)

            def rwkv(l):
                pad_raw()
                for n in range(25):
                    dst = rkv[:, n, :] if n < 24 else lora
                    dve.wait_ge(S["proj_evac"], c.need("proj_evac"))
                    v.tensor_tensor(dst, raw[:, n % 4, 2:258], raw[:, n % 4, 3:259], ALU.subtract).then_inc(*c.inc("dve_step"))
                    dve.wait_ge(*c.last())
                    v.scalar_tensor_tensor(dst, dst, pc(l, "mu", n), raw[:, n % 4, 3:259], ALU.mult, ALU.add).then_inc(*c.inc("raw_free"))
                    dve.wait_ge(*c.last())
                v.memset(NT, 0.0).then_inc(*c.inc("dve_step"))
                dve.wait_ge(*c.last())
                if l:
                    for j in range(KT):
                        d = tmp[:, 2 + j % 2, :]
                        v.tensor_tensor(d, vfirst[:, j, :], rkv[:, 16 + j, :], ALU.subtract).then_inc(*c.inc("dve_step"))
                        dve.wait_ge(*c.last())
                        dve.wait_ge(S["vres_sig"], c.need("vres_sig"))
                        v.tensor_tensor(d, d, tmp[:, j % 2, :], ALU.mult).then_inc(*c.inc("dve_step"))
                        dve.wait_ge(*c.last())
                        v.tensor_tensor(rkv[:, 16 + j, :], rkv[:, 16 + j, :], d, ALU.add).then_inc(*c.inc("vres_done"))
                        dve.wait_ge(*c.last())
                for lo in (0, 64):
                    v.memset(VV[lo:lo + 64, :, lo:lo + 64], 0.0).then_inc(*c.inc("dve_step"))
                    dve.wait_ge(*c.last())
                for j in range(RW_PAIRS):
                    jj = j % 4
                    r_, k_, v_ = rkv[:, j, :], rkv[:, 8 + j, :], rkv[:, 16 + j, :]
                    t_ = lambda n: tmp[:, n, :]
                    dve.wait_ge(S["rw_sig"], c.need("rw_sig"))
                    for q in range(4):
                        s = slice(64 * q, 64 * q + 64)
                        v.tensor_tensor_scan(tmp[:, 1, s], C("ones")[:, 0:64], tmp[:, 0, s], 0.0, ALU.mult, ALU.add).then_inc(*c.inc("dve_step"))
                        dve.wait_ge(*c.last())
                    v.tensor_tensor(t_(2), t_(1), t_(0), ALU.subtract).then_inc(*c.inc("rw_cum"))
                    dve.wait_ge(*c.last())
                    v.tensor_scalar(t_(9), k_, pc(l, "k_k", j), None, ALU.mult).then_inc(*c.inc("dve_step"))
                    dve.wait_ge(*c.last())
                    v.tensor_tensor(t_(5), t_(9), t_(9), ALU.mult).then_inc(*c.inc("rw_kksq"))
                    dve.wait_ge(*c.last())
                    v.tensor_scalar(t_(12), t_(8), -1.0, pc(l, "k_a", j), ALU.add, ALU.mult).then_inc(*c.inc("dve_step"))
                    dve.wait_ge(*c.last())
                    v.scalar_tensor_tensor(t_(10), t_(12), 1.0, k_, ALU.add, ALU.mult).then_inc(*c.inc("dve_step"))
                    dve.wait_ge(*c.last())
                    v.scalar_tensor_tensor(t_(7), r_, pc(l, "r_k", j), t_(10), ALU.mult, ALU.mult).then_inc(*c.inc("rw_bon"))
                    dve.wait_ge(*c.last())
                    dve.wait_ge(S["rw_sums"], c.need("rw_sums"))
                    v.tensor_scalar(t_(11), bk(4, 0, T), EPS, None, ALU.add).then_inc(*c.inc("rw_nrm"))
                    dve.wait_ge(*c.last())
                    v.tensor_tensor(k_, bk(4, T, T), v_, ALU.mult).then_inc(*c.inc("dve_step"))
                    dve.wait_ge(*c.last())
                    dve.wait_ge(S["rw_sqrt"], c.need("rw_sqrt"))
                    v.reciprocal(t_(11), t_(13)).then_inc(*c.inc("dve_step"))
                    dve.wait_ge(*c.last())
                    v.tensor_tensor(t_(9), t_(9), t_(11), ALU.mult).then_inc(*c.inc("dve_step"))
                    dve.wait_ge(*c.last())
                    v.tensor_tensor(t_(12), t_(9), t_(8), ALU.mult).then_inc(*c.inc("dve_step"))
                    dve.wait_ge(*c.last())
                    dve.wait_ge(S["rw_exp"], c.need("rw_exp"))
                    for lo in (0, 64):
                        p_ = slice(lo, lo + 64)
                        za, zb = slice(lo, lo + 64), slice(64 - lo, 128 - lo)
                        f = lambda n: r4(tmp[p_, n, :])
                        v.scalar_tensor_tensor(ZR[p_, jj, :, za], f(9), -1.0, f(4), ALU.mult, ALU.mult).then_inc(*c.inc("dve_step"))
                        dve.wait_ge(*c.last())
                        v.tensor_tensor(ZR[p_, jj, :, zb], r4(rkv[p_, j, :]), f(3), ALU.mult).then_inc(*c.inc("dve_step"))
                        dve.wait_ge(*c.last())
                        v.tensor_tensor(BK[p_, :, za], f(12), f(6), ALU.mult).then_inc(*c.inc("dve_step"))
                        dve.wait_ge(*c.last())
                        v.tensor_tensor(BK[p_, :, zb], f(10), f(6), ALU.mult).then_inc(*c.inc("dve_step"))
                        dve.wait_ge(*c.last())
                    v.tensor_copy(wc[:, jj, :], tmp[:, 3, 63:T:64]).then_inc(*c.inc("rw_fm"))
                    dve.wait_ge(*c.last())
                    dve.wait_ge(S["rw_G"], c.need("rw_G"))
                    v.tensor_tensor(GA[:, jj], bk4(7), b4(C("maskGA")), ALU.mult).then_inc(*c.inc("dve_step"))
                    dve.wait_ge(*c.last())
                    v.tensor_tensor(GB[:, jj], bk4(2), b4(C("maskGB")), ALU.mult).then_inc(*c.inc("dve_step"))
                    dve.wait_ge(*c.last())
                    v.tensor_copy(NT[0:64, :, 0:64], GA[0:64, jj, :, 0:64]).then_inc(*c.inc("dve_step"))
                    dve.wait_ge(*c.last())
                    v.tensor_copy(NT[64:128, :, 64:128], GB[64:128, jj, :, 64:128]).then_inc(*c.inc("rw_N"))
                    dve.wait_ge(*c.last())
                    inverted(6, XT[:, jj], X, Ym, 3)
                    if jj == 3:
                        recur_rw(j)
                for i in range(4):
                    o = branch[:, 2 * i:2 * i + 2, :]
                    b2 = lambda n: bank[n][:, :].rearrange("p (a b) -> p a b", a=2)
                    dve.wait_ge(S["gn_m"], c.need("gn_m"))
                    v.scalar_tensor_tensor(o, b2(5), -1.0 / 64, o, ALU.mult, ALU.add).then_inc(*c.inc("dve_step"))
                    dve.wait_ge(*c.last())
                    v.tensor_tensor(tmp[:, 0:2, :], o, o, ALU.mult).then_inc(*c.inc("gn_sq"))
                    dve.wait_ge(*c.last())
                    dve.wait_ge(S["gn_v"], c.need("gn_v"))
                    v.tensor_scalar(tmp[:, 2:4, :], b2(6), 1.0 / 64, GN_EPS, ALU.mult, ALU.add).then_inc(*c.inc("gn_var"))
                    dve.wait_ge(*c.last())
                    dve.wait_ge(S["gn_sd"], c.need("gn_sd"))
                    v.reciprocal(tmp[:, 6:8, :], tmp[:, 4:6, :]).then_inc(*c.inc("dve_step"))
                    dve.wait_ge(*c.last())
                    v.tensor_tensor(o, o, tmp[:, 6:8, :], ALU.mult).then_inc(*c.inc("dve_step"))
                    dve.wait_ge(*c.last())
                    for j in (2 * i, 2 * i + 1):
                        v.tensor_scalar(branch[:, j, :], branch[:, j, :], pc(l, "gn_g", j), pc(l, "gn_b", j), ALU.mult, ALU.add).then_inc(*c.inc("dve_step"))
                        dve.wait_ge(*c.last())
                    v.tensor_tensor(o, o, rkv[:, 8 + 2 * i:10 + 2 * i, :], ALU.add).then_inc(*c.inc("gn_y"))
                    dve.wait_ge(*c.last())
                gated(True, False)

            def recur_rw(j):
                for q in range(RW_CHUNKS):
                    dve.wait_ge(S["rc_P1"], c.need("rc_P1"))
                    v.tensor_tensor(Rbd, bk4(6), b4(C("maskbd")), ALU.mult).then_inc(*c.inc("rc_R"))
                    dve.wait_ge(*c.last())
                    dve.wait_ge(S["rc_U"], c.need("rc_U"))
                    v.tensor_tensor(UV, bk4(7), Vad[:, :, q, :], ALU.add).then_inc(*c.inc("rc_UV"))
                    dve.wait_ge(*c.last())
                    more = q < RW_CHUNKS - 1
                    if more:
                        dve.wait_ge(S["rc_S"], c.need("rc_S"))
                        if q:
                            v.tensor_tensor(Stmp, bk4(3), Sst, ALU.add).then_inc(*c.inc("dve_step"))
                            dve.wait_ge(*c.last())
                    dve.wait_ge(S["rc_P2"], c.need("rc_P2"))
                    v.tensor_tensor(Oad, bk4(2), b4(C("antibd")), ALU.mult).then_inc(*c.inc("rc_O"))
                    dve.wait_ge(*c.last())
                    if more:
                        for jj in range(4):
                            v.scalar_tensor_tensor(Sst[:, jj, :], Stmp[:, jj, :] if q else bk(3, jj * P, P),
                                                     wc[:, jj, q:q + 1], C("maskbd"), ALU.mult, ALU.mult).then_inc(*c.inc("rc_Sn" if jj == 3 else "dve_step"))
                            dve.wait_ge(*c.last())

            def gdn(l):
                pad_raw()
                for n in range(24):
                    dst = rkv[:, n, :]
                    dve.wait_ge(S["proj_evac"], c.need("proj_evac"))
                    v.tensor_scalar(dst, raw[:, n % 4, 0:256], pc(l, "conv", n), None, ALU.mult).then_inc(*c.inc("dve_step"))
                    dve.wait_ge(*c.last())
                    for i in range(1, 4):
                        v.scalar_tensor_tensor(dst, raw[:, n % 4, i:i + 256], pc(l, "conv", 24 * i + n), dst,
                                                 ALU.mult, ALU.add).then_inc(*c.inc("raw_free" if i == 3 else "dve_step"))
                        dve.wait_ge(*c.last())
                dve.wait_ge(S["rkv_ready"], c.need("rkv_ready", 2))
                dve.wait_ge(S["gd_abs"], c.need("gd_abs"))
                v.tensor_tensor(ab[0:8, 2, :], ab[0:8, 2, :], ab[0:8, 3, :], ALU.add).then_inc(*c.inc("dve_step"))
                dve.wait_ge(*c.last())
                v.tensor_scalar(ab[0:8, 2, :], ab[0:8, 2, :], small[0:8, 8:9], -1.0, ALU.mult, ALU.mult).then_inc(*c.inc("dve_step"))
                dve.wait_ge(*c.last())
                for t in range(TT):
                    s = slice(t * P, t * P + P)
                    v.tensor_tensor_scan(g8[0:8, s], C("ones")[0:8, :], ab[0:8, 2, s], 0.0, ALU.mult, ALU.add).then_inc(*c.inc("gd_g" if t else "dve_step"))
                    dve.wait_ge(*c.last())
                dve.wait_ge(S["gd_gT"], c.need("gd_gT"))
                v.tensor_copy(gbt, bk(4, 0, 32).rearrange("p (a b) -> p a b", a=2)).then_inc(*c.inc("dve_step"))
                dve.wait_ge(*c.last())
                t2 = lambda ap: ap.rearrange("p (a b) -> p a b", a=2)
                for h in range(GH):
                    hh = h % 4
                    q_, k_ = rkv[:, h, :], rkv[:, 8 + h, :]
                    v.tensor_tensor(gt[:, 0, :], q_, q_, ALU.mult).then_inc(*c.inc("dve_step"))
                    dve.wait_ge(*c.last())
                    v.tensor_tensor(gt[:, 1, :], k_, k_, ALU.mult).then_inc(*c.inc("gd_sq"))
                    dve.wait_ge(*c.last())
                    dve.wait_ge(S["gd_ss"], c.need("gd_ss"))
                    v.tensor_scalar(gt[:, 4:6, :], t2(bk(2)), EPS, None, ALU.add).then_inc(*c.inc("gd_nrm"))
                    dve.wait_ge(*c.last())
                    dve.wait_ge(S["gd_eg"], c.need("gd_eg"))
                    for t in range(TT):
                        v.tensor_scalar(dec[:, t, :], bk(3, t * P, P), gbt[:, t, h:h + 1], 0.0, ALU.subtract, ALU.min).then_inc(*c.inc("dve_step"))
                        dve.wait_ge(*c.last())
                    v.tensor_scalar(small[:, 24 + h:25 + h], gbt[:, 0, h:h + 1], -1.0, bk(3, P - 1, 1), ALU.mult, ALU.add).then_inc(*c.inc("gd_dif"))
                    dve.wait_ge(*c.last())
                    dve.wait_ge(S["gd_sqrt"], c.need("gd_sqrt"))
                    v.reciprocal(gt[:, 6:8, :], gt[:, 6:8, :]).then_inc(*c.inc("dve_step"))
                    dve.wait_ge(*c.last())
                    v.tensor_tensor(gt[:, 3, :], k_, gt[:, 7, :], ALU.mult).then_inc(*c.inc("dve_step"))
                    dve.wait_ge(*c.last())
                    v.scalar_tensor_tensor(kq[:, :, 1, :], t2(q_), P ** -0.5, t2(gt[:, 6, :]), ALU.mult, ALU.mult).then_inc(*c.inc("dve_step"))
                    dve.wait_ge(*c.last())
                    v.tensor_tensor(kq[:, :, 0, :], t2(gt[:, 3, :]), t2(bk(3, T, T)), ALU.mult).then_inc(*c.inc("dve_step"))
                    dve.wait_ge(*c.last())
                    v.tensor_tensor(ke[:, hh, :], gt[:, 3, :], gt[:, 2, :], ALU.mult).then_inc(*c.inc("dve_step"))
                    dve.wait_ge(*c.last())
                    v.tensor_tensor(t2(qe[:, hh, :]), kq[:, :, 1, :], t2(gt[:, 2, :]), ALU.mult).then_inc(*c.inc("gd_fm"))
                    dve.wait_ge(*c.last())
                    dve.wait_ge(S["gd_kk"], c.need("gd_kk"))
                    dve.wait_ge(S["gd_dec"], c.need("gd_dec"))
                    m = gt[:, 8:10, :].rearrange("p t (b c) -> p t b c", b=2)
                    v.tensor_tensor(m, bk(5).rearrange("p (a b c) -> p a b c", a=2, b=2),
                                      dec.unsqueeze(2).to_broadcast([P, TT, 2, P]), ALU.mult).then_inc(*c.inc("dve_step"))
                    dve.wait_ge(*c.last())
                    v.tensor_tensor(gNT[:, hh], m[:, :, 0, :], b4(C("gdnmask", 0, P), 2), ALU.mult).then_inc(*c.inc("dve_step"))
                    dve.wait_ge(*c.last())
                    v.tensor_tensor(gAT[:, hh], m[:, :, 1, :], b4(C("gdnmask", P, 2 * P), 2), ALU.mult).then_inc(*c.inc("gd_N"))
                    dve.wait_ge(*c.last())
                    if h % 2:
                        inverted(7, gXT[:, hh - 1:hh + 1].rearrange("p a b c -> p (a b) c"), gX, gYm, 2)
                    if hh == 3:
                        recur_gd(h - 3)
                dve.wait_ge(S["gr_Of"], c.need("gr_Of", 4))
                for i in range(4):
                    o = branch[:, 2 * i:2 * i + 2, :]
                    v.tensor_tensor(gt[:, 0:2, :], o, o, ALU.mult).then_inc(*c.inc("gt_sq"))
                    dve.wait_ge(*c.last())
                    dve.wait_ge(S["gt_ss"], c.need("gt_ss"))
                    v.tensor_scalar(gt[:, 2:4, :], t2(bk(2)), 1.0 / P, EPS, ALU.mult, ALU.add).then_inc(*c.inc("gt_ms"))
                    dve.wait_ge(*c.last())
                    dve.wait_ge(S["gt_sd"], c.need("gt_sd"))
                    v.reciprocal(gt[:, 6:8, :], gt[:, 4:6, :]).then_inc(*c.inc("dve_step"))
                    dve.wait_ge(*c.last())
                    v.scalar_tensor_tensor(o, o, pc(l, "gdn_norm"), gt[:, 6:8, :], ALU.mult, ALU.mult).then_inc(*c.inc("gn_y" if i == 3 else "dve_step"))
                    dve.wait_ge(*c.last())
                gated(False, False)

            def recur_gd(h0):
                for t in range(TT):
                    src = vtm[:, :, t, :]
                    if t == 0:
                        dve.wait_ge(S["gd_tm"], c.need("gd_tm", 4))
                    else:
                        dve.wait_ge(S["gr_in"], c.need("gr_in"))
                        v.tensor_tensor(gR, src, bk4(5), ALU.subtract).then_inc(*c.inc("dve_step"))
                        dve.wait_ge(*c.last())
                        src = gR
                    for i in range(4):
                        v.tensor_scalar(gR[:, i, :], src[:, i, :], gbt[:, t, 8 + h0 + i:9 + h0 + i], None, ALU.mult).then_inc(*c.inc("gr_R" if i == 3 else "dve_step"))
                        dve.wait_ge(*c.last())
                    dve.wait_ge(S["gr_V"], c.need("gr_V"))
                    v.tensor_copy(gV, bk4(6)).then_inc(*c.inc("gr_Vs"))
                    dve.wait_ge(*c.last())
                    if t == 0:
                        dve.wait_ge(S["gr_S"], c.need("gr_S"))
                        v.tensor_copy(gS, bk4(7)).then_inc(*c.inc("gr_Ss"))
                        dve.wait_ge(*c.last())

            def attention(heads, masked):
                neg = negm.rearrange("p a b -> p (a b)")
                for h in range(heads):
                    dve.wait_ge(S["at_L"], c.need("at_L"))
                    if masked:
                        v.tensor_tensor(Lm[:, h % 2, :], bk(2 + h % 2), neg, ALU.add).then_inc(*c.inc("dve_step"))
                        dve.wait_ge(*c.last())
                        src = Lm[:, h % 2, :]
                    else:
                        src = bk(2 + h % 2)
                    v.tensor_reduce(amax[:, h % 2, :], src.rearrange("p (a b) -> p a b", a=2), AX.X, ALU.max,
                                      negate=True).then_inc(*c.inc("at_max"))
                    dve.wait_ge(*c.last())
                    dve.wait_ge(S["at_exp"], c.need("at_exp", 2))
                    v.reciprocal(ainv[:, h % 2, :], asum[:, h % 2, :]).then_inc(*c.inc("dve_step"))
                    dve.wait_ge(*c.last())
                    for qt in range(TT):
                        s = slice(qt * T, qt * T + T)
                        v.tensor_scalar(Pr[:, h % 2, s], Pr[:, h % 2, s], ainv[:, h % 2, qt:qt + 1], None, ALU.mult).then_inc(*c.inc("at_p" if qt else "dve_step"))
                        dve.wait_ge(*c.last())

            def mla(l):
                dve.wait_ge(S["proj_evac"], c.need("proj_evac", 6))
                v.tensor_tensor(mt[:, 0:4, :], cqk, cqk, ALU.mult).then_inc(*c.inc("ml_sq"))
                dve.wait_ge(*c.last())
                dve.wait_ge(S["kI_m"], c.need("kI_m"))
                v.scalar_tensor_tensor(kI, bk(3, 0, T), -1.0 / 64, kI, ALU.mult, ALU.add).then_inc(*c.inc("dve_step"))
                dve.wait_ge(*c.last())
                v.tensor_tensor(mt[:, 4, :], kI, kI, ALU.mult).then_inc(*c.inc("kI_v"))
                dve.wait_ge(*c.last())
                dve.wait_ge(S["kI_var"], c.need("kI_var"))
                v.tensor_scalar(mt[:, 4, :], bk(3, T, T), 1.0 / 64, EPS, ALU.mult, ALU.add).then_inc(*c.inc("kI_ms"))
                dve.wait_ge(*c.last())
                v.tensor_scalar(mt[:, 0:2, :], bk(2).rearrange("p (a b) -> p a b", a=2), 1.0 / 256, EPS,
                                  ALU.mult, ALU.add).then_inc(*c.inc("ml_ms"))
                dve.wait_ge(*c.last())
                dve.wait_ge(S["kI_sd"], c.need("kI_sd"))
                v.reciprocal(mt[:, 4, :], mt[:, 5, :]).then_inc(*c.inc("dve_step"))
                dve.wait_ge(*c.last())
                v.scalar_tensor_tensor(kI, kI, pc(l, "kI_g"), mt[:, 4, :], ALU.mult, ALU.mult).then_inc(*c.inc("dve_step"))
                dve.wait_ge(*c.last())
                v.tensor_scalar(kI, kI, pc(l, "kI_b"), None, ALU.add).then_inc(*c.inc("kI_n"))
                dve.wait_ge(*c.last())
                dve.wait_ge(S["ml_ss"], c.need("ml_ss"))
                dve.wait_ge(S["ml_sd"], c.need("ml_sd"))
                v.reciprocal(mt[:, 0:2, :], mt[:, 2:4, :]).then_inc(*c.inc("dve_step"))
                dve.wait_ge(*c.last())
                for i in range(4):
                    gain = pc(l, "q_norm", i) if i < 2 else pc(l, "kv_norm", i - 2)
                    v.scalar_tensor_tensor(cqk[:, i, :], cqk[:, i, :], gain, mt[:, i // 2, :], ALU.mult, ALU.mult).then_inc(*c.inc("ml_n" if i == 3 else "dve_step"))
                    dve.wait_ge(*c.last())
                c.skip("proj_evac", 28)
                for n in range(16):
                    qt, h = n // 8, n % 8
                    dve.wait_ge(S["ix_rl"], c.need("ix_rl"))
                    w_ = wI[:, qt, h:h + 1]
                    if h == 0:
                        v.tensor_scalar(score[:, qt, :], rl[:, n % 4, :], w_, None, ALU.mult).then_inc(*c.inc("ix_free"))
                        dve.wait_ge(*c.last())
                    else:
                        v.scalar_tensor_tensor(score[:, qt, :], rl[:, n % 4, :], w_, score[:, qt, :], ALU.mult, ALU.add).then_inc(*c.inc("ix_free"))
                        dve.wait_ge(*c.last())
                v.tensor_tensor(score, score, C("fill").rearrange("p (a b) -> p a b", a=2), ALU.add).then_inc(*c.inc("dve_step"))
                dve.wait_ge(*c.last())
                for qt in range(TT):
                    for _ in range(TOPK // 8):
                        v.max(m8, score[:, qt, :]).then_inc(*c.inc("dve_step"))
                        dve.wait_ge(*c.last())
                        v.match_replace(score[:, qt, :], m8, score[:, qt, :], TAKEN).then_inc(*c.inc("dve_step"))
                        dve.wait_ge(*c.last())
                v.tensor_scalar(negm, score, (FILL + TAKEN) / 2, -1.0, ALU.is_le, ALU.add).then_inc(*c.inc("dve_step"))
                dve.wait_ge(*c.last())
                v.scalar_tensor_tensor(negm, negm, 1e30, C("fill").rearrange("p (a b) -> p a b", a=2), ALU.mult, ALU.add).then_inc(*c.inc("dve_step"))
                dve.wait_ge(*c.last())
                attention(8, True)
                dve.wait_ge(S["at_Of"], c.need("at_Of", 8))
                gated(False, True)

            def residual():
                for h in range(2):
                    for t in range(TT):
                        dve.wait_ge(S["mix_full"], c.need("mix_full"))
                        o = xt[:, t, h * 512:(h + 1) * 512]
                        v.tensor_tensor(o, bk(4 + 2 * h + t), o, ALU.add).then_inc(*c.inc("x_new"))
                        dve.wait_ge(*c.last())

            nf = [0]

            nff = [0]

            def low_part():
                b = nff[0] % FFN_BUFS
                nff[0] += 1
                dve.wait_ge(S["w_hi"], c.need("w_hi"))
                v.tensor_tensor(w_parts[b][1], ring[:, b * FFN_SLOT:(b + 1) * FFN_SLOT], w_parts[b][0], ALU.subtract
                                ).then_inc(*c.inc("w_lo"))

            def ffn(steps, e=None, more=False):
                for f in range(steps):
                    for j in range(2):
                        n = nf[0] % 4
                        nf[0] += 1
                        dve.wait_ge(S["silu"], c.need("silu"))
                        v.tensor_tensor(silu_t[:, n, :], bk(n, T, T), silu_t[:, n, :], ALU.mult).then_inc(*c.inc("act_f"))
                        dve.wait_ge(*c.last())
                        v.tensor_copy(act_parts[0][:, n, :], silu_t[:, n, :]).then_inc(*c.inc("act_f"))
                        dve.wait_ge(*c.last())
                        v.tensor_tensor(act_parts[1][:, n, :], silu_t[:, n, :], act_parts[0][:, n, :], ALU.subtract
                                        ).then_inc(*c.inc("act_t"))
                        if f < steps - 1 or more:
                            low_part()
                    if f < steps - 1 or more:
                        low_part()
                dve.wait_ge(S["down_full"], c.need("down_full"))
                for t in range(TT):
                    for h in range(2):
                        o = xt[:, t, h * 512:(h + 1) * 512]
                        if e is None:
                            v.tensor_tensor(o, bk(4 + 2 * t + h), o, ALU.add).then_inc(*c.inc("x_new"))
                        else:
                            v.scalar_tensor_tensor(o, bk(4 + 2 * t + h), gates[:, t, bass.ds(e, 1)], o, ALU.mult, ALU.add
                                                   ).then_inc(*c.inc("x_new"))
                dve.wait_ge(*c.last())

            def route():
                lg = small[:, 48:64].rearrange("p (a b) -> p a b", a=2)
                s1, s2, cum, l2 = (view(rtmp, 16 * i, 2, 8) for i in range(4))
                dve.wait_ge(S["rt_full"], c.need("rt_full"))
                v.tensor_copy(lg, bk(3, 0, 16).rearrange("p (a b) -> p a b", a=2)).then_inc(*c.inc("rt_l"))
                dve.wait_ge(*c.last())

                def first_max(src, m, s):
                    v.tensor_reduce(m, src, AX.X, ALU.max).then_inc(*c.inc("dve_step"))
                    dve.wait_ge(*c.last())
                    v.tensor_tensor(s, src, m.unsqueeze(2).to_broadcast([P, TT, NE]), ALU.is_equal).then_inc(*c.inc("dve_step"))
                    dve.wait_ge(*c.last())
                    for t in range(TT):
                        v.tensor_tensor_scan(cum[:, t, :], C("ones")[:, 0:NE], s[:, t, :], 0.0, ALU.mult, ALU.add).then_inc(*c.inc("dve_step"))
                        dve.wait_ge(*c.last())
                    v.scalar_tensor_tensor(s, cum, 1.0, s, ALU.is_equal, ALU.mult).then_inc(*c.inc("dve_step"))
                    dve.wait_ge(*c.last())

                m1, m2 = small[:, 38:40], small[:, 40:42]
                first_max(lg, m1, s1)
                v.scalar_tensor_tensor(l2, s1, -1e30, lg, ALU.mult, ALU.add).then_inc(*c.inc("dve_step"))
                dve.wait_ge(*c.last())
                first_max(l2, m2, s2)
                v.tensor_tensor(small[:, 42:44], m2, m1, ALU.subtract).then_inc(*c.inc("rt_d"))
                dve.wait_ge(*c.last())
                dve.wait_ge(S["rt_e"], c.need("rt_e"))
                e2, p1, p2 = small[:, 44:46], small[:, 46:48], small[:, 64:66]
                v.tensor_scalar(p2, e2, 1.0, None, ALU.add).then_inc(*c.inc("dve_step"))
                dve.wait_ge(*c.last())
                v.reciprocal(p1, p2).then_inc(*c.inc("dve_step"))
                dve.wait_ge(*c.last())
                v.tensor_tensor(p2, e2, p1, ALU.mult).then_inc(*c.inc("dve_step"))
                dve.wait_ge(*c.last())
                v.tensor_tensor(s1, s1, p1.unsqueeze(2).to_broadcast([P, TT, NE]), ALU.mult).then_inc(*c.inc("dve_step"))
                dve.wait_ge(*c.last())
                v.tensor_tensor(s2, s2, p2.unsqueeze(2).to_broadcast([P, TT, NE]), ALU.mult).then_inc(*c.inc("dve_step"))
                dve.wait_ge(*c.last())
                v.tensor_tensor(gates[:, :, :], s1, s2, ALU.add).then_inc(*c.inc("dve_step"))
                dve.wait_ge(*c.last())

            dve.wait_ge(S["par_dma"], 48)
            dve.wait_ge(S["mem_dma"], 16)
            norm(yflat.rearrange("p (a b) -> p a b", a=TT))
            dve.wait_ge(S["in_dma"], 16)
            for l in range(LAYERS):
                norm(xt)
                rwkv(l)
                gdn(l)
                mla(l)
                residual()
                norm(xt)
                c.skip("proj_evac", 24)
                attention(4, False)
                residual()
                v.memset(small[:, 70:71], 0.0).then_inc(*c.inc("mixers_done"))
                dve.wait_ge(*c.last())
                norm(xt)
                dve.wait_ge(S["f_hi"], c.need("f_hi"))
                v.tensor_tensor(feat_parts[1], feat[:, :, :], feat_parts[0], ALU.subtract).then_inc(*c.inc("dve_step"))
                for _ in range(3):
                    low_part()
                if l == 0:
                    ffn(FF // 256)
                else:
                    route()
                    ffn(FE // 256, 0, True)
                    with dve.Fori(1, NE - 1) as e:
                        c.begin_loop(e - 1, dict(silu=FE // P, act_t=FE // P, act_f=2 * FE // P, down_full=1, x_new=4,
                                                 w_hi=FE_CHUNKS, w_lo=FE_CHUNKS))
                        ffn(FE // 256, e, True)
                    c.end_loop(NE - 2)
                    ffn(FE // 256, NE - 1)
            norm(xt, final=True)
    return nc


_WEIGHTS = ["w_in", "rw_w2", "rw_a2", "rw_v1", "rw_v2", "mla_w_uq", "mla_w_uk", "mla_w_uv", "idx_w_q", "w_mix_out",
            "xa_w_q", "xa_w_kv", "xa_w_o", "ffn_w_gate", "ffn_w_up", "ffn_w_down", "moe_router", "moe_w_gate",
            "moe_w_up", "moe_w_down", "final_norm"]


def pack_params(i):
    out = np.zeros((LAYERS, P, NPAR), np.float32)
    for l in range(LAYERS):
        vec = {"norm_mix": i["norm_mix"][l], "mu": i["rw_mu"][l], "w0": i["rw_w0"][l], "a0": i["rw_a0"][l],
               "k_k": i["rw_k_k"][l], "k_a": i["rw_k_a"][l], "r_k": i["rw_r_k"][l].reshape(-1),
               "gn_g": i["rw_gn_g"][l], "gn_b": i["rw_gn_b"][l], "norm_xattn": i["norm_xattn"][l],
               "norm_ffn": i["norm_ffn"][l], "q_norm": i["mla_q_norm"][l], "kv_norm": i["mla_kv_norm"][l],
               "gdn_norm": i["gdn_norm_g"][l], "mem_norm": i["mem_norm"], "conv": i["gdn_conv"][l].reshape(-1)}
        if l:
            vec["v0"] = i["rw_v0"][l - 1]
        for name, a in vec.items():
            a = np.asarray(a).reshape(-1, P)
            out[l, :, PCOL[name]:PCOL[name] + a.shape[0]] = a.T
        for h in range(2):
            out[l, 64 * h:64 * h + 64, PCOL["kI_g"]] = i["idx_k_g"][l]
            out[l, 64 * h:64 * h + 64, PCOL["kI_b"]] = i["idx_k_b"][l]
        out[l, 0:GH, PCOL["A_log"]] = i["gdn_A_log"][l]
        out[l, 0:GH, PCOL["dt_bias"]] = i["gdn_dt_bias"][l]
    return out


def kernel(**inputs):
    import concourse.bacc as bacc
    from concourse.bass_utils import run_bass_kernel_spmd

    inp = {k: np.asarray(v) for k, v in inputs.items()}
    arrays = {"x": inp["x"].reshape(T, D), "mem": inp["mem"].reshape(T, D), "consts": make_consts(),
              "params": pack_params(inp)}
    for n in _WEIGHTS:
        a = inp[n]
        if n in ("mla_w_uk", "mla_w_uv"):
            a = a.reshape(LAYERS, 256, D)
        if n == "moe_router":
            a = a.reshape(D, NE)
        arrays[n] = a
    arrays = {f"in_{n}": np.ascontiguousarray(a) for n, a in arrays.items()}
    nc = bacc.Bacc("TRN2", target_bir_lowering=False, num_devices=1)
    args = [nc.dram_tensor(n, a.shape, F32, kind="ExternalInput").ap() for n, a in arrays.items()]
    out = nc.dram_tensor("out", (T, D), F32, kind="ExternalOutput").ap()
    build(nc, *args, out)
    r = run_bass_kernel_spmd(nc, [arrays], core_ids=[0])
    return r.results[0]["out"].reshape(1, T, D)
```

```python
import math
from contextlib import ExitStack

import numpy as np

import concourse.bass as bass
from concourse import mybir

F32 = mybir.dt.float32
ALU = mybir.AluOpType
ACT = mybir.ActivationFunctionType
AX = mybir.AxisListType

P = 128
D = 1024
T = 256
LAYERS = 2
KT = D // P
TT = T // P
EPS = 1e-6
RW_N = 64
RW_CHUNKS = T // RW_N
RW_PAIRS = D // P
GN_EPS = 64e-5
GH = D // P
TOPK = 64
FF = 2816
FE = 3584
NE = 8
A_IN, B_IN = 3 * D + 128, 3 * D + 16
C0 = A_IN + B_IN
G0 = C0 + 256 + 256 + 64 + 8
DECAY = math.exp(-0.5)
SLOT = 4096
MIX_SLOTS = 3
FFN_SLOT, FFN_BUFS = 2048, 6
FE_CHUNKS = 3 * FE // 256
PASSES = ((0, 0), (0, 1), (1, 0))
FILL, TAKEN = -3.0e38, -3.39e38

PARAMS = [("norm_mix", 8), ("mu", 25), ("w0", 8), ("a0", 8), ("k_k", 8), ("k_a", 8), ("r_k", 8),
          ("gn_g", 8), ("gn_b", 8), ("v0", 8), ("norm_xattn", 8), ("norm_ffn", 8), ("q_norm", 2),
          ("kv_norm", 2), ("gdn_norm", 1), ("kI_g", 1), ("kI_b", 1), ("mem_norm", 8), ("conv", 96),
          ("A_log", 1), ("dt_bias", 1)]
PCOL, NPAR = {}, 0
for _n, _k in PARAMS:
    PCOL[_n] = NPAR
    NPAR += _k

LEVELS = 7
CONSTS = [("ident", 128), ("ones", 128), ("blk", 128), ("maskbd", 128), ("antibd", 128),
          ("maskGA", 128), ("maskGB", 128), ("gdnmask", 256), ("level", 128 * LEVELS),
          ("sel", 1024), ("fill", 512), ("cumask", 512)]
CCOL, NCONST = {}, 0
for _n, _k in CONSTS:
    CCOL[_n] = (NCONST, _k)
    NCONST += _k


def make_consts():
    i = np.arange(P)
    s, t = i[:, None], i[None, :]
    sm, tm = s % 64, t % 64
    same = (s // 64 == t // 64)
    strict, incl = sm < tm, sm <= tm
    c = {
        "ident": s == t, "ones": np.ones((P, P)), "blk": same, "maskbd": same, "antibd": ~same,
        "maskGA": np.where(t < 64, strict, incl), "maskGB": np.where(t < 64, incl, strict),
        "gdnmask": np.concatenate([np.where(s < t, -1.0, 0.0), np.where(s <= t, 1.0, 0.0)], 1),
        "level": np.concatenate([(s // (2 * b) == t // (2 * b)) & ((s // b) % 2 == 1) & ((t // b) % 2 == 0)
                                 for b in (2 ** k for k in range(LEVELS))], 1),
        "sel": np.concatenate([(s == h) & (t >= 0) for h in range(8)], 1),
    }
    c["cumask"] = (np.arange(2 * T)[None, :] % RW_N != 0) & (i[:, None] >= 0)
    q = i[:, None]
    k = np.arange(T)[None, :]
    c["fill"] = np.concatenate([np.where(k <= q + P * a, 0.0, FILL) for a in range(TT)], 1)
    return np.concatenate([np.asarray(c[n], np.float32).reshape(P, w) for n, w in CONSTS], 1)


SEMS = ("in_dma par_dma mem_dma out_dma slot0 slot1 slot2 weights_used mixers_done "
        "dve_step act_step norm_ss norm_ms norm_sd norm_xn norm_T feat_ready feat_half x_new "
        "proj_full proj_evac raw_free gate_sig rkv_ready vlow_full vlow vres_full vres_sig vres_done "
        "rw_lora rw_sig rw_cum rw_exp rw_kksq rw_bon rw_sums rw_nrm rw_sqrt rw_vv rw_fm rw_tr rw_G rw_tm rw_N "
        "rw_NT inv_Y inv_Ym inv_D inv_X inv_T inv_XT rc_P1 rc_R rc_U rc_UV rc_P2 rc_S rc_O rc_Sn rc_OT rc_Of "
        "gn_m gn_sq gn_v gn_var gn_sd gn_y merged "
        "gd_ab gd_abs gd_g gd_gT gd_sq gd_ss gd_nrm gd_sqrt gd_bc gd_eg gd_fm gd_kk gd_dif gd_dec gd_N gd_tr gd_tm "
        "gr_in gr_R gr_V gr_Vs gr_S gr_Ss gr_O gr_Of gt_sq gt_ss gt_ms gt_sd "
        "ml_sq ml_ss ml_ms ml_sd ml_n kI_m kI_v kI_var kI_ms kI_sd kI_n ix_full ix_rl ix_free "
        "at_L at_max at_exp at_p at_T at_PT at_O at_Of mix_full "
        "fslot0 fslot1 fslot2 fslot3 fslot4 fslot5 w_hi w_lo wb_used f_hi act_f gu_full silu act_t down_full rt_full rt_l rt_d rt_e").split()


class Counter:

    def __init__(self, sems):
        self.sems, self.sent, self.seen, self.loop, self.latest = sems, {}, {}, None, None

    def _at(self, name, n):
        return n if self.loop is None else n + self.loop[0] * self.loop[1][name]

    def inc(self, name):
        self.sent[name] = self.sent.get(name, 0) + 1
        self.latest = name
        return self.sems[name], 1

    def last(self):
        return self.sems[self.latest], self._at(self.latest, self.sent[self.latest])

    def need(self, name, k=1, spare=0, view=None):
        n = self.seen[name, view] = self.seen.get((name, view), 0) + k
        return self._at(name, n - spare) if n > spare else None

    def skip(self, name, k, view=None):
        self.seen[name, view] = self.seen.get((name, view), 0) + k

    def begin_loop(self, done, per):
        self.loop = (done, per)

    def end_loop(self, rounds):
        per = self.loop[1]
        self.loop = None
        for n in self.sent:
            self.sent[n] += (rounds - 1) * per.get(n, 0)
        for n, v in self.seen:
            self.seen[n, v] += (rounds - 1) * per.get(n, 0)


def build(nc, x, mem, consts, params, w_in, w2, a2, v1, v2, w_uq, w_uk, w_uv, w_qI, w_mix, xa_q, xa_kv, xa_o,
          ff_g, ff_u, ff_d, router, me_g, me_u, me_d, final_norm, out):
    ctx = ExitStack()
    with ctx:
        def sb(name, shape):
            return ctx.enter_context(nc.sbuf_tensor(name, shape, F32))

        S = {n: ctx.enter_context(nc.semaphore(n)) for n in SEMS}
        bank = [ctx.enter_context(nc.psum_tensor(f"bank{i}", [P, 512], F32)) for i in range(8)]

        xt = sb("xt", [P, TT, D])
        feat = sb("feat", [P, KT, T])
        memf = sb("memf", [P, KT, T])
        vfirst = sb("vfirst", [P, KT, T])
        cs = sb("cs", [P, NCONST])
        par = sb("par", [P, LAYERS, NPAR])
        ring = sb("ring", [P, MIX_SLOTS * SLOT])
        gates = sb("gates", [P, TT, NE])
        rout = sb("rout", [P, KT, NE])
        rtmp = sb("rtmp", [P, 64])
        small = sb("small", [P, 80])
        yacc = sb("yacc", [P, KT, T])
        MIXF = 28688
        NORM_AT = 16384
        arena = sb("arena", [P, MIXF])
        at = 0

        def view(buf, start, *shape):
            v = buf[:, start:start + math.prod(shape)]
            names = "abcd"[:len(shape)]
            if len(shape) > 1:
                v = v.rearrange(f"p ({' '.join(names)}) -> p {' '.join(names)}", **dict(zip(names, shape)))
            return v

        def area(*shape):
            nonlocal at
            v = view(arena, at, *shape)
            at += math.prod(shape)
            assert at <= MIXF
            return v

        yflat = yacc[:, :, :].rearrange("p a b -> p (a b)")
        xn = view(arena, NORM_AT, TT, D)
        sqj = view(arena, NORM_AT + TT * D, D)
        rkv = area(24, T)
        branch = rkv[:, 0:KT, :]
        BASE = at
        raw = area(4, 260)
        at = BASE
        tmp = area(16, T)
        gate_rw = tmp[:, 8:16, :]
        lora, vlo = area(T), area(T)
        ZR, BKt, Vad, GA, GB, XT = (area(4, 4, P) for _ in range(6))
        Ym1 = area(4, P)

        def tw(i):
            return tmp[:, 2 * i:2 * i + 2, :]

        NT12 = area(8, P)
        NT = [NT12[:, 0:4], NT12[:, 4:8]]
        Rbd, UV, Oad, Stmp, Wst = (area(4, P) for _ in range(5))
        Sst = [area(4, P), area(4, P)]
        wc = area(4, 4)
        X1, BK, VV = view(yflat, 0, 4, P), view(yflat, 512, 8, P), view(yflat, 1536, 4, P)
        X, Ym = [X1, Rbd], [Ym1, UV]
        at = BASE
        gt = area(10, T)
        g8, b8 = area(T), area(T)
        ab_at = at
        ab = area(4, T)
        gbt = area(TT, 16)
        ke, qe = area(8, T), area(8, T)
        kq = area(TT, 2, P)
        dec = area(TT, P)
        gNT, gXT, gAT = area(8, TT, P), area(8, TT, P), area(8, TT, P)
        gate_gd = gNT.rearrange("p a b c -> p (a b c)").rearrange("p (a b) -> p a b", a=KT)
        ktm, vtm = area(8, P), area(8, TT, P)
        inv_at = at
        gX1, gYm1 = area(4, P), area(4, P)
        gR, gV, gS = area(4, P), area(4, P), area(4, P)
        gX, gYm = [gX1, view(arena, ab_at, 4, P)], [gYm1, view(arena, ab_at + 512, 4, P)]

        gt_b = view(arena, inv_at, 10, T)
        kq_b, dec_b = view(arena, ab_at, TT, 2, P), view(arena, ab_at + 512, TT, P)
        GD_BUFS = [(gt, kq, dec, (0, 1, 7, 6)), (gt_b, kq_b, dec_b, (2, 3, 4, 5))]

        def heads2(a, i):
            return a[:, 2 * i:2 * i + 2].rearrange("p a b c -> p (a b) c")

        qf = branch
        at = KT * T
        kf = area(KT, T)
        qI = area(4, T)
        rl = area(4, T)
        at = BASE + 1040 + 1024
        cqk = area(4, T)
        kI = area(T)
        wI = area(TT, 8)
        mt = area(6, T)
        vt = area(TT, D)
        score, negm = area(TT, T), area(TT, T)
        m8 = area(8)
        Lm, Pr, PT = area(2, 2 * T), area(2, 2 * T), area(2, 2 * T)
        amax, asum, ainv = area(2, 2), area(2, 2), area(2, 2)
        gate_ml = area(KT, T)
        at = NORM_AT + TT * D + D
        kf_x, vt_x = area(KT, T), area(TT, D)
        at = 0

        def parts(*shape):
            a = area(math.prod(shape)).bitcast(mybir.dt.bfloat16)
            return [view(a, i * math.prod(shape), *shape) for i in range(2)]

        w_parts = [parts(FFN_SLOT) for _ in range(FFN_BUFS)]
        feat_parts = parts(KT, T)
        act_parts = parts(4, T)
        assert at <= NORM_AT
        silu_t = yacc[:, 0:4, :]

        def C(name, a=0, b=None):
            lo, w = CCOL[name]
            return cs[:, lo + a:lo + (w if b is None else b)]

        def pc(l, name, j=0):
            return par[:, l, PCOL[name] + j:PCOL[name] + j + 1]

        def b4(ap, n=4):
            return ap.unsqueeze(1).to_broadcast([ap.shape[0], n, ap.shape[1]])

        def bk(i, lo=0, w=512):
            return bank[i][:, lo:lo + w]

        def bk4(i):
            return bank[i][:, :].rearrange("p (a b) -> p a b", a=4)

        def slot_ap(s):
            return ring[:, s * SLOT:(s + 1) * SLOT]

        def beside(main, side, per=1, turns=None):
            n = 0
            for _ in main or ():
                for _ in range(per):
                    if side is not None and (turns is None or n < turns):
                        next(side, None)
                        n += 1
            if side is not None and turns is None:
                for _ in side:
                    pass

        def rows(w):
            return w.rearrange("(k p) n -> p k n", p=P)

        def col_chunk(w, c0, n=512):
            k = w.shape[0] // P
            return [(0, (k, n), rows(w)[:, :, c0:c0 + n], 0, P)]

        def mix_chunks(l):
            w = w_in[l]
            for i in range(6):
                yield col_chunk(w, 512 * i)
            lo = [(0, (8, 128), rows(w)[:, :, 3 * D:3 * D + 128], 0, P),
                  (1024, (1, D), w2[l].unsqueeze(1), 0, 64), (1024, (1, D), a2[l].unsqueeze(1), 64, 64)]
            if l:
                lo += [(2048, (8, 32), rows(v1[l - 1]), 0, P), (2304, (1, D), v2[l - 1].unsqueeze(1), 0, 32)]
            yield lo
            for i in range(2):
                yield col_chunk(w, G0 + 512 * i)
            for i in range(6):
                yield col_chunk(w, A_IN + 512 * i)
            yield [(0, (8, 16), rows(w)[:, :, A_IN + 3 * D:A_IN + 3 * D + 16], 0, P)]
            for i in range(2):
                yield col_chunk(w, G0 + D + 512 * i)
            yield col_chunk(w, C0)
            kc = rows(w)[:, :, C0 + 512:C0 + 576]
            yield [(0, (8, 128), kc, 0, P), (1024, (8, 8), rows(w)[:, :, C0 + 576:C0 + 584], 0, P)]
            for i in range(2):
                yield col_chunk(xa_kv[l], 512 * i)
            yield [(0, (2, D), rows(w_uq[l]), 0, P), (2048, (2, D), rows(w_uk[l]), 0, P)]
            yield [(0, (2, D), rows(w_uv[l]), 0, P), (2048, (2, 512), rows(w_qI[l]), 0, P)]
            for i in range(2):
                yield col_chunk(xa_kv[l], D + 512 * i)
            for i in range(2):
                yield col_chunk(w, G0 + 2 * D + 512 * i)
            for w_, n in ((w_mix[l], 2), (xa_q[l], 2), (xa_o[l], 2)):
                for i in range(n):
                    yield col_chunk(w_, 512 * i)

        def ffn_chunks(g, u, d, n):
            for f in range(0, n, 256):
                w = 256
                yield col_chunk(g, f, w)
                yield col_chunk(u, f, w)
                yield [(0, (w // P, D), rows(d[f:f + w]), 0, P)]

        class Stream:
            def __init__(self):
                self.n, self.last, self.count = 0, {}, [0] * MIX_SLOTS

            def next(self, slots):
                s = self.pos % slots
                self.pos += 1
                need = self.last.get(s, -1) + 1
                self.last[s] = self.n
                self.n += 1
                return s, need

            def phase(self):
                self.pos = 0

        sp_s, pe_s = Stream(), Stream()

        block = ctx.enter_context(nc.Block())

        @block.sync
        def _(sp):
            sp.dma_start(par[:, :, :], params.rearrange("l p n -> p l n")).then_inc(S["par_dma"], 16)
            sp.dma_start(yacc[:, :, :].rearrange("p a b -> p (a b)").rearrange("p (a d) -> p a d", a=TT),
                         mem.rearrange("(a p) d -> p a d", p=P)).then_inc(S["mem_dma"], 16)
            sp.dma_start(xt[:, :, :], x.rearrange("(a p) d -> p a d", p=P)).then_inc(S["in_dma"], 16)
            sp.dma_start(cs[:, :], consts).then_inc(S["par_dma"], 16)
            sp.dma_start(rout[:, :, :], rows(router)).then_inc(S["par_dma"], 16)

            def load(chunk, slots, rounds=0):
                s, need = sp_s.next(slots)
                if need:
                    sp.wait_ge(S["weights_used"], rounds + need)
                for col, shape, src, p0, np_ in chunk:
                    dst = slot_ap(s)[p0:p0 + np_, col:col + math.prod(shape)].rearrange("p (k n) -> p k n", k=shape[0])
                    sp.dma_start(dst[:, :, 0:src.shape[-1]], src).then_inc(S[f"slot{s}"], 16)
                    if src.shape[-1] < shape[1]:
                        sp.dma_start(dst[:, :, src.shape[-1]:], src).then_inc(S[f"slot{s}"], 16)

            nff = [0]

            def load_ffn(chunks, done=0):
                for ch in chunks:
                    n = nff[0]
                    nff[0] += 1
                    if n in first_round:
                        sp.wait_ge(S["weights_used"], first_round[n])
                    else:
                        sp.wait_ge(S["w_lo"], done + n - FFN_BUFS + 1)
                    for _, shape, src, _, _ in ch:
                        sp.dma_start(view(ring, (n % FFN_BUFS) * FFN_SLOT, *shape), src
                                     ).then_inc(S[f"fslot{n % FFN_BUFS}"], 16)

            for l in range(LAYERS):
                sp_s.phase()
                if l:
                    sp.wait_ge(S["w_lo"], nff[0])
                for ch in mix_chunks(l):
                    load(ch, MIX_SLOTS)
                first_round = {nff[0] + i: sp_s.last[(nff[0] + i) % FFN_BUFS * FFN_SLOT // SLOT] + 1 for i in range(FFN_BUFS)}
                if l == 0:
                    load_ffn(ffn_chunks(ff_g[0], ff_u[0], ff_d[0], FF))
            load_ffn(ffn_chunks(me_g[0, 0], me_u[0, 0], me_d[0, 0], FE))
            sp.wait_ge(S["mixers_done"], LAYERS)
            sp.dma_start(memf[:, 0:4, :].rearrange("p a b -> p (a b)"),
                         final_norm.partition_broadcast(P)).then_inc(S["par_dma"], 16)
            with sp.Fori(1, NE - 1) as e:
                load_ffn(ffn_chunks(me_g[0, e], me_u[0, e], me_d[0, e], FE), (e - 1) * FE_CHUNKS)
            nff[0] += (NE - 3) * FE_CHUNKS
            load_ffn(ffn_chunks(me_g[0, NE - 1], me_u[0, NE - 1], me_d[0, NE - 1], FE))
            sp.wait_ge(S["norm_xn"], 2 * (2 + 3 * LAYERS))
            sp.dma_start(out.rearrange("(a p) d -> p a d", p=P),
                         yacc[:, :, :].rearrange("p a b -> p (a b)").rearrange("p (a d) -> p a d", a=TT)
                         ).then_inc(S["out_dma"], 16)
            sp.wait_ge(S["out_dma"], 16)

        @block.tensor
        def _(pe):
            c = Counter(S)
            owed = [0]
            slot_seen = [0] * MIX_SLOTS

            mm, tr_ = nc.tensor.matmul, nc.tensor.transpose

            def tr(o, i_):
                return tr_(o, i_, C("ident")[0:i_.shape[0], 0:i_.shape[0]])

            def release(i):
                if owed[0]:
                    i.then_inc(S["weights_used"], owed[0])
                    owed[0] = 0

            def chunk(slots, ndma=1):
                s, _ = pe_s.next(slots)
                slot_seen[s] += 16 * ndma
                pe.wait_ge(S[f"slot{s}"], slot_seen[s])
                return slot_ap(s)

            nproj = [0]

            def proj_slot():
                n = nproj[0] % 2
                nproj[0] += 1
                due = c.need("proj_evac", 1, spare=2)
                if due is not None:
                    pe.wait_ge(S["proj_evac"], due)
                return bk(n, 0, 256)

            def proj(w, ntiles, src, kt=KT):
                for j in range(ntiles):
                    o = proj_slot()
                    for k in range(kt):
                        m = mm(o, w[:, k, j * P:(j + 1) * P], src[:, k, :], start=k == 0, stop=k == kt - 1)
                        if k == 0:
                            release(m)
                        if k == kt - 1:
                            m.then_inc(S["proj_full"], 1)

            def proj_chunks(n, src):
                for _ in range(n):
                    w = chunk(MIX_SLOTS).rearrange("p (k n) -> p k n", k=KT)
                    proj(w, 4, src)
                    owed[0] += 1

            def proj_tok(w, src, kt, quarters):
                for t in range(TT):
                    for q in range(quarters):
                        o = proj_slot()
                        for k in range(kt):
                            m = mm(o, src[:, k, t * P:(t + 1) * P], w[:, k, q * 256:(q + 1) * 256], start=k == 0, stop=k == kt - 1)
                            if k == 0:
                                release(m)
                            if k == kt - 1:
                                m.then_inc(S["proj_full"], 1)

            def norm():
                pe.wait_ge(S["norm_xn"], c.need("norm_xn", 2))
                for b in range(4):
                    for k in (2 * b, 2 * b + 1):
                        for t in range(TT):
                            m = tr(bk(4 + b, (k % 2) * 256 + t * P, P), xn[:, t, k * P:(k + 1) * P])
                            if not k and not t:
                                release(m)
                            if k % 2 and t == 1:
                                m.then_inc(S["norm_T"], 1)
                pe.wait_ge(S["feat_ready"], c.need("feat_ready", 4))
                pe.wait_ge(S["feat_half"], c.need("feat_half", 4))

            def invert(levels, sets):
                for b in range(levels):
                    for i, (nt, xtv, xv, yv) in enumerate(sets):
                        if b:
                            pe.wait_ge(S["inv_X"], c.need("inv_X"))
                        for k in range(4):
                            m = mm(bk(2 + i, k * P, P), nt[:, k, :], xv[:, k, :], start=True, stop=True) if b else tr(bk(2 + i, k * P, P), nt[:, k, :])
                            if k == 3:
                                m.then_inc(S["inv_Y"], 1)
                        if b:
                            for k in range(4):
                                m = tr(bk(4 + i, k * P, P), xv[:, k, :])
                                if k == 3:
                                    m.then_inc(S["inv_T"], 1)
                    if levels == LEVELS:
                        yield
                    if b:
                        for i, (nt, xtv, xv, yv) in enumerate(sets):
                            pe.wait_ge(S["inv_XT"], c.need("inv_XT"))
                            pe.wait_ge(S["inv_Ym"], c.need("inv_Ym"))
                            for k in range(4):
                                m = mm(bk(2 + i, k * P, P), xtv[:, k, :], yv[:, k, :], start=True, stop=True)
                                if k == 3:
                                    m.then_inc(S["inv_D"], 1)
                    yield
                for i, (nt, xtv, xv, yv) in enumerate(sets):
                    pe.wait_ge(S["inv_X"], c.need("inv_X"))
                    for k in range(4):
                        m = tr(bk(4 + i, k * P, P), xv[:, k, :])
                        if k == 3:
                            m.then_inc(S["inv_T"], 1)
                pe.wait_ge(S["inv_XT"], c.need("inv_XT", len(sets)))

            def gates_beside():
                for _ in range(2):
                    w = chunk(MIX_SLOTS).rearrange("p (k n) -> p k n", k=KT)
                    for j in range(4):
                        o = proj_slot()
                        for k in range(KT):
                            m = mm(o, w[:, k, j * P:(j + 1) * P], feat[:, k, :], start=k == 0, stop=k == KT - 1)
                            if k == 0:
                                release(m)
                            if k == KT // 2 - 1:
                                yield
                        m.then_inc(S["proj_full"], 1)
                        if j == 3:
                            owed[0] += 1
                        yield

            def front_rw(cp, wl):
                for p in range(2):
                    j = 2 * cp + p
                    mm(bk(0, p * T, T), wl[0:64, j * P:(j + 1) * P], lora[0:64, :], start=True, stop=True)
                    m = mm(bk(1, p * T, T), wl[64:128, j * P:(j + 1) * P], lora[64:128, :], start=True, stop=True)
                m.then_inc(S["rw_lora"], 1)
                yield
                pe.wait_ge(S["rw_kksq"], c.need("rw_kksq"))
                mm(bk(6), C("blk"), tw(4), start=True, stop=True)
                pe.wait_ge(S["rw_bon"], c.need("rw_bon"))
                mm(bk(7), C("blk"), tw(5), start=True, stop=True).then_inc(S["rw_sums"], 1)
                yield
                yield
                pe.wait_ge(S["rw_fm"], c.need("rw_fm"))
                for p in range(2):
                    s = (2 * cp + p) % 4
                    pe.wait_ge(S["rw_vv"], c.need("rw_vv"))
                    for q in range(4):
                        mm(bk(0, q * P, P), BK[0:64, 4 * p + q, :], ZR[0:64, s, q, :], start=True, stop=True)
                    for q in range(4):
                        m = mm(bk(1, q * P, P), BK[64:128, 4 * p + q, :], ZR[64:128, s, q, :], start=True, stop=True)
                        if q == 3:
                            m.then_inc(S["rw_G"], 1)
                    for q in range(4):
                        tr(bk(6, q * P, P), BK[:, 4 * p + q, :])
                    for q in range(4):
                        m = tr(bk(7, q * P, P), VV[:, q, :])
                        if q == 3:
                            m.then_inc(S["rw_tr"], 1)
                    yield
                    pe.wait_ge(S["rw_tm"], c.need("rw_tm"))
                    pe.wait_ge(S["rw_N"], c.need("rw_N"))

            def rwkv(l):
                proj_chunks(6, feat)
                w = chunk(MIX_SLOTS, 5 if l else 3)
                proj(w[:, 0:1024].rearrange("p (k n) -> p k n", k=KT), 1, feat)
                wl = w[:, 1024:2048]
                pe.wait_ge(S["rkv_ready"], c.need("rkv_ready"))
                if l:
                    for k in range(KT):
                        m = mm(bk(2, 0, T)[0:32], w[:, 2048 + 32 * k:2080 + 32 * k], rkv[:, 16 + k, :], start=k == 0, stop=k == KT - 1)
                        if k == KT - 1:
                            m.then_inc(S["vlow_full"], 1)
                    pe.wait_ge(S["vlow"], c.need("vlow"))
                    for j in range(KT):
                        due = c.need("vres_sig", 1, spare=2)
                        if due is not None:
                            pe.wait_ge(S["vres_sig"], due)
                        mm(bk(3 + j % 2, 0, T), w[0:32, 2304 + j * P:2304 + (j + 1) * P], vlo[0:32, :], start=True, stop=True).then_inc(S["vres_full"], 1)
                    pe.wait_ge(S["vres_sig"], c.need("vres_sig", 0))
                gate = gates_beside()
                for g in range(2):
                    a, b = front_rw(2 * g, wl), front_rw(2 * g + 1, wl)
                    beside(recur_rw(g - 1) if g else None, a, 1, 2)
                    beside(None, a)
                    pe.wait_ge(S["rw_NT"], c.need("rw_NT", 2))
                    beside(invert(6, [(NT[i], XT[:, i], X[i], Ym[i]) for i in range(2)]), b)
                    pe.wait_ge(S["rw_NT"], c.need("rw_NT", 2))
                    beside(invert(6, [(NT[i], XT[:, 2 + i], X[i], Ym[i]) for i in range(2)]), None)
                owed[0] += 1
                beside(recur_rw(1), gate, 1, 8)
                for i in range(4):
                    mm(bk(5), C("blk"), branch[:, 2 * i:2 * i + 2, :], start=True, stop=True).then_inc(S["gn_m"], 1)
                    next(gate)
                    pe.wait_ge(S["gn_sq"], c.need("gn_sq"))
                    mm(bk(6), C("blk"), tmp[:, 0:2, :], start=True, stop=True).then_inc(S["gn_v"], 1)
                    next(gate)
                    pe.wait_ge(S["gn_y"], c.need("gn_y"))

            def recur_rw(g):
                def own(b, rhs, q):
                    for i in range(4):
                        mm(bk(b, i * P, 64), GA[:, i, q, :], rhs[:, i, 0:64], start=not i, stop=False, skip_group_check=True)
                        m = mm(bk(b, i * P + 64, 64), GB[:, i, q, :], rhs[:, i, 64:128], start=False, stop=not q and i == 3, skip_group_check=True)
                    return m

                def past(b, q):
                    for i in range(4):
                        m = mm(bk(b, i * P, P), ZR[:, i, q, :], Sst[q % 2][:, i, :], start=False, stop=i == 3, skip_group_check=True)
                    return m

                def transposed():
                    pe.wait_ge(S["rc_O"], c.need("rc_O"))
                    for i in range(4):
                        m = tr(bk(4, i * P, P), Oad[:, i, :])
                        if i == 3:
                            m.then_inc(S["rc_OT"], 1)

                own(2, Vad[:, 0:4, 0, :], 0).then_inc(S["rc_P1"], 1)
                for q in range(RW_CHUNKS):
                    more = q < RW_CHUNKS - 1
                    pe.wait_ge(S["rc_R"], c.need("rc_R"))
                    for i in range(4):
                        m = mm(bk(3, i * P, P), XT[:, i, q, :], Rbd[:, i, :], start=True, stop=True)
                        if i == 3:
                            m.then_inc(S["rc_U"], 1)
                    if q:
                        transposed()
                    if more:
                        own(2, Vad[:, 0:4, q + 1, :], q + 1)
                    yield
                    pe.wait_ge(S["rc_UV"], c.need("rc_UV"))
                    if q:
                        pe.wait_ge(S["rc_Of"], c.need("rc_Of"))
                    if more:
                        for i in range(4):
                            m = mm(bk(4, i * P, P), BKt[:, i, q, :], UV[:, i, :], start=True, stop=True)
                            if i == 3:
                                m.then_inc(S["rc_S"], 1)
                    out_ = own(5, UV, q)
                    if q == 0:
                        out_.then_inc(S["rc_P2"], 1)
                    if more:
                        pe.wait_ge(S["rc_Sn"], c.need("rc_Sn"))
                        past(2, q + 1).then_inc(S["rc_P1"], 1)
                    if q:
                        past(5, q).then_inc(S["rc_P2"], 1)
                    yield
                transposed()
                pe.wait_ge(S["rc_Of"], c.need("rc_Of"))

            def front_gd(heads, bufs):
                gt, kq, dec, (b_bc, b_ss, b_kk, b_tr) = bufs
                for h in heads:
                    sel = C("sel", P * h, P * h + P)[0:8]
                    mm(bk(b_bc, 0, T), sel, g8[0:8, :], start=True, stop=True)
                    mm(bk(b_bc, T, T), sel, b8[0:8, :], start=True, stop=True).then_inc(S["gd_bc"], 1)
                    pe.wait_ge(S["gd_sq"], c.need("gd_sq"))
                    mm(bk(b_ss), C("ones"), gt[:, 0:2, :], start=True, stop=True).then_inc(S["gd_ss"], 1)
                    yield
                    yield
                    pe.wait_ge(S["gd_fm"], c.need("gd_fm"))
                    for t in range(TT):
                        m = mm(bk(b_kk, 256 * t, 256), gt[:, 3, t * P:(t + 1) * P], kq[:, t], start=True, stop=True)
                        if t:
                            m.then_inc(S["gd_kk"], 1)
                    tr(bk(b_tr, 0, P), gt[:, 3, 0:P])
                    for t in range(TT):
                        m = tr(bk(b_tr, (1 + t) * P, P), rkv[:, 16 + h, t * P:(t + 1) * P])
                        if t:
                            m.then_inc(S["gd_tr"], 1)
                    yield
                    pe.wait_ge(S["gd_N"], c.need("gd_N"))
                    pe.wait_ge(S["gd_tm"], c.need("gd_tm"))

            def gdn(l):
                proj_chunks(6, feat)
                w = chunk(MIX_SLOTS)[:, 0:128].rearrange("p (k n) -> p k n", k=KT)
                for h in range(2):
                    for k in range(KT):
                        m = mm(bk(2 + h, 0, T)[0:8], w[:, k, 8 * h:8 * h + 8], feat[:, k, :], start=k == 0, stop=k == KT - 1)
                        if k == KT - 1:
                            m.then_inc(S["gd_ab"], 1)
                owed[0] += 1
                pe.wait_ge(S["gd_g"], c.need("gd_g"))
                for t in range(TT):
                    release(tr(bk(4, 16 * t, 8), g8[0:8, t * P:(t + 1) * P]))
                    m = tr(bk(4, 16 * t + 8, 8), b8[0:8, t * P:(t + 1) * P])
                    if t:
                        m.then_inc(S["gd_gT"], 1)
                pe.wait_ge(S["rkv_ready"], c.need("rkv_ready"))
                second = front_gd(range(4, 8), GD_BUFS[0])
                beside(front_gd((0, 2), GD_BUFS[0]), front_gd((1, 3), GD_BUFS[1]))
                beside(invert(7, [(heads2(gNT, i), heads2(gXT, i), gX[i], gYm[i]) for i in range(2)]), second, 1)
                beside(invert(7, [(heads2(gNT, 2 + i), heads2(gXT, 2 + i), gX[i], gYm[i]) for i in range(2)]), recur_gd(0))
                beside(recur_gd(1), None)
                gate = gates_beside()
                for i in range(4):
                    pe.wait_ge(S["gt_sq"], c.need("gt_sq"))
                    mm(bk(2), C("ones"), gt[:, 0:2, :], start=True, stop=True).then_inc(S["gt_ss"], 1)
                    for _ in range(4):
                        next(gate)
                pe.wait_ge(S["gn_y"], c.need("gn_y"))

            def recur_gd(g):
                for t in range(TT):
                    if t:
                        pe.wait_ge(S["gr_Ss"], c.need("gr_Ss"))
                        for i in range(4):
                            m = mm(bk(0, i * P, P), ke[:, 4 * g + i, P:T], gS[:, i, :], start=True, stop=True)
                            if i == 3:
                                m.then_inc(S["gr_in"], 1)
                        yield
                    pe.wait_ge(S["gr_R"], c.need("gr_R"))
                    for i in range(4):
                        m = mm(bk(1, i * P, P), gXT[:, 4 * g + i, t, :], gR[:, i, :], start=True, stop=True)
                        if i == 3:
                            m.then_inc(S["gr_V"], 1)
                    yield
                    pe.wait_ge(S["gr_Vs"], c.need("gr_Vs"))
                    if t == 0:
                        for i in range(4):
                            m = mm(bk(6, i * P, P), ktm[:, 4 * g + i, :], gV[:, i, :], start=True, stop=True)
                            if i == 3:
                                m.then_inc(S["gr_S"], 1)
                    else:
                        pe.wait_ge(S["gr_Of"], c.need("gr_Of"))
                    for i in range(4):
                        o = bk(7, i * P, P)
                        if t:
                            mm(o, gS[:, i, :], qe[:, 4 * g + i, P:T], start=True, stop=False)
                        m = mm(o, gV[:, i, :], gAT[:, 4 * g + i, t, :], start=not t, stop=True)
                        if i == 3:
                            m.then_inc(S["gr_O"], 1)
                    yield
                pe.wait_ge(S["gr_Of"], c.need("gr_Of"))

            def attention(heads, kt, kf, vt, side=None):
                def logits(h):
                    for qt in range(TT):
                        for k in range(kt):
                            m = mm(bk(2 + h % 2, 256 * qt, 256), qf[:, h * kt + k, qt * P:(qt + 1) * P], kf[:, h * kt + k, :], start=k == 0, stop=k == kt - 1)
                            if not qt and not k:
                                release(m)
                            if qt and k == kt - 1:
                                m.then_inc(S["at_L"], 1)

                logits(0)
                for h in range(heads):
                    if h + 1 < heads:
                        logits(h + 1)
                    if side is not None:
                        next(side)
                    pe.wait_ge(S["at_p"], c.need("at_p"))
                    for s in range(TT):
                        for qt in range(TT):
                            m = tr(bk(4 + h % 2, 256 * s + P * qt, P), Pr[:, h % 2, qt * 256 + s * P:qt * 256 + (s + 1) * P])
                            if s and qt:
                                m.then_inc(S["at_T"], 1)
                    if side is not None:
                        next(side)
                    pe.wait_ge(S["at_PT"], c.need("at_PT"))
                    for d in range(kt):
                        j = h * kt + d
                        due = c.need("at_Of", 1, spare=2)
                        if due is not None:
                            pe.wait_ge(S["at_Of"], due)
                        for s in range(TT):
                            m = mm(bk(6 + j % 2, 0, T), vt[:, s, j * P:(j + 1) * P], PT[:, h % 2, s * 256:(s + 1) * 256], start=s == 0, stop=s == 1)
                            if s:
                                m.then_inc(S["at_O"], 1)
                pe.wait_ge(S["at_Of"], c.need("at_Of", 0))

            def mla(l):
                proj_chunks(1, feat)
                w = chunk(MIX_SLOTS, 3)
                proj(w[:, 0:1024].rearrange("p (k n) -> p k n", k=KT), 1, feat)
                o = proj_slot()
                for t in range(TT):
                    for k in range(KT):
                        m = mm(o[:, 8 * t:8 * t + 8], feat[:, k, t * P:(t + 1) * P], w[:, 1024 + 8 * k:1032 + 8 * k], start=k == 0, stop=k == KT - 1)
                        if t and k == KT - 1:
                            m.then_inc(S["proj_full"], 1)
                owed[0] += 1
                pe.wait_ge(S["ml_sq"], c.need("ml_sq"))
                for i in range(4):
                    m = mm(bk(2, 256 * (i // 2), T), C("ones"), mt[:, i, :], start=i % 2 == 0, stop=i % 2 == 1)
                    if i == 3:
                        m.then_inc(S["ml_ss"], 1)
                    if i == 0:
                        release(m)
                mm(bk(3, 0, T), C("blk"), kI, start=True, stop=True).then_inc(S["kI_m"], 1)
                w = chunk(MIX_SLOTS).rearrange("p (k n) -> p k n", k=KT)
                proj(w[:, :, 0:256], 2, memf)
                pe.wait_ge(S["kI_v"], c.need("kI_v"))
                mm(bk(3, T, T), C("blk"), mt[:, 4, :], start=True, stop=True).then_inc(S["kI_var"], 1)
                proj(w[:, :, 256:512], 2, memf)
                owed[0] += 1
                proj_chunks(1, memf)
                pe.wait_ge(S["ml_n"], c.need("ml_n"))
                w = chunk(MIX_SLOTS, 2)
                proj(w[:, 0:2048].rearrange("p (k n) -> p k n", k=2), 8, cqk[:, 0:2], 2)
                proj(w[:, 2048:4096].rearrange("p (k n) -> p k n", k=2), 8, cqk[:, 2:4], 2)
                owed[0] += 1
                w = chunk(MIX_SLOTS, 2)
                proj_tok(w[:, 0:2048].rearrange("p (k n) -> p k n", k=2), cqk[:, 2:4], 2, 4)
                proj(w[:, 2048:3072].rearrange("p (k n) -> p k n", k=2), 4, cqk[:, 0:2], 2)
                owed[0] += 1
                pe.wait_ge(S["kI_n"], c.need("kI_n"))
                pe.wait_ge(S["proj_evac"], c.need("proj_evac", 0))
                for n in range(TT * 8):
                    qt, h = n // 8, n % 8
                    r = 64 * (h % 2)
                    due = c.need("ix_rl", 1, spare=4)
                    if due is not None:
                        pe.wait_ge(S["ix_rl"], due)
                    mm(bk(2 + h % 4, 0, 256), qI[r:r + 64, h // 2, qt * P:(qt + 1) * P], kI[r:r + 64, :], start=True, stop=True).then_inc(S["ix_full"], 1)
                pe.wait_ge(S["ix_rl"], c.need("ix_rl", 0))
                for i in range(2):
                    w = chunk(MIX_SLOTS).rearrange("p (k n) -> p k n", k=KT)
                    proj_tok(w, memf, KT, 2)
                    owed[0] += 1
                attention(8, 1, kf, vt, gates_beside())

            def to_residual(src):
                for h in range(2):
                    w = chunk(MIX_SLOTS).rearrange("p (k n) -> p k n", k=KT)
                    for t in range(TT):
                        for k in range(KT):
                            m = mm(bk(4 + 2 * h + t), src[:, k, t * P:(t + 1) * P], w[:, k, :], start=k == 0, stop=k == KT - 1)
                            if k == 0:
                                release(m)
                            if k == KT - 1:
                                m.then_inc(S["mix_full"], 1)
                    owed[0] += 1
                c.skip("x_new", 4)

            def xattn(l):
                proj_chunks(2, feat)
                pe.wait_ge(S["proj_evac"], c.need("proj_evac", 0))
                attention(4, 2, kf_x, vt_x)
                to_residual(branch)

            ngu = [0]

            nff = [0]

            def weights_of(*shape):
                b = nff[0] % FFN_BUFS
                nff[0] += 1
                pe.wait_ge(S["w_lo"], c.need("w_lo"))
                return [view(w_parts[b][i], 0, *shape) for i in range(2)]

            def ffn(steps):
                for f in range(steps):
                    wg = weights_of(KT, 2 * P)
                    wu = weights_of(KT, 2 * P)
                    for j in range(2):
                        b = ngu[0] % 4
                        ngu[0] += 1
                        due = c.need("act_t", 1, spare=4, view="bank")
                        if due is not None:
                            pe.wait_ge(S["act_t"], due)
                        for col, w in ((0, wg), (T, wu)):
                            for n, (wi, xi) in enumerate(PASSES):
                                for k in range(KT):
                                    m = mm(bk(b, col, T), w[wi][:, k, j * P:(j + 1) * P], feat_parts[xi][:, k, :],
                                           start=n == 0 and k == 0, stop=n == 2 and k == KT - 1)
                                    if n == 0 and k == 0 and not col and bufs_owed[0]:
                                        m.then_inc(S["wb_used"], bufs_owed[0])
                                        bufs_owed[0] = 0
                        m.then_inc(S["gu_full"], 1)
                    wd = weights_of(2, D)
                    if f == 0:
                        pe.wait_ge(S["x_new"], c.need("x_new", 0))
                    for j in range(2):
                        pe.wait_ge(S["act_t"], c.need("act_t"))
                        for t in range(TT):
                            for h in range(2):
                                for n, (wi, xi) in enumerate(PASSES):
                                    m = mm(bk(4 + 2 * t + h), act_parts[xi][:, nact[0] % 4, t * P:(t + 1) * P],
                                           wd[wi][:, j, h * 512:(h + 1) * 512],
                                           start=f == 0 and j == 0 and n == 0, stop=f == steps - 1 and j == 1 and n == 2)
                                    if j == 0 and t == 0 and h == 0 and n == 0:
                                        m.then_inc(S["wb_used"], 2)
                        nact[0] += 1
                    bufs_owed[0] = 1
                m.then_inc(S["down_full"], 1)
                c.skip("x_new", 4)

            nact = [0]
            bufs_owed = [0]

            pe.wait_ge(S["par_dma"], c.need("par_dma", 48))
            norm()
            for l in range(LAYERS):
                norm()
                pe_s.phase()
                rwkv(l)
                gdn(l)
                mla(l)
                pe.wait_ge(S["merged"], c.need("merged"))
                to_residual(yacc)
                norm()
                xattn(l)
                norm()
                pe_s.phase()
                if l == 0:
                    ffn(FF // 256)
                else:
                    for t in range(TT):
                        for k in range(KT):
                            m = mm(bk(3, 8 * t, 8), feat[:, k, t * P:(t + 1) * P], rout[:, k, :], start=k == 0, stop=k == KT - 1)
                            if t and k == KT - 1:
                                m.then_inc(S["rt_full"], 1)
                    pe.wait_ge(S["rt_l"], c.need("rt_l"))
                    ffn(FE // 256)
                    with pe.Fori(1, NE - 1) as e:
                        c.begin_loop(e - 1, dict(act_t=FE // P, x_new=4, w_lo=FE_CHUNKS))
                        ffn(FE // 256)
                    c.end_loop(NE - 2)
                    ffn(FE // 256)

        @block.scalar
        def _(act):
            c = Counter(S)

            sc = nc.scalar

            def norm(src, gain, l, dst, x_new=(0, 0)):
                sc.preload_act_table_set("sqrt_and_others")
                for t in range(TT):
                    if x_new[t]:
                        act.wait_ge(S["x_new"], c.need("x_new", x_new[t]))
                    act.wait_ge(*c.last())
                    sc.activation(sqj, src[:, t, :], ACT.Square, accum_out=small[:, t:t + 1]).then_inc(*c.inc("norm_ss"))
                act.wait_ge(S["norm_ms"], c.need("norm_ms"))
                act.wait_ge(*c.last())
                sc.activation(small[:, 4:6], small[:, 2:4], ACT.Sqrt).then_inc(*c.inc("norm_sd"))
                if dst is None:
                    return
                for k in range(KT // 2):
                    if k % 2 == 0:
                        act.wait_ge(S["norm_T"], c.need("norm_T"))
                    act.wait_ge(*c.last())
                    sc.activation(dst[:, k, :], bk(4 + k // 2, (k % 2) * 256, T), ACT.Copy, scale=pc(l, gain, k)).then_inc(*c.inc("feat_ready"))
                c.skip("norm_T", 2)

            nproj = [0]

            def evac(dst, f=ACT.Copy, **kw):
                n = nproj[0] % 2
                nproj[0] += 1
                act.wait_ge(S["proj_full"], c.need("proj_full"))
                act.wait_ge(*c.last())
                sc.activation(dst, bk(n, 0, 256) if dst.shape[-1] != 8 else
                  bk(n, 0, 16).rearrange("p (a b) -> p a b", a=2), f, **kw).then_inc(*c.inc("proj_evac"))

            def inverted(levels, sets):
                for b in range(levels + 1):
                    for i, xtv in enumerate(sets if b else ()):
                        act.wait_ge(S["inv_T"], c.need("inv_T"))
                        act.wait_ge(*c.last())
                        sc.activation(xtv, bk4(4 + i), ACT.Copy).then_inc(*c.inc("inv_XT"))
                    if b < levels:
                        if levels == LEVELS:
                            yield
                        yield

            def gates_beside(dst):
                for j in range(KT):
                    yield
                    evac(dst[:, j, :])
                    yield

            def gates(dst):
                for i in range(2):
                    act.wait_ge(*c.last())
                    sc.activation(dst[:, 4 * i:4 * i + 4, :], dst[:, 4 * i:4 * i + 4, :], ACT.Sigmoid).then_inc(*c.inc("gate_sig"))

            def front_rw(l, cp):
                def values(p):
                    j = 2 * cp + p
                    act.wait_ge(*c.last())
                    sc.activation(VV[0:64, :, 64:128], rkv[0:64, 16 + j, :].rearrange("p (a b) -> p a b", a=4), ACT.Copy).then_inc(*c.inc("act_step"))
                    act.wait_ge(*c.last())
                    sc.activation(VV[64:128, :, 0:64], rkv[64:128, 16 + j, :].rearrange("p (a b) -> p a b", a=4), ACT.Copy).then_inc(*c.inc("rw_vv"))

                values(0)
                act.wait_ge(S["rw_lora"], c.need("rw_lora"))
                for p in range(2):
                    act.wait_ge(*c.last())
                    sc.activation(tmp[:, 0 + p, :], bk(0, p * T, T), ACT.Sigmoid, bias=pc(l, "w0", 2 * cp + p)).then_inc(*c.inc("act_step"))
                    act.wait_ge(*c.last())
                    sc.activation(tmp[:, 6 + p, :], bk(1, p * T, T), ACT.Sigmoid, bias=pc(l, "a0", 2 * cp + p)).then_inc(*c.inc("rw_sig" if p else "act_step"))
                sc.preload_act_table_set("natural_log_exp_and_others")
                yield
                act.wait_ge(S["rw_nrm"], c.need("rw_nrm"))
                act.wait_ge(*c.last())
                sc.activation(tw(4), tw(4), ACT.Ln).then_inc(*c.inc("act_step"))
                act.wait_ge(*c.last())
                sc.activation(tw(4), tw(4), ACT.Exp, scale=-0.5).then_inc(*c.inc("rw_sqrt"))
                act.wait_ge(S["rw_cum"], c.need("rw_cum"))
                act.wait_ge(*c.last())
                sc.activation(tw(2), tw(1), ACT.Exp, scale=-DECAY).then_inc(*c.inc("act_step"))
                act.wait_ge(*c.last())
                sc.activation(tw(0), tw(0), ACT.Exp, scale=-DECAY).then_inc(*c.inc("act_step"))
                act.wait_ge(*c.last())
                sc.activation(tw(1), tw(1), ACT.Exp, scale=DECAY).then_inc(*c.inc("rw_exp"))
                if cp < RW_PAIRS // 2 - 1:
                    sc.preload_act_table_set("sigmoid_and_others")
                yield
                yield
                for p in range(2):
                    s = (2 * cp + p) % 4
                    act.wait_ge(S["rw_tr"], c.need("rw_tr"))
                    if p == 0:
                        values(1)
                    act.wait_ge(*c.last())
                    sc.activation(BKt[:, s], bk4(6), ACT.Copy).then_inc(*c.inc("act_step"))
                    act.wait_ge(*c.last())
                    sc.activation(Vad[:, s], bk4(7), ACT.Copy).then_inc(*c.inc("rw_tm"))
                    yield

            def recur_rw(g):
                def outputs(q):
                    act.wait_ge(S["rc_OT"], c.need("rc_OT"))
                    for lo in (0, 64):
                        act.wait_ge(*c.last())
                        sc.activation(branch[lo:lo + 64, 4 * g:4 * g + 4, 64 * q:64 * q + 64], bk4(4)[lo:lo + 64, :, 64 - lo:128 - lo], ACT.Copy).then_inc(*c.inc("rc_Of" if lo else "act_step"))

                for q in range(RW_CHUNKS):
                    if q:
                        outputs(q - 1)
                    yield
                    yield
                outputs(RW_CHUNKS - 1)

            def rwkv(l):
                for n in range(25):
                    due = c.need("raw_free", 1, spare=4)
                    if due is not None:
                        act.wait_ge(S["raw_free"], due)
                    evac(raw[:, n % 4, 3:259])
                act.wait_ge(S["raw_free"], c.need("raw_free", 0))
                if l == 0:
                    act.wait_ge(*c.last())
                    sc.activation(vfirst[:, :, :], rkv[:, 16:24, :], ACT.Copy).then_inc(*c.inc("act_step"))
                act.wait_ge(*c.last())
                sc.activation(lora[0:64, :], lora[0:64, :], ACT.Tanh).then_inc(*c.inc("rkv_ready"))
                if l:
                    act.wait_ge(S["vlow_full"], c.need("vlow_full"))
                    act.wait_ge(*c.last())
                    sc.activation(vlo[0:32, :], bk(2, 0, T)[0:32], ACT.Copy).then_inc(*c.inc("vlow"))
                    for j in range(KT):
                        act.wait_ge(S["vres_full"], c.need("vres_full"))
                        due = c.need("vres_done", 1, spare=2)
                        if due is not None:
                            act.wait_ge(S["vres_done"], due)
                        act.wait_ge(*c.last())
                        sc.activation(tmp[:, j % 2, :], bk(3 + j % 2, 0, T), ACT.Sigmoid, bias=pc(l, "v0", j)).then_inc(*c.inc("vres_sig"))
                if l:
                    act.wait_ge(S["vres_done"], c.need("vres_done", 0))
                gate = gates_beside(gate_rw)
                for g in range(2):
                    a, b = front_rw(l, 2 * g), front_rw(l, 2 * g + 1)
                    beside(recur_rw(g - 1) if g else None, a, 1, 2)
                    beside(None, a)
                    beside(inverted(6, [XT[:, i] for i in range(2)]), b)
                    beside(inverted(6, [XT[:, 2 + i] for i in range(2)]), None)
                beside(recur_rw(1), gate, 1, 8)
                for i in range(4):
                    next(gate)
                    act.wait_ge(S["gn_var"], c.need("gn_var"))
                    act.wait_ge(*c.last())
                    sc.activation(tmp[:, 4:6, :], tmp[:, 2:4, :], ACT.Ln).then_inc(*c.inc("act_step"))
                    act.wait_ge(*c.last())
                    sc.activation(tmp[:, 6:8, :], tmp[:, 4:6, :], ACT.Exp, scale=-0.5).then_inc(*c.inc("gn_sd"))
                    next(gate)
                gates(gate_rw)

            def front_gd(heads, bufs):
                gt, kq, dec, (b_bc, b_ss, b_kk, b_tr) = bufs
                for h in heads:
                    act.wait_ge(S["gd_bc"], c.need("gd_bc"))
                    act.wait_ge(*c.last())
                    sc.activation(gt[:, 2, :], bk(b_bc, 0, T), ACT.Exp).then_inc(*c.inc("gd_eg"))
                    act.wait_ge(S["gd_nrm"], c.need("gd_nrm"))
                    act.wait_ge(*c.last())
                    sc.activation(gt[:, 4:6, :], gt[:, 4:6, :], ACT.Ln).then_inc(*c.inc("act_step"))
                    act.wait_ge(*c.last())
                    sc.activation(gt[:, 6:8, :], gt[:, 4:6, :], ACT.Exp, scale=-0.5).then_inc(*c.inc("gd_sqrt"))
                    act.wait_ge(S["gd_dif"], c.need("gd_dif"))
                    act.wait_ge(*c.last())
                    sc.activation(small[:, 32 + h:33 + h], small[:, 24 + h:25 + h], ACT.Exp).then_inc(*c.inc("act_step"))
                    act.wait_ge(*c.last())
                    sc.activation(dec, dec, ACT.Exp).then_inc(*c.inc("gd_dec"))
                    yield
                    yield
                    act.wait_ge(S["gd_tr"], c.need("gd_tr"))
                    act.wait_ge(*c.last())
                    sc.activation(ktm[:, h, :], bk(b_tr, 0, P), ACT.Copy, scale=small[:, 32 + h:33 + h]).then_inc(*c.inc("act_step"))
                    act.wait_ge(*c.last())
                    sc.activation(vtm[:, h].rearrange("p a b -> p (a b)"), bk(b_tr, P, T), ACT.Copy).then_inc(*c.inc("gd_tm"))
                    yield

            def recur_gd(g):
                for t in range(TT):
                    if t:
                        yield
                    yield
                    act.wait_ge(S["gr_O"], c.need("gr_O"))
                    act.wait_ge(*c.last())
                    sc.activation(branch[:, 4 * g:4 * g + 4, t * P:(t + 1) * P], bk4(7), ACT.Copy).then_inc(*c.inc("gr_Of"))
                    yield

            def gdn(l):
                for n in range(24):
                    due = c.need("raw_free", 1, spare=4)
                    if due is not None:
                        act.wait_ge(S["raw_free"], due)
                    if n >= 2:
                        act.wait_ge(S["raw_free"], 49 * l + 25 + n - 1)
                        act.wait_ge(*c.last())
                        sc.activation(rkv[:, n - 2, :], rkv[:, n - 2, :], ACT.Silu).then_inc(*c.inc("act_step"))
                    evac(raw[:, n % 4, 3:259])
                for n in (22, 23):
                    act.wait_ge(S["raw_free"], 49 * l + 25 + n + 1)
                    act.wait_ge(*c.last())
                    sc.activation(rkv[:, n, :], rkv[:, n, :], ACT.Silu).then_inc(*c.inc("rkv_ready" if n == 23 else "act_step"))
                act.wait_ge(S["gd_ab"], c.need("gd_ab", 2))
                act.wait_ge(*c.last())
                sc.activation(b8[0:8, :], bk(3, 0, T)[0:8], ACT.Sigmoid).then_inc(*c.inc("act_step"))
                act.wait_ge(*c.last())
                sc.activation(ab[0:8, 0, :], bk(2, 0, T)[0:8], ACT.Abs, bias=pc(l, "dt_bias")[0:8]).then_inc(*c.inc("act_step"))
                act.wait_ge(*c.last())
                sc.activation(ab[0:8, 3, :], bk(2, 0, T)[0:8], ACT.Relu, bias=pc(l, "dt_bias")[0:8]).then_inc(*c.inc("act_step"))
                act.wait_ge(*c.last())
                sc.preload_act_table_set("natural_log_exp_and_others")
                sc.activation(small[0:8, 8:9], pc(l, "A_log")[0:8], ACT.Exp).then_inc(*c.inc("act_step"))
                act.wait_ge(*c.last())
                sc.activation(ab[0:8, 1, :], ab[0:8, 0, :], ACT.Exp, scale=-1.0).then_inc(*c.inc("act_step"))
                act.wait_ge(*c.last())
                sc.activation(ab[0:8, 2, :], ab[0:8, 1, :], ACT.Ln, bias=1.0).then_inc(*c.inc("gd_abs"))
                second = front_gd(range(4, 8), GD_BUFS[0])
                beside(front_gd((0, 2), GD_BUFS[0]), front_gd((1, 3), GD_BUFS[1]))
                beside(inverted(7, [heads2(gXT, i) for i in range(2)]), second, 1)
                beside(inverted(7, [heads2(gXT, 2 + i) for i in range(2)]), recur_gd(0))
                beside(recur_gd(1), None)
                gate = gates_beside(gate_gd)
                for i in range(4):
                    act.wait_ge(S["gt_ms"], c.need("gt_ms"))
                    act.wait_ge(*c.last())
                    sc.activation(gt[:, 4:6, :], gt[:, 2:4, :], ACT.Ln).then_inc(*c.inc("act_step"))
                    act.wait_ge(*c.last())
                    sc.activation(gt[:, 6:8, :], gt[:, 4:6, :], ACT.Exp, scale=-0.5).then_inc(*c.inc("gt_sd"))
                    for _ in range(4):
                        next(gate)
                gates(gate_gd)

            def attention(heads, kt, masked, side=None):
                for h in range(heads):
                    act.wait_ge(S["at_max"], c.need("at_max"))
                    for qt in range(TT):
                        src = Lm[:, h % 2, qt * T:(qt + 1) * T] if masked else bk(2 + h % 2, qt * T, T)
                        act.wait_ge(*c.last())
                        sc.activation(Pr[:, h % 2, qt * T:(qt + 1) * T], src, ACT.Exp, bias=amax[:, h % 2, qt:qt + 1], accum_out=asum[:, h % 2, qt:qt + 1]).then_inc(*c.inc("at_exp"))
                    if side is not None:
                        next(side)
                    act.wait_ge(S["at_T"], c.need("at_T"))
                    act.wait_ge(*c.last())
                    sc.activation(PT[:, h % 2, :], bk(4 + h % 2), ACT.Copy).then_inc(*c.inc("at_PT"))
                    for d in range(kt):
                        j = h * kt + d
                        act.wait_ge(S["at_O"], c.need("at_O"))
                        act.wait_ge(*c.last())
                        sc.activation(branch[:, j, :], bk(6 + j % 2, 0, T), ACT.Copy).then_inc(*c.inc("at_Of"))
                    if side is not None:
                        next(side)

            def mla(l):
                for n in range(4):
                    evac(cqk[:, n, :])
                evac(kI)
                evac(wI, scale=8 ** -0.5 * 64 ** -0.5)
                act.wait_ge(S["kI_ms"], c.need("kI_ms"))
                act.wait_ge(*c.last())
                sc.activation(mt[:, 5, :], mt[:, 4, :], ACT.Sqrt).then_inc(*c.inc("kI_sd"))
                act.wait_ge(S["ml_ms"], c.need("ml_ms"))
                act.wait_ge(*c.last())
                sc.activation(mt[:, 2:4, :], mt[:, 0:2, :], ACT.Sqrt).then_inc(*c.inc("ml_sd"))
                for n in range(8):
                    evac(kf_x[:, n, :])
                for n in range(8):
                    evac(qf[:, n, :], scale=P ** -0.5)
                for n in range(8):
                    evac(kf[:, n, :])
                for n in range(8):
                    evac(vt[:, n // 4, (n % 4) * 256:(n % 4 + 1) * 256])
                for n in range(4):
                    evac(qI[:, n, :])
                for n in range(16):
                    h = n % 8
                    act.wait_ge(S["ix_full"], c.need("ix_full"))
                    due = c.need("ix_free", 1, spare=4)
                    if due is not None:
                        act.wait_ge(S["ix_free"], due)
                    act.wait_ge(*c.last())
                    sc.activation(rl[:, n % 4, :], bk(2 + h % 4, 0, 256), ACT.Relu).then_inc(*c.inc("ix_rl"))
                for i in range(2):
                    for n in range(4):
                        t, q = n // 2, n % 2
                        evac(vt_x[:, t, i * 512 + q * 256:i * 512 + (q + 1) * 256])
                attention(8, 1, True, gates_beside(gate_ml))
                gates(gate_ml)

            def xattn(l):
                for n in range(8):
                    evac(qf[:, n, :], scale=256 ** -0.5)
                attention(4, 2, False)

            nf = [0]

            nff = [0]

            def high_part():
                n = nff[0]
                nff[0] += 1
                b = n % FFN_BUFS
                act.wait_ge(S[f"fslot{b}"], c.need(f"fslot{b}", 16))
                due = c.need("wb_used", 1, spare=FFN_BUFS)
                if due is not None:
                    act.wait_ge(S["wb_used"], due)
                sc.activation(w_parts[b][0], ring[:, b * FFN_SLOT:(b + 1) * FFN_SLOT], ACT.Copy).then_inc(*c.inc("w_hi"))

            def ffn(steps, more=False):
                for f in range(steps):
                    for j in range(2):
                        n = nf[0] % 4
                        nf[0] += 1
                        act.wait_ge(S["gu_full"], c.need("gu_full"))
                        sc.activation(silu_t[:, n, :], bk(n, 0, T), ACT.Silu).then_inc(*c.inc("silu"))
                        if f < steps - 1 or more:
                            high_part()
                    if f < steps - 1 or more:
                        high_part()

            act.wait_ge(S["par_dma"], 48)
            sc.activation(small[0:1, 78:79], par[0:1, 0, 0:1], ACT.Copy).then_inc(*c.inc("act_step"))
            act.wait_ge(S["mem_dma"], 16)
            norm(yflat.rearrange("p (a b) -> p a b", a=TT), "mem_norm", 0, memf)
            act.wait_ge(S["in_dma"], 16)
            for l in range(LAYERS):
                if l:
                    act.wait_ge(S["x_new"], c.need("x_new", 4))
                norm(xt, "norm_mix", l, feat)
                rwkv(l)
                gdn(l)
                mla(l)
                norm(xt, "norm_xattn", l, feat, (3, 1))
                xattn(l)
                norm(xt, "norm_ffn", l, feat, (3, 1))
                c.skip("feat_half", 8 if l else 12)
                act.wait_ge(S["feat_half"], c.need("feat_half", 4))
                act.wait_ge(*c.last())
                sc.activation(feat_parts[0], feat[:, :, :], ACT.Copy).then_inc(*c.inc("f_hi"))
                for _ in range(3):
                    high_part()
                if l == 0:
                    ffn(FF // 256)
                else:
                    act.wait_ge(S["rt_d"], c.need("rt_d"))
                    sc.activation(small[:, 44:46], small[:, 42:44], ACT.Exp).then_inc(*c.inc("rt_e"))
                    ffn(FE // 256, True)
                    with act.Fori(1, NE - 1) as e:
                        c.begin_loop(e - 1, dict(gu_full=FE // P, wb_used=FE_CHUNKS,
                                                 **{f"fslot{b}": 16 * FE_CHUNKS // FFN_BUFS for b in range(FFN_BUFS)}))
                        ffn(FE // 256, True)
                    c.end_loop(NE - 2)
                    ffn(FE // 256)
            act.wait_ge(S["x_new"], c.need("x_new", 4 * NE))
            norm(xt, None, 0, None)

        @block.vector
        def _(dve):
            c = Counter(S)

            v = nc.vector

            def norm(src, gain=None, l=0, dst=None):
                final = dst is None
                dve.wait_ge(S["norm_ss"], c.need("norm_ss", 2))
                v.tensor_scalar(small[:, 2:4], small[:, 0:2], 1.0 / D, EPS, ALU.mult, ALU.add).then_inc(*c.inc("norm_ms"))
                dve.wait_ge(*c.last())
                dve.wait_ge(S["norm_sd"], c.need("norm_sd"))
                v.reciprocal(small[:, 6:8], small[:, 4:6]).then_inc(*c.inc("dve_step"))
                dve.wait_ge(*c.last())
                for t in range(TT):
                    if final:
                        if t == 0:
                            dve.wait_ge(S["par_dma"], 64)
                        v.scalar_tensor_tensor(yflat[:, t * D:(t + 1) * D], src[:, t, :], small[:, 6 + t:7 + t],
                                                 memf[:, 0:4, :].rearrange("p a b -> p (a b)"), ALU.mult, ALU.mult).then_inc(*c.inc("norm_xn"))
                        dve.wait_ge(*c.last())
                    else:
                        v.tensor_scalar(xn[:, t, :], src[:, t, :], small[:, 6 + t:7 + t], None, ALU.mult).then_inc(*c.inc("norm_xn"))
                        dve.wait_ge(*c.last())
                if not final:
                    c.skip("norm_T", 2)
                    for k in range(KT // 2, KT):
                        if k % 2 == 0:
                            dve.wait_ge(S["norm_T"], c.need("norm_T"))
                        v.tensor_scalar(dst[:, k, :], bk(4 + k // 2, (k % 2) * 256, T), pc(l, gain, k), None, ALU.mult).then_inc(*c.inc("feat_half"))
                        dve.wait_ge(*c.last())

            def pad_raw():
                for n in range(4):
                    v.memset(raw[:, n, 0:3], 0.0).then_inc(*c.inc("dve_step"))
                    dve.wait_ge(*c.last())

            def gated(g, first, last):
                c.skip("proj_evac", KT)
                for i in range(2):
                    t = slice(4 * i, 4 * i + 4)
                    dve.wait_ge(S["gate_sig"], c.need("gate_sig"))
                    v.tensor_tensor(yacc[:, t, :] if first else branch[:, t, :], g[:, t, :], branch[:, t, :], ALU.mult).then_inc(*c.inc("dve_step"))
                    dve.wait_ge(*c.last())
                    if not first:
                        v.tensor_tensor(yacc[:, t, :], yacc[:, t, :], branch[:, t, :], ALU.add).then_inc(*c.inc("merged" if last and i else "dve_step"))
                        dve.wait_ge(*c.last())

            def inverted(levels, sets):
                for b in range(levels):
                    for i, (xv, yv) in enumerate(sets):
                        dve.wait_ge(S["inv_Y"], c.need("inv_Y"))
                        v.tensor_tensor(yv, bk4(2 + i), b4(C("level", P * b, P * b + P)), ALU.mult).then_inc(*c.inc("inv_Ym" if b else "dve_step"))
                        dve.wait_ge(*c.last())
                        if b == 0:
                            v.tensor_tensor(xv, b4(C("ident")), yv, ALU.add).then_inc(*c.inc("inv_X"))
                            dve.wait_ge(*c.last())
                    if levels == LEVELS:
                        yield
                    if b:
                        for i, (xv, yv) in enumerate(sets):
                            dve.wait_ge(S["inv_D"], c.need("inv_D"))
                            v.tensor_tensor(xv, bk4(2 + i), xv, ALU.add).then_inc(*c.inc("inv_X"))
                            dve.wait_ge(*c.last())
                    yield
                dve.wait_ge(S["inv_XT"], c.need("inv_XT", levels * len(sets)))

            def r4(ap):
                return ap.rearrange("p (a b) -> p a b", a=4)

            def front_rw(l, cp):
                j = 2 * cp
                s = j % 4
                r_, k_, v_ = (rkv[:, 8 * i + j:8 * i + j + 2, :] for i in range(3))
                sig, cum, dec_, icl, nrm, bon, kk, kx = (tw(i) for i in range(8))
                for p in range(2):
                    v.tensor_scalar(kk[:, p, :], k_[:, p, :], pc(l, "k_k", j + p), None, ALU.mult).then_inc(*c.inc("dve_step"))
                    dve.wait_ge(*c.last())
                v.tensor_tensor(nrm, kk, kk, ALU.mult).then_inc(*c.inc("rw_kksq"))
                dve.wait_ge(*c.last())
                dve.wait_ge(S["rw_sig"], c.need("rw_sig"))
                for p in range(2):
                    v.tensor_scalar(bon[:, p, :], icl[:, p, :], -1.0, pc(l, "k_a", j + p), ALU.add, ALU.mult).then_inc(*c.inc("dve_step"))
                    dve.wait_ge(*c.last())
                v.scalar_tensor_tensor(kx, bon, 1.0, k_, ALU.add, ALU.mult).then_inc(*c.inc("dve_step"))
                dve.wait_ge(*c.last())
                for p in range(2):
                    v.scalar_tensor_tensor(bon[:, p, :], r_[:, p, :], pc(l, "r_k", j + p), kx[:, p, :], ALU.mult, ALU.mult).then_inc(*c.inc("rw_bon" if p else "dve_step"))
                    dve.wait_ge(*c.last())
                yield
                v.tensor_tensor_scan(cum.rearrange("p a b -> p (a b)"), C("cumask"), sig.rearrange("p a b -> p (a b)"), 0.0, ALU.mult, ALU.add).then_inc(*c.inc("dve_step"))
                dve.wait_ge(*c.last())
                v.tensor_tensor(sig, cum, sig, ALU.subtract).then_inc(*c.inc("rw_cum"))
                dve.wait_ge(*c.last())
                dve.wait_ge(S["rw_sums"], c.need("rw_sums"))
                v.tensor_scalar(nrm, bank[6][:, :].rearrange("p (a b) -> p a b", a=2), EPS, None, ALU.add).then_inc(*c.inc("rw_nrm"))
                dve.wait_ge(*c.last())
                v.tensor_tensor(k_, bank[7][:, :].rearrange("p (a b) -> p a b", a=2), v_, ALU.mult).then_inc(*c.inc("dve_step"))
                dve.wait_ge(*c.last())
                yield
                dve.wait_ge(S["rw_sqrt"], c.need("rw_sqrt"))
                v.tensor_tensor(kk, kk, nrm, ALU.mult).then_inc(*c.inc("dve_step"))
                dve.wait_ge(*c.last())
                v.tensor_tensor(icl, kk, icl, ALU.mult).then_inc(*c.inc("dve_step"))
                dve.wait_ge(*c.last())
                dve.wait_ge(S["rw_exp"], c.need("rw_exp"))
                for lo in (0, 64):
                    p_ = slice(lo, lo + 64)
                    za, zb = slice(lo, lo + 64), slice(64 - lo, 128 - lo)
                    f = lambda ap: ap[p_].rearrange("p a (b c) -> p (a b) c", b=4)
                    zr = ZR[p_, s:s + 2].rearrange("p a b c -> p (a b) c")
                    v.tensor_tensor(BK[p_, :, za], f(icl), f(cum), ALU.mult).then_inc(*c.inc("dve_step"))
                    dve.wait_ge(*c.last())
                    v.tensor_tensor(BK[p_, :, zb], f(kx), f(cum), ALU.mult).then_inc(*c.inc("dve_step"))
                    dve.wait_ge(*c.last())
                    v.scalar_tensor_tensor(zr[:, :, za], f(kk), -1.0, f(sig), ALU.mult, ALU.mult).then_inc(*c.inc("dve_step"))
                    dve.wait_ge(*c.last())
                    v.tensor_tensor(zr[:, :, zb], f(r_), f(dec_), ALU.mult).then_inc(*c.inc("rw_fm" if lo else "dve_step"))
                    dve.wait_ge(*c.last())
                for p in range(2):
                    v.tensor_copy(wc[:, s + p, :], dec_[:, p, 63:T:64]).then_inc(*c.inc("dve_step"))
                    dve.wait_ge(*c.last())
                yield
                for p in range(2):
                    dve.wait_ge(S["rw_G"], c.need("rw_G"))
                    v.tensor_tensor(GA[:, s + p], bk4(0), b4(C("maskGA")), ALU.mult).then_inc(*c.inc("dve_step"))
                    dve.wait_ge(*c.last())
                    v.tensor_tensor(GB[:, s + p], bk4(1), b4(C("maskGB")), ALU.mult).then_inc(*c.inc("rw_N"))
                    dve.wait_ge(*c.last())
                    yield
                for p in range(2):
                    v.tensor_copy(NT[p][0:64, :, 0:64], GA[0:64, s + p, :, 0:64]).then_inc(*c.inc("dve_step"))
                    dve.wait_ge(*c.last())
                    v.tensor_copy(NT[p][64:128, :, 64:128], GB[64:128, s + p, :, 64:128]).then_inc(*c.inc("rw_NT"))
                    dve.wait_ge(*c.last())

            def rwkv(l):
                pad_raw()
                for n in range(25):
                    dst = rkv[:, n, :] if n < 24 else lora
                    dve.wait_ge(S["proj_evac"], c.need("proj_evac"))
                    v.tensor_tensor(dst, raw[:, n % 4, 2:258], raw[:, n % 4, 3:259], ALU.subtract).then_inc(*c.inc("dve_step"))
                    dve.wait_ge(*c.last())
                    v.scalar_tensor_tensor(dst, dst, pc(l, "mu", n), raw[:, n % 4, 3:259], ALU.mult, ALU.add).then_inc(*c.inc("raw_free"))
                    dve.wait_ge(*c.last())
                v.memset(NT12, 0.0).then_inc(*c.inc("dve_step"))
                dve.wait_ge(*c.last())
                if l:
                    for j in range(KT):
                        d = tmp[:, 2 + j % 2, :]
                        v.tensor_tensor(d, vfirst[:, j, :], rkv[:, 16 + j, :], ALU.subtract).then_inc(*c.inc("dve_step"))
                        dve.wait_ge(*c.last())
                        dve.wait_ge(S["vres_sig"], c.need("vres_sig"))
                        v.tensor_tensor(d, d, tmp[:, j % 2, :], ALU.mult).then_inc(*c.inc("dve_step"))
                        dve.wait_ge(*c.last())
                        v.tensor_tensor(rkv[:, 16 + j, :], rkv[:, 16 + j, :], d, ALU.add).then_inc(*c.inc("vres_done"))
                        dve.wait_ge(*c.last())
                for lo in (0, 64):
                    v.memset(VV[lo:lo + 64, :, lo:lo + 64], 0.0).then_inc(*c.inc("dve_step"))
                    dve.wait_ge(*c.last())
                for g in range(2):
                    a, b = front_rw(l, 2 * g), front_rw(l, 2 * g + 1)
                    beside(recur_rw(g - 1) if g else None, a, 1, 2)
                    beside(None, a)
                    beside(inverted(6, [(X[i], Ym[i]) for i in range(2)]), b)
                    beside(inverted(6, [(X[i], Ym[i]) for i in range(2)]), None)
                beside(recur_rw(1), None)
                for i in range(4):
                    o = branch[:, 2 * i:2 * i + 2, :]
                    b2 = lambda n: bank[n][:, :].rearrange("p (a b) -> p a b", a=2)
                    dve.wait_ge(S["gn_m"], c.need("gn_m"))
                    v.scalar_tensor_tensor(o, b2(5), -1.0 / 64, o, ALU.mult, ALU.add).then_inc(*c.inc("dve_step"))
                    dve.wait_ge(*c.last())
                    v.tensor_tensor(tmp[:, 0:2, :], o, o, ALU.mult).then_inc(*c.inc("gn_sq"))
                    dve.wait_ge(*c.last())
                    dve.wait_ge(S["gn_v"], c.need("gn_v"))
                    v.tensor_scalar(tmp[:, 2:4, :], b2(6), 1.0 / 64, GN_EPS, ALU.mult, ALU.add).then_inc(*c.inc("gn_var"))
                    dve.wait_ge(*c.last())
                    dve.wait_ge(S["gn_sd"], c.need("gn_sd"))
                    v.tensor_tensor(o, o, tmp[:, 6:8, :], ALU.mult).then_inc(*c.inc("dve_step"))
                    dve.wait_ge(*c.last())
                    for j in (2 * i, 2 * i + 1):
                        v.tensor_scalar(branch[:, j, :], branch[:, j, :], pc(l, "gn_g", j), pc(l, "gn_b", j), ALU.mult, ALU.add).then_inc(*c.inc("dve_step"))
                        dve.wait_ge(*c.last())
                    v.tensor_tensor(o, o, rkv[:, 8 + 2 * i:10 + 2 * i, :], ALU.add).then_inc(*c.inc("gn_y"))
                    dve.wait_ge(*c.last())
                gated(gate_rw, True, False)

            def recur_rw(g):
                def scales(q):
                    for i in range(4):
                        v.tensor_scalar(Wst[:, i, :], C("maskbd"), wc[:, i, q:q + 1], None, ALU.mult).then_inc(*c.inc("dve_step"))
                        dve.wait_ge(*c.last())

                def right_side():
                    dve.wait_ge(S["rc_P1"], c.need("rc_P1"))
                    v.tensor_tensor(Rbd, bk4(2), b4(C("maskbd")), ALU.mult).then_inc(*c.inc("rc_R"))
                    dve.wait_ge(*c.last())

                right_side()
                scales(0)
                for q in range(RW_CHUNKS):
                    dve.wait_ge(S["rc_U"], c.need("rc_U"))
                    v.tensor_tensor(UV, bk4(3), Vad[:, 0:4, q, :], ALU.add).then_inc(*c.inc("rc_UV"))
                    dve.wait_ge(*c.last())
                    yield
                    if q < RW_CHUNKS - 1:
                        dve.wait_ge(S["rc_S"], c.need("rc_S"))
                        if q:
                            v.tensor_tensor(Stmp, bk4(4), Sst[q % 2], ALU.add).then_inc(*c.inc("dve_step"))
                            dve.wait_ge(*c.last())
                        v.tensor_tensor(Sst[(q + 1) % 2], Stmp if q else bk4(4), Wst, ALU.mult).then_inc(*c.inc("rc_Sn"))
                        dve.wait_ge(*c.last())
                        if q < RW_CHUNKS - 2:
                            scales(q + 1)
                        right_side()
                    dve.wait_ge(S["rc_P2"], c.need("rc_P2"))
                    v.tensor_tensor(Oad, bk4(5), b4(C("antibd")), ALU.mult).then_inc(*c.inc("rc_O"))
                    dve.wait_ge(*c.last())
                    yield

            def front_gd(heads, bufs):
                t2 = lambda ap: ap.rearrange("p (a b) -> p a b", a=2)
                gt, kq, dec, (b_bc, b_ss, b_kk, b_tr) = bufs
                for h in heads:
                    q_, k_ = rkv[:, h, :], rkv[:, 8 + h, :]
                    v.tensor_tensor(gt[:, 0, :], q_, q_, ALU.mult).then_inc(*c.inc("dve_step"))
                    dve.wait_ge(*c.last())
                    v.tensor_tensor(gt[:, 1, :], k_, k_, ALU.mult).then_inc(*c.inc("gd_sq"))
                    dve.wait_ge(*c.last())
                    dve.wait_ge(S["gd_ss"], c.need("gd_ss"))
                    v.tensor_scalar(gt[:, 4:6, :], t2(bk(b_ss)), EPS, None, ALU.add).then_inc(*c.inc("gd_nrm"))
                    dve.wait_ge(*c.last())
                    dve.wait_ge(S["gd_eg"], c.need("gd_eg"))
                    for t in range(TT):
                        v.tensor_scalar(dec[:, t, :], bk(b_bc, t * P, P), gbt[:, t, h:h + 1], 0.0, ALU.subtract, ALU.min).then_inc(*c.inc("dve_step"))
                        dve.wait_ge(*c.last())
                    v.tensor_scalar(small[:, 24 + h:25 + h], gbt[:, 0, h:h + 1], -1.0, bk(b_bc, P - 1, 1), ALU.mult, ALU.add).then_inc(*c.inc("gd_dif"))
                    dve.wait_ge(*c.last())
                    yield
                    dve.wait_ge(S["gd_sqrt"], c.need("gd_sqrt"))
                    v.tensor_tensor(gt[:, 3, :], k_, gt[:, 7, :], ALU.mult).then_inc(*c.inc("dve_step"))
                    dve.wait_ge(*c.last())
                    v.scalar_tensor_tensor(kq[:, :, 1, :], t2(q_), P ** -0.5, t2(gt[:, 6, :]), ALU.mult, ALU.mult).then_inc(*c.inc("dve_step"))
                    dve.wait_ge(*c.last())
                    v.tensor_tensor(kq[:, :, 0, :], t2(gt[:, 3, :]), t2(bk(b_bc, T, T)), ALU.mult).then_inc(*c.inc("dve_step"))
                    dve.wait_ge(*c.last())
                    v.tensor_tensor(ke[:, h, :], gt[:, 3, :], gt[:, 2, :], ALU.mult).then_inc(*c.inc("dve_step"))
                    dve.wait_ge(*c.last())
                    v.tensor_tensor(t2(qe[:, h, :]), kq[:, :, 1, :], t2(gt[:, 2, :]), ALU.mult).then_inc(*c.inc("gd_fm"))
                    dve.wait_ge(*c.last())
                    yield
                    dve.wait_ge(S["gd_kk"], c.need("gd_kk"))
                    dve.wait_ge(S["gd_dec"], c.need("gd_dec"))
                    m = gt[:, 8:10, :].rearrange("p t (b c) -> p t b c", b=2)
                    v.tensor_tensor(m, bk(b_kk).rearrange("p (a b c) -> p a b c", a=2, b=2),
                                      dec.unsqueeze(2).to_broadcast([P, TT, 2, P]), ALU.mult).then_inc(*c.inc("dve_step"))
                    dve.wait_ge(*c.last())
                    v.tensor_tensor(gNT[:, h], m[:, :, 0, :], b4(C("gdnmask", 0, P), 2), ALU.mult).then_inc(*c.inc("dve_step"))
                    dve.wait_ge(*c.last())
                    v.tensor_tensor(gAT[:, h], m[:, :, 1, :], b4(C("gdnmask", P, 2 * P), 2), ALU.mult).then_inc(*c.inc("gd_N"))
                    dve.wait_ge(*c.last())
                    yield

            def gdn(l):
                pad_raw()
                for n in range(24):
                    dst = rkv[:, n, :]
                    dve.wait_ge(S["proj_evac"], c.need("proj_evac"))
                    v.tensor_scalar(dst, raw[:, n % 4, 0:256], pc(l, "conv", n), None, ALU.mult).then_inc(*c.inc("dve_step"))
                    dve.wait_ge(*c.last())
                    for i in range(1, 4):
                        v.scalar_tensor_tensor(dst, raw[:, n % 4, i:i + 256], pc(l, "conv", 24 * i + n), dst,
                                                 ALU.mult, ALU.add).then_inc(*c.inc("raw_free" if i == 3 else "dve_step"))
                        dve.wait_ge(*c.last())
                dve.wait_ge(S["rkv_ready"], c.need("rkv_ready", 2))
                dve.wait_ge(S["gd_abs"], c.need("gd_abs"))
                v.tensor_tensor(ab[0:8, 2, :], ab[0:8, 2, :], ab[0:8, 3, :], ALU.add).then_inc(*c.inc("dve_step"))
                dve.wait_ge(*c.last())
                v.tensor_scalar(ab[0:8, 2, :], ab[0:8, 2, :], small[0:8, 8:9], -1.0, ALU.mult, ALU.mult).then_inc(*c.inc("dve_step"))
                dve.wait_ge(*c.last())
                for t in range(TT):
                    s = slice(t * P, t * P + P)
                    v.tensor_tensor_scan(g8[0:8, s], C("ones")[0:8, :], ab[0:8, 2, s], 0.0, ALU.mult, ALU.add).then_inc(*c.inc("gd_g" if t else "dve_step"))
                    dve.wait_ge(*c.last())
                dve.wait_ge(S["gd_gT"], c.need("gd_gT"))
                v.tensor_copy(gbt, bk(4, 0, 32).rearrange("p (a b) -> p a b", a=2)).then_inc(*c.inc("dve_step"))
                dve.wait_ge(*c.last())
                t2 = lambda ap: ap.rearrange("p (a b) -> p a b", a=2)
                second = front_gd(range(4, 8), GD_BUFS[0])
                beside(front_gd((0, 2), GD_BUFS[0]), front_gd((1, 3), GD_BUFS[1]))
                beside(inverted(7, [(gX[i], gYm[i]) for i in range(2)]), second, 1)
                beside(inverted(7, [(gX[i], gYm[i]) for i in range(2)]), recur_gd(0))
                beside(recur_gd(1), None)
                dve.wait_ge(S["gr_Of"], c.need("gr_Of", 4))
                for i in range(4):
                    o = branch[:, 2 * i:2 * i + 2, :]
                    v.tensor_tensor(gt[:, 0:2, :], o, o, ALU.mult).then_inc(*c.inc("gt_sq"))
                    dve.wait_ge(*c.last())
                    dve.wait_ge(S["gt_ss"], c.need("gt_ss"))
                    v.tensor_scalar(gt[:, 2:4, :], t2(bk(2)), 1.0 / P, EPS, ALU.mult, ALU.add).then_inc(*c.inc("gt_ms"))
                    dve.wait_ge(*c.last())
                    dve.wait_ge(S["gt_sd"], c.need("gt_sd"))
                    v.scalar_tensor_tensor(o, o, pc(l, "gdn_norm"), gt[:, 6:8, :], ALU.mult, ALU.mult).then_inc(*c.inc("gn_y" if i == 3 else "dve_step"))
                    dve.wait_ge(*c.last())
                gated(gate_gd, False, False)

            def recur_gd(g):
                for t in range(TT):
                    src = vtm[:, 4 * g:4 * g + 4, t, :]
                    if t == 0:
                        dve.wait_ge(S["gd_tm"], c.need("gd_tm", 4))
                    else:
                        dve.wait_ge(S["gr_in"], c.need("gr_in"))
                        v.tensor_tensor(gR, src, bk4(0), ALU.subtract).then_inc(*c.inc("dve_step"))
                        dve.wait_ge(*c.last())
                        src = gR
                    for i in range(4):
                        v.tensor_scalar(gR[:, i, :], src[:, i, :], gbt[:, t, 8 + 4 * g + i:9 + 4 * g + i], None, ALU.mult).then_inc(*c.inc("gr_R" if i == 3 else "dve_step"))
                        dve.wait_ge(*c.last())
                    if t:
                        yield
                    dve.wait_ge(S["gr_V"], c.need("gr_V"))
                    v.tensor_copy(gV, bk4(1)).then_inc(*c.inc("gr_Vs"))
                    dve.wait_ge(*c.last())
                    yield
                    if t == 0:
                        dve.wait_ge(S["gr_S"], c.need("gr_S"))
                        v.tensor_copy(gS, bk4(6)).then_inc(*c.inc("gr_Ss"))
                        dve.wait_ge(*c.last())
                    yield

            def attention(heads, masked):
                neg = negm.rearrange("p a b -> p (a b)")
                for h in range(heads):
                    dve.wait_ge(S["at_L"], c.need("at_L"))
                    if masked:
                        v.tensor_tensor(Lm[:, h % 2, :], bk(2 + h % 2), neg, ALU.add).then_inc(*c.inc("dve_step"))
                        dve.wait_ge(*c.last())
                        src = Lm[:, h % 2, :]
                    else:
                        src = bk(2 + h % 2)
                    v.tensor_reduce(amax[:, h % 2, :], src.rearrange("p (a b) -> p a b", a=2), AX.X, ALU.max,
                                      negate=True).then_inc(*c.inc("at_max"))
                    dve.wait_ge(*c.last())
                    dve.wait_ge(S["at_exp"], c.need("at_exp", 2))
                    v.reciprocal(ainv[:, h % 2, :], asum[:, h % 2, :]).then_inc(*c.inc("dve_step"))
                    dve.wait_ge(*c.last())
                    for qt in range(TT):
                        s = slice(qt * T, qt * T + T)
                        v.tensor_scalar(Pr[:, h % 2, s], Pr[:, h % 2, s], ainv[:, h % 2, qt:qt + 1], None, ALU.mult).then_inc(*c.inc("at_p" if qt else "dve_step"))
                        dve.wait_ge(*c.last())

            def mla(l):
                dve.wait_ge(S["proj_evac"], c.need("proj_evac", 6))
                v.tensor_tensor(mt[:, 0:4, :], cqk, cqk, ALU.mult).then_inc(*c.inc("ml_sq"))
                dve.wait_ge(*c.last())
                dve.wait_ge(S["kI_m"], c.need("kI_m"))
                v.scalar_tensor_tensor(kI, bk(3, 0, T), -1.0 / 64, kI, ALU.mult, ALU.add).then_inc(*c.inc("dve_step"))
                dve.wait_ge(*c.last())
                v.tensor_tensor(mt[:, 4, :], kI, kI, ALU.mult).then_inc(*c.inc("kI_v"))
                dve.wait_ge(*c.last())
                dve.wait_ge(S["kI_var"], c.need("kI_var"))
                v.tensor_scalar(mt[:, 4, :], bk(3, T, T), 1.0 / 64, EPS, ALU.mult, ALU.add).then_inc(*c.inc("kI_ms"))
                dve.wait_ge(*c.last())
                v.tensor_scalar(mt[:, 0:2, :], bk(2).rearrange("p (a b) -> p a b", a=2), 1.0 / 256, EPS,
                                  ALU.mult, ALU.add).then_inc(*c.inc("ml_ms"))
                dve.wait_ge(*c.last())
                dve.wait_ge(S["kI_sd"], c.need("kI_sd"))
                v.reciprocal(mt[:, 4, :], mt[:, 5, :]).then_inc(*c.inc("dve_step"))
                dve.wait_ge(*c.last())
                v.scalar_tensor_tensor(kI, kI, pc(l, "kI_g"), mt[:, 4, :], ALU.mult, ALU.mult).then_inc(*c.inc("dve_step"))
                dve.wait_ge(*c.last())
                v.tensor_scalar(kI, kI, pc(l, "kI_b"), None, ALU.add).then_inc(*c.inc("kI_n"))
                dve.wait_ge(*c.last())
                dve.wait_ge(S["ml_ss"], c.need("ml_ss"))
                dve.wait_ge(S["ml_sd"], c.need("ml_sd"))
                v.reciprocal(mt[:, 0:2, :], mt[:, 2:4, :]).then_inc(*c.inc("dve_step"))
                dve.wait_ge(*c.last())
                for i in range(4):
                    gain = pc(l, "q_norm", i) if i < 2 else pc(l, "kv_norm", i - 2)
                    v.scalar_tensor_tensor(cqk[:, i, :], cqk[:, i, :], gain, mt[:, i // 2, :], ALU.mult, ALU.mult).then_inc(*c.inc("ml_n" if i == 3 else "dve_step"))
                    dve.wait_ge(*c.last())
                c.skip("proj_evac", 44)
                for n in range(16):
                    qt, h = n // 8, n % 8
                    dve.wait_ge(S["ix_rl"], c.need("ix_rl"))
                    w_ = wI[:, qt, h:h + 1]
                    if h == 0:
                        v.tensor_scalar(score[:, qt, :], rl[:, n % 4, :], w_, None, ALU.mult).then_inc(*c.inc("ix_free"))
                        dve.wait_ge(*c.last())
                    else:
                        v.scalar_tensor_tensor(score[:, qt, :], rl[:, n % 4, :], w_, score[:, qt, :], ALU.mult, ALU.add).then_inc(*c.inc("ix_free"))
                        dve.wait_ge(*c.last())
                v.tensor_tensor(score, score, C("fill").rearrange("p (a b) -> p a b", a=2), ALU.add).then_inc(*c.inc("dve_step"))
                dve.wait_ge(*c.last())
                for qt in range(TT):
                    for _ in range(TOPK // 8):
                        v.max(m8, score[:, qt, :]).then_inc(*c.inc("dve_step"))
                        dve.wait_ge(*c.last())
                        v.match_replace(score[:, qt, :], m8, score[:, qt, :], TAKEN).then_inc(*c.inc("dve_step"))
                        dve.wait_ge(*c.last())
                v.tensor_scalar(negm, score, (FILL + TAKEN) / 2, -1.0, ALU.is_le, ALU.add).then_inc(*c.inc("dve_step"))
                dve.wait_ge(*c.last())
                v.scalar_tensor_tensor(negm, negm, 1e30, C("fill").rearrange("p (a b) -> p a b", a=2), ALU.mult, ALU.add).then_inc(*c.inc("dve_step"))
                dve.wait_ge(*c.last())
                attention(8, True)
                dve.wait_ge(S["at_Of"], c.need("at_Of", 8))
                gated(gate_ml, False, True)

            def residual():
                for h in range(2):
                    for t in range(TT):
                        dve.wait_ge(S["mix_full"], c.need("mix_full"))
                        o = xt[:, t, h * 512:(h + 1) * 512]
                        v.tensor_tensor(o, bk(4 + 2 * h + t), o, ALU.add).then_inc(*c.inc("x_new"))
                        dve.wait_ge(*c.last())

            nf = [0]

            nff = [0]

            def low_part():
                b = nff[0] % FFN_BUFS
                nff[0] += 1
                dve.wait_ge(S["w_hi"], c.need("w_hi"))
                v.tensor_tensor(w_parts[b][1], ring[:, b * FFN_SLOT:(b + 1) * FFN_SLOT], w_parts[b][0], ALU.subtract
                                ).then_inc(*c.inc("w_lo"))

            def ffn(steps, e=None, more=False):
                for f in range(steps):
                    for j in range(2):
                        n = nf[0] % 4
                        nf[0] += 1
                        dve.wait_ge(S["silu"], c.need("silu"))
                        v.tensor_tensor(silu_t[:, n, :], bk(n, T, T), silu_t[:, n, :], ALU.mult).then_inc(*c.inc("act_f"))
                        dve.wait_ge(*c.last())
                        v.tensor_copy(act_parts[0][:, n, :], silu_t[:, n, :]).then_inc(*c.inc("act_f"))
                        dve.wait_ge(*c.last())
                        v.tensor_tensor(act_parts[1][:, n, :], silu_t[:, n, :], act_parts[0][:, n, :], ALU.subtract
                                        ).then_inc(*c.inc("act_t"))
                        if f < steps - 1 or more:
                            low_part()
                    if f < steps - 1 or more:
                        low_part()
                dve.wait_ge(S["down_full"], c.need("down_full"))
                for t in range(TT):
                    for h in range(2):
                        o = xt[:, t, h * 512:(h + 1) * 512]
                        if e is None:
                            v.tensor_tensor(o, bk(4 + 2 * t + h), o, ALU.add).then_inc(*c.inc("x_new"))
                        else:
                            v.scalar_tensor_tensor(o, bk(4 + 2 * t + h), gates[:, t, bass.ds(e, 1)], o, ALU.mult, ALU.add
                                                   ).then_inc(*c.inc("x_new"))
                dve.wait_ge(*c.last())

            def route():
                lg = small[:, 48:64].rearrange("p (a b) -> p a b", a=2)
                s1, s2, cum, l2 = (view(rtmp, 16 * i, 2, 8) for i in range(4))
                dve.wait_ge(S["rt_full"], c.need("rt_full"))
                v.tensor_copy(lg, bk(3, 0, 16).rearrange("p (a b) -> p a b", a=2)).then_inc(*c.inc("rt_l"))
                dve.wait_ge(*c.last())

                def first_max(src, m, s):
                    v.tensor_reduce(m, src, AX.X, ALU.max).then_inc(*c.inc("dve_step"))
                    dve.wait_ge(*c.last())
                    v.tensor_tensor(s, src, m.unsqueeze(2).to_broadcast([P, TT, NE]), ALU.is_equal).then_inc(*c.inc("dve_step"))
                    dve.wait_ge(*c.last())
                    for t in range(TT):
                        v.tensor_tensor_scan(cum[:, t, :], C("ones")[:, 0:NE], s[:, t, :], 0.0, ALU.mult, ALU.add).then_inc(*c.inc("dve_step"))
                        dve.wait_ge(*c.last())
                    v.scalar_tensor_tensor(s, cum, 1.0, s, ALU.is_equal, ALU.mult).then_inc(*c.inc("dve_step"))
                    dve.wait_ge(*c.last())

                m1, m2 = small[:, 38:40], small[:, 40:42]
                first_max(lg, m1, s1)
                v.scalar_tensor_tensor(l2, s1, -1e30, lg, ALU.mult, ALU.add).then_inc(*c.inc("dve_step"))
                dve.wait_ge(*c.last())
                first_max(l2, m2, s2)
                v.tensor_tensor(small[:, 42:44], m2, m1, ALU.subtract).then_inc(*c.inc("rt_d"))
                dve.wait_ge(*c.last())
                dve.wait_ge(S["rt_e"], c.need("rt_e"))
                e2, p1, p2 = small[:, 44:46], small[:, 46:48], small[:, 64:66]
                v.tensor_scalar(p2, e2, 1.0, None, ALU.add).then_inc(*c.inc("dve_step"))
                dve.wait_ge(*c.last())
                v.reciprocal(p1, p2).then_inc(*c.inc("dve_step"))
                dve.wait_ge(*c.last())
                v.tensor_tensor(p2, e2, p1, ALU.mult).then_inc(*c.inc("dve_step"))
                dve.wait_ge(*c.last())
                v.tensor_tensor(s1, s1, p1.unsqueeze(2).to_broadcast([P, TT, NE]), ALU.mult).then_inc(*c.inc("dve_step"))
                dve.wait_ge(*c.last())
                v.tensor_tensor(s2, s2, p2.unsqueeze(2).to_broadcast([P, TT, NE]), ALU.mult).then_inc(*c.inc("dve_step"))
                dve.wait_ge(*c.last())
                v.tensor_tensor(gates[:, :, :], s1, s2, ALU.add).then_inc(*c.inc("dve_step"))
                dve.wait_ge(*c.last())

            dve.wait_ge(S["par_dma"], 48)
            dve.wait_ge(S["mem_dma"], 16)
            norm(yflat.rearrange("p (a b) -> p a b", a=TT), "mem_norm", 0, memf)
            dve.wait_ge(S["in_dma"], 16)
            for l in range(LAYERS):
                norm(xt, "norm_mix", l, feat)
                rwkv(l)
                gdn(l)
                mla(l)
                residual()
                norm(xt, "norm_xattn", l, feat)
                c.skip("proj_evac", 8)
                attention(4, False)
                residual()
                v.memset(small[:, 70:71], 0.0).then_inc(*c.inc("mixers_done"))
                dve.wait_ge(*c.last())
                norm(xt, "norm_ffn", l, feat)
                dve.wait_ge(S["f_hi"], c.need("f_hi"))
                v.tensor_tensor(feat_parts[1], feat[:, :, :], feat_parts[0], ALU.subtract).then_inc(*c.inc("dve_step"))
                for _ in range(3):
                    low_part()
                if l == 0:
                    ffn(FF // 256)
                else:
                    route()
                    ffn(FE // 256, 0, True)
                    with dve.Fori(1, NE - 1) as e:
                        c.begin_loop(e - 1, dict(silu=FE // P, act_t=FE // P, act_f=2 * FE // P, down_full=1, x_new=4,
                                                 w_hi=FE_CHUNKS, w_lo=FE_CHUNKS))
                        ffn(FE // 256, e, True)
                    c.end_loop(NE - 2)
                    ffn(FE // 256, NE - 1)
            norm(xt)
    return nc


_WEIGHTS = ["w_in", "rw_w2", "rw_a2", "rw_v1", "rw_v2", "mla_w_uq", "mla_w_uk", "mla_w_uv", "idx_w_q", "w_mix_out",
            "xa_w_q", "xa_w_kv", "xa_w_o", "ffn_w_gate", "ffn_w_up", "ffn_w_down", "moe_router", "moe_w_gate",
            "moe_w_up", "moe_w_down", "final_norm"]


def pack_params(i):
    out = np.zeros((LAYERS, P, NPAR), np.float32)
    for l in range(LAYERS):
        vec = {"norm_mix": i["norm_mix"][l], "mu": i["rw_mu"][l], "w0": i["rw_w0"][l], "a0": i["rw_a0"][l],
               "k_k": i["rw_k_k"][l], "k_a": i["rw_k_a"][l], "r_k": i["rw_r_k"][l].reshape(-1),
               "gn_g": i["rw_gn_g"][l], "gn_b": i["rw_gn_b"][l], "norm_xattn": i["norm_xattn"][l],
               "norm_ffn": i["norm_ffn"][l], "q_norm": i["mla_q_norm"][l], "kv_norm": i["mla_kv_norm"][l],
               "gdn_norm": i["gdn_norm_g"][l], "mem_norm": i["mem_norm"], "conv": i["gdn_conv"][l].reshape(-1)}
        if l:
            vec["v0"] = i["rw_v0"][l - 1]
        for name, a in vec.items():
            a = np.asarray(a).reshape(-1, P)
            out[l, :, PCOL[name]:PCOL[name] + a.shape[0]] = a.T
        for h in range(2):
            out[l, 64 * h:64 * h + 64, PCOL["kI_g"]] = i["idx_k_g"][l]
            out[l, 64 * h:64 * h + 64, PCOL["kI_b"]] = i["idx_k_b"][l]
        out[l, 0:GH, PCOL["A_log"]] = i["gdn_A_log"][l]
        out[l, 0:GH, PCOL["dt_bias"]] = i["gdn_dt_bias"][l]
    return out


def kernel(**inputs):
    import concourse.bacc as bacc
    from concourse.bass_utils import run_bass_kernel_spmd

    inp = {k: np.asarray(v) for k, v in inputs.items()}
    arrays = {"x": inp["x"].reshape(T, D), "mem": inp["mem"].reshape(T, D), "consts": make_consts(),
              "params": pack_params(inp)}
    for n in _WEIGHTS:
        a = inp[n]
        if n in ("mla_w_uk", "mla_w_uv"):
            a = a.reshape(LAYERS, 256, D)
        if n == "moe_router":
            a = a.reshape(D, NE)
        arrays[n] = a
    arrays = {f"in_{n}": np.ascontiguousarray(a) for n, a in arrays.items()}
    nc = bacc.Bacc("TRN2", target_bir_lowering=False, num_devices=1, dynamic_dma_scratch_size=1024)
    args = [nc.dram_tensor(n, a.shape, F32, kind="ExternalInput").ap() for n, a in arrays.items()]
    out = nc.dram_tensor("out", (T, D), F32, kind="ExternalOutput").ap()
    build(nc, *args, out)
    r = run_bass_kernel_spmd(nc, [arrays], core_ids=[0])
    return r.results[0]["out"].reshape(1, T, D)
```
